# Optimizing a Trainium2 kernel written in Bass

```python
import jax, jax.numpy as jnp
from jax import lax
import numpy as np

D_MODEL = 2048
BATCH = 1
SEQ = 256
DEPTH = 1

PLE_DIM = 256
MIX_WIDTH = D_MODEL
HG_KEY = 128
HG_VAL = 128
HG_WIDTH = MIX_WIDTH // 2
HG_HEADS = HG_WIDTH // HG_KEY
ATT_HEAD_DIM = 128
ATT_WIDTH = MIX_WIDTH - HG_WIDTH
ATT_HEADS = ATT_WIDTH // ATT_HEAD_DIM
DILATED_BRANCHES = ((128, 1), (512, 4), (2048, 16))
ATT_BLOCK = 128
CHUNK = 64
D_FF = 5632
CONV_WIDTH = 3
EPS = 1e-6
IN_SIZES = (HG_WIDTH, HG_WIDTH, HG_WIDTH, HG_WIDTH, ATT_WIDTH, ATT_WIDTH, ATT_WIDTH)
IN_COLS = sum(IN_SIZES)


def rms_norm(x, w):
    x32 = x.astype(jnp.float32)
    y = x32 * lax.rsqrt(jnp.mean(x32 * x32, axis=-1, keepdims=True) + EPS)
    return (y * w.astype(jnp.float32)).astype(x.dtype)

def hgrn2_mixer(q_raw, f_raw, i_raw, g_raw, lb, norm_w):
    B, S, _ = q_raw.shape
    f32 = jnp.float32
    q = jax.nn.silu(q_raw.astype(f32)).reshape(B, S, HG_HEADS, HG_KEY)
    lbh = lb.astype(f32).reshape(HG_HEADS, HG_KEY)
    f = lbh + (1.0 - lbh) * jax.nn.sigmoid(f_raw.astype(f32).reshape(B, S, HG_HEADS, HG_KEY))
    k = 1.0 - f
    logf = jnp.log(f)
    v = i_raw.astype(f32).reshape(B, S, HG_HEADS, HG_VAL)
    n_chunks = S // CHUNK

    def to_chunks(t):
        return t.reshape(B, n_chunks, CHUNK, HG_HEADS, t.shape[-1]).transpose(1, 0, 3, 2, 4)

    qc, kc, vc = to_chunks(q), to_chunks(k), to_chunks(v)
    bc = jnp.cumsum(to_chunks(logf), axis=3)
    causal = jnp.tril(jnp.ones((CHUNK, CHUNK), dtype=bool))

    def step(state, xs):
        qt, kt, vt, bt = xs
        inter = jnp.einsum('bhck,bhkv->bhcv', qt * jnp.exp(bt), state)
        rel = bt[:, :, :, None, :] - bt[:, :, None, :, :]
        decay = jnp.exp(jnp.where(causal[:, :, None], rel, -jnp.inf))
        scores = jnp.einsum('bhtk,bhsk,bhtsk->bhts', qt, kt, decay)
        intra = jnp.einsum('bhts,bhsv->bhtv', scores, vt)
        b_last = bt[:, :, -1, :]
        new_state = jnp.exp(b_last)[..., None] * state + jnp.einsum(
            'bhsk,bhsv->bhkv', kt * jnp.exp(b_last[:, :, None, :] - bt), vt)
        return new_state, inter + intra

    s0 = jnp.zeros((B, HG_HEADS, HG_KEY, HG_VAL), f32)
    _, oc = lax.scan(step, s0, (qc, kc, vc, bc))
    o = oc.transpose(1, 0, 3, 2, 4).reshape(B, S, HG_HEADS, HG_VAL)
    o = o * lax.rsqrt(jnp.mean(o * o, axis=-1, keepdims=True) + EPS)
    o = o.reshape(B, S, HG_WIDTH) * norm_w.astype(f32) * jax.nn.silu(g_raw.astype(f32))
    return o.astype(q_raw.dtype)

def dilated_branch(q, k, v, window, dilation):
    B, Sp, H, E = q.shape
    span = window // dilation
    nb = Sp // dilation // ATT_BLOCK

    def to_blocks(t):
        return t.reshape(B, nb, ATT_BLOCK, dilation, H, E).transpose(0, 3, 4, 1, 2, 5)

    def with_prev(t):
        prev = jnp.pad(t[:, :, :, :-1], ((0, 0), (0, 0), (0, 0), (1, 0), (0, 0), (0, 0)))
        return jnp.concatenate([prev, t], axis=4)

    qb = to_blocks(q)
    kw, vw = with_prev(to_blocks(k)), with_prev(to_blocks(v))
    s = jnp.einsum('brhnqe,brhnke->brhnqk', qb, kw) * (E ** -0.5)
    qi = jnp.arange(ATT_BLOCK)[:, None]
    kj = jnp.arange(2 * ATT_BLOCK)[None, :]
    dist = ATT_BLOCK + qi - kj
    blk = jnp.arange(nb)[:, None, None]
    valid = (dist >= 0) & (dist <= span) & ((blk > 0) | (kj >= ATT_BLOCK)[None])
    s = jnp.where(valid, s, -jnp.inf)
    lse = jax.nn.logsumexp(s, axis=-1)
    o = jnp.einsum('brhnqk,brhnke->brhnqe', jnp.exp(s - lse[..., None]), vw)
    o = o.transpose(0, 3, 4, 1, 2, 5).reshape(B, Sp, H, E)
    lse = lse.transpose(0, 3, 4, 1, 2).reshape(B, Sp, H)
    return o, lse

def dilated_attention_mixer(q_raw, k_raw, v_raw):
    B, S, _ = q_raw.shape
    unit = ATT_BLOCK * max(d for _, d in DILATED_BRANCHES)
    Sp = -(-S // unit) * unit

    def prep(t):
        t = t.astype(jnp.float32).reshape(B, S, ATT_HEADS, ATT_HEAD_DIM)
        return jnp.pad(t, ((0, 0), (0, Sp - S), (0, 0), (0, 0)))

    q, k, v = prep(q_raw), prep(k_raw), prep(v_raw)
    branches = [dilated_branch(q, k, v, w, d) for w, d in DILATED_BRANCHES]
    outs = jnp.stack([o for o, _ in branches])
    lses = jnp.stack([l for _, l in branches])
    wts = jax.nn.softmax(lses, axis=0)
    o = jnp.einsum('nbsh,nbshe->bshe', wts, outs)[:, :S]
    return o.reshape(B, S, ATT_WIDTH).astype(q_raw.dtype)

def conv_gated_mlp(u, w_up, conv_w, conv_b, w_down):
    S = u.shape[1]
    up = u @ w_up
    pad = jnp.pad(up, ((0, 0), (CONV_WIDTH - 1, 0), (0, 0)))
    up = conv_b + sum(pad[:, j:j + S] * conv_w[j] for j in range(CONV_WIDTH))
    gate, val = jnp.split(up, 2, axis=-1)
    return (jax.nn.gelu(gate, approximate=True) * val) @ w_down

def first_inputs(seed: int = 0) -> dict:
    key = jax.random.key(seed)
    ks = jax.random.split(key, 20)
    f32 = jnp.float32

    def nrm(k, shape, scale):
        return jax.random.normal(k, shape, f32) * scale

    def gain(k, shape):
        return 1.0 + 0.05 * jax.random.normal(k, shape, f32)

    L = DEPTH
    return {
        'x': nrm(ks[0], (BATCH, SEQ, D_MODEL), 1.0),
        'p': nrm(ks[1], (DEPTH, BATCH, SEQ, PLE_DIM), 1.0),
        'ln_mix_pre': gain(ks[2], (L, D_MODEL)),
        'w_in': nrm(ks[3], (L, D_MODEL, IN_COLS), D_MODEL ** -0.5),
        'lb_logits': nrm(ks[4], (L, HG_WIDTH), 0.1),
        'hgrn_norm': gain(ks[5], (L, HG_WIDTH)),
        'w_out': nrm(ks[6], (L, MIX_WIDTH, D_MODEL), MIX_WIDTH ** -0.5),
        'ln_mix_post': gain(ks[7], (L, D_MODEL)),
        'ln_ffn_pre': gain(ks[8], (L, D_MODEL)),
        'w_up': nrm(ks[9], (L, D_MODEL, 2 * D_FF), D_MODEL ** -0.5),
        'conv_w': nrm(ks[10], (L, CONV_WIDTH, 2 * D_FF), CONV_WIDTH ** -0.5),
        'conv_b': nrm(ks[11], (L, 2 * D_FF), 0.02),
        'w_down': nrm(ks[12], (L, D_FF, D_MODEL), D_FF ** -0.5),
        'ln_ffn_post': gain(ks[13], (L, D_MODEL)),
        'w_pe': nrm(ks[14], (L, PLE_DIM, D_MODEL), PLE_DIM ** -0.5),
        'w_pg': nrm(ks[15], (L, D_MODEL, D_MODEL), D_MODEL ** -0.5),
    }

def first_block(x, p, ln_mix_pre, w_in, lb_logits, hgrn_norm, w_out, ln_mix_post,
              ln_ffn_pre, w_up, conv_w, conv_b, w_down, ln_ffn_post, w_pe, w_pg):
    lb_all = jnp.cumsum(jax.nn.softmax(lb_logits.astype(jnp.float32), axis=0), axis=0)
    lb_all = lb_all - lb_all[0]
    split_at = [int(c) for c in np.cumsum(IN_SIZES)[:-1]]
    h = x
    for l in range(DEPTH):
        u = rms_norm(h, ln_mix_pre[l])
        hq, hf, hi, hg, aq, ak, av = jnp.split(u @ w_in[l], split_at, axis=-1)
        o_rec = hgrn2_mixer(hq, hf, hi, hg, lb_all[l], hgrn_norm[l])
        o_att = dilated_attention_mixer(aq, ak, av)
        mixed = jnp.concatenate([o_rec, o_att], axis=-1) @ w_out[l]
        h = h + rms_norm(mixed, ln_mix_post[l])
        y = conv_gated_mlp(rms_norm(h, ln_ffn_pre[l]), w_up[l], conv_w[l], conv_b[l], w_down[l])
        h = h + rms_norm(y, ln_ffn_post[l])
        h = h + (p[l] @ w_pe[l]) * jax.nn.sigmoid(h @ w_pg[l])
    return h


MEM_LEN = 256
HEAD_DIM = 128
N_CONV_GROUPS = 4
CONV_W = N_CONV_GROUPS * HEAD_DIM
CONV_K = 31
N_FOX_HEADS = 8
FOX_W = N_FOX_HEADS * HEAD_DIM
N_MEM_HEADS = 4
MEM_W = N_MEM_HEADS * HEAD_DIM
MIX_W = CONV_W + FOX_W + MEM_W
Q_BLOCK = 128
FORGET_BIAS_INIT = 2.0

SPLITS = (
    CONV_W,
    2 * CONV_W,
    3 * CONV_W,
    3 * CONV_W + FOX_W,
    3 * CONV_W + 2 * FOX_W,
    3 * CONV_W + 3 * FOX_W,
    3 * CONV_W + 3 * FOX_W + N_FOX_HEADS,
    3 * CONV_W + 4 * FOX_W + N_FOX_HEADS,
    3 * CONV_W + 4 * FOX_W + N_FOX_HEADS + MEM_W,
)
D_IN = 3 * CONV_W + 4 * FOX_W + N_FOX_HEADS + 2 * MEM_W


def rmsnorm(x, g):
    xf = x.astype(jnp.float32)
    y = xf * lax.rsqrt(jnp.mean(xf * xf, axis=-1, keepdims=True) + EPS)
    return (y * g.astype(jnp.float32)).astype(x.dtype)

def layernorm(x, g, b):
    xf = x.astype(jnp.float32)
    mu = jnp.mean(xf, axis=-1, keepdims=True)
    var = jnp.mean(jnp.square(xf - mu), axis=-1, keepdims=True)
    y = (xf - mu) * lax.rsqrt(var + EPS)
    return (y * g.astype(jnp.float32) + b.astype(jnp.float32)).astype(x.dtype)

def causal_depthwise_conv(u, w, b):
    y = lax.conv_general_dilated(
        u, w[:, None, :], window_strides=(1,), padding=[(CONV_K - 1, 0)],
        dimension_numbers=('NWC', 'WIO', 'NWC'), feature_group_count=u.shape[-1])
    return y + b

def fox_attention(q, k, v, logf):
    B, S, H, Dh = q.shape
    nb = S // Q_BLOCK
    cT = jnp.cumsum(logf, axis=1).transpose(0, 2, 1)
    qb = q.reshape(B, nb, Q_BLOCK, H, Dh).transpose(1, 0, 2, 3, 4)
    cb = cT.reshape(B, H, nb, Q_BLOCK).transpose(2, 0, 1, 3)
    k_pos = jnp.arange(S)
    scale = Dh ** -0.5

    def block(args):
        i, qi, ci = args
        s = jnp.einsum('bqhd,bkhd->bhqk', qi, k).astype(jnp.float32) * scale
        bias = ci[..., :, None] - cT[..., None, :]
        q_pos = i * Q_BLOCK + jnp.arange(Q_BLOCK)
        mask = k_pos[None, :] <= q_pos[:, None]
        s = jnp.where(mask, s + bias, -jnp.inf)
        p = jax.nn.softmax(s, axis=-1).astype(v.dtype)
        return jnp.einsum('bhqk,bkhd->bqhd', p, v)

    out = lax.map(block, (jnp.arange(nb), qb, cb))
    return out.transpose(1, 0, 2, 3, 4).reshape(B, S, H * Dh)

def memory_attention(q, mk, mv):
    B, S, H, Dh = q.shape
    s = jnp.einsum('bshd,bmhd->bhsm', q, mk).astype(jnp.float32) * (Dh ** -0.5)
    p = jax.nn.softmax(s, axis=-1).astype(mv.dtype)
    return jnp.einsum('bhsm,bmhd->bshd', p, mv).reshape(B, S, H * Dh)

def second_inputs(seed: int = 0) -> dict:
    key = jax.random.key(seed)
    ks = jax.random.split(key, 16)
    n = jax.random.normal
    f32 = jnp.float32
    return {
        "x": n(ks[0], (BATCH, SEQ, D_MODEL), f32),
        "mem": n(ks[1], (BATCH, MEM_LEN, D_MODEL), f32),
        "norm_g": 1.0 + 0.05 * n(ks[2], (DEPTH, D_MODEL), f32),
        "mem_norm_g": 1.0 + 0.05 * n(ks[3], (DEPTH, D_MODEL), f32),
        "w_in": n(ks[4], (DEPTH, D_MODEL, D_IN), f32) * D_MODEL ** -0.5,
        "b_f": FORGET_BIAS_INIT + 0.1 * n(ks[5], (DEPTH, N_FOX_HEADS), f32),
        "conv_w": n(ks[6], (DEPTH, CONV_K, CONV_W), f32) * CONV_K ** -0.5,
        "conv_b": 0.02 * n(ks[7], (DEPTH, CONV_W), f32),
        "conv_ln_g": 1.0 + 0.05 * n(ks[8], (DEPTH, CONV_W), f32),
        "conv_ln_b": 0.02 * n(ks[9], (DEPTH, CONV_W), f32),
        "w_conv_pw": n(ks[10], (DEPTH, CONV_W, CONV_W), f32) * CONV_W ** -0.5,
        "w_mem_kv": n(ks[11], (DEPTH, D_MODEL, 2 * MEM_W), f32) * D_MODEL ** -0.5,
        "w_out": n(ks[12], (DEPTH, MIX_W, D_MODEL), f32) * MIX_W ** -0.5,
        "final_g": 1.0 + 0.05 * n(ks[13], (D_MODEL,), f32),
    }

def second_block(x, mem, norm_g, mem_norm_g, w_in, b_f, conv_w, conv_b, conv_ln_g,
              conv_ln_b, w_conv_pw, w_mem_kv, w_out, final_g):
    B, S, _ = x.shape
    for l in range(DEPTH):
        h = rmsnorm(x, norm_g[l])
        proj = h @ w_in[l]
        (cv_a, cv_b, cv_gate, fq, fk, fv, f_logit, fox_gate,
         mq, mem_gate) = jnp.split(proj, SPLITS, axis=-1)

        u = cv_a * jax.nn.sigmoid(cv_b)
        u = causal_depthwise_conv(u, conv_w[l], conv_b[l])
        u = jax.nn.silu(layernorm(u, conv_ln_g[l], conv_ln_b[l]))
        y_conv = (u @ w_conv_pw[l]) * jax.nn.silu(cv_gate)

        logf = jax.nn.log_sigmoid(f_logit.astype(jnp.float32) + b_f[l].astype(jnp.float32))
        shp = (B, S, N_FOX_HEADS, HEAD_DIM)
        y_fox = fox_attention(fq.reshape(shp), fk.reshape(shp), fv.reshape(shp), logf)
        y_fox = y_fox * jax.nn.silu(fox_gate)

        mkv = rmsnorm(mem, mem_norm_g[l]) @ w_mem_kv[l]
        mk, mv = jnp.split(mkv, 2, axis=-1)
        mshp = (B, mem.shape[1], N_MEM_HEADS, HEAD_DIM)
        y_mem = memory_attention(mq.reshape(B, S, N_MEM_HEADS, HEAD_DIM),
                                 mk.reshape(mshp), mv.reshape(mshp))
        y_mem = y_mem * jax.nn.silu(mem_gate)

        y = jnp.concatenate([y_conv, y_fox, y_mem], axis=-1)
        x = x + y @ w_out[l]
    return rmsnorm(x, final_g)


def setup_inputs(seed=0):
    out = dict(first_inputs(seed))
    for name, value in second_inputs(seed + 1).items():
        if name != "x":
            out[name + "_2"] = value
    return out


def reference(
    x, p, ln_mix_pre, w_in, lb_logits, hgrn_norm, w_out, ln_mix_post, ln_ffn_pre, w_up, conv_w,
    conv_b, w_down, ln_ffn_post, w_pe, w_pg, mem_2, norm_g_2, mem_norm_g_2, w_in_2, b_f_2,
    conv_w_2, conv_b_2, conv_ln_g_2, conv_ln_b_2, w_conv_pw_2, w_mem_kv_2, w_out_2, final_g_2,
):
    x = first_block(
        x, p, ln_mix_pre, w_in, lb_logits, hgrn_norm, w_out, ln_mix_post, ln_ffn_pre, w_up,
        conv_w, conv_b, w_down, ln_ffn_post, w_pe, w_pg,
    )
    return second_block(
        x, mem_2, norm_g_2, mem_norm_g_2, w_in_2, b_f_2, conv_w_2, conv_b_2, conv_ln_g_2,
        conv_ln_b_2, w_conv_pw_2, w_mem_kv_2, w_out_2, final_g_2,
    )


_drawn_inputs = setup_inputs


def setup_inputs(seed=0):
    import zlib

    import numpy as np

    out = dict(_drawn_inputs(seed))
    spreads = {}
    factors = {'conv_b': 3.489,
     'mem_2': 3.391,
     'norm_g_2': 4.972,
     'mem_norm_g_2': 8.0,
     'b_f_2': 64.0,
     'conv_b_2': 39.043,
     'conv_ln_g_2': 42.152,
     'conv_ln_b_2': 171.871,
     'w_mem_kv_2': 3.228}
    for name, (base, spread) in spreads.items():
        noise = np.random.default_rng([zlib.crc32(name.encode()), seed]).standard_normal(out[name].shape)
        drawn = base * np.exp(spread * noise) if base else spread * noise
        out[name] = __import__('jax').numpy.asarray(drawn.astype(out[name].dtype))
    for name, factor in factors.items():
        out[name] = (out[name] * factor).astype(out[name].dtype)
    return out
```

```python
from contextlib import ExitStack

import numpy as np

import concourse.bass as bass
from concourse import mybir

F32 = mybir.dt.float32
F32R = mybir.dt.float32r
BF16 = mybir.dt.bfloat16
U8 = mybir.dt.uint8
ALU = mybir.AluOpType
ACT = mybir.ActivationFunctionType
AX_X = mybir.AxisListType.X

P = 128
T = 256
D = 2048
KT = D // P
HEADS = 8
MEM_HEADS = 4
GROUPS = 4
TAPS = 31
FF = 5632
FT = FF // P
DOWN_CELLS = 11
BW = KT * P
NS = 4
EPS = 1e-6
SCALE = float(P) ** -0.5
LEVELS = 8
MASKED = -1e30
LARGE = 1e38

G_MIX, U_MIX = 0, 0
G_OUT, U_OUT = 64, 64
G_UP, U_UP = 80, 80
G_DOWN, U_DOWN = 168, 168
G_PE, U_PE = 232, 184
G_PG, U_PG = 234, 200
G_CONV, U_CONV = 250, 216
G_FOX, U_FOX = 258, 224
G_MEM, U_MEM = 290, 256
G_CG, U_CG = 298, 264
G_PW, U_PW = 302, 268
G_OUT2, U_OUT2 = 303, 272
N_BLOCKS = 319

V = {}


def _vector_columns():
    at = 0
    for name, n in (("ln_mix_pre", KT), ("lb", HEADS), ("hgrn_norm", HEADS), ("ln_mix_post", KT), ("ln_ffn_pre", KT),
                    ("conv", 4 * 2 * FT), ("ln_ffn_post", KT), ("norm_g_2", KT), ("mem_norm_g_2", KT),
                    ("taps", GROUPS * TAPS), ("conv_b_2", GROUPS), ("conv_ln_g", GROUPS), ("conv_ln_b", GROUPS),
                    ("final_g", KT)):
        V[name] = at
        at += n
    return at


N_VEC = _vector_columns()


class Chain:

    def __init__(self, eng, sem):
        self.eng, self.sem, self.base, self.j = eng, sem, 0, 0

    def link(self, ins):
        self.j += 1
        ins.then_inc(self.sem, 1)
        self.eng.wait_ge(self.sem, self.base + self.j)

    def enter(self, i, per):
        self.start, self.per = self.base + self.j, per
        self.base, self.j = self.start + i * per, 0

    def leave(self, n):
        assert self.j == self.per, f"{self.sem}: {self.j} steps in the loop's body, {self.per} stated"
        self.base, self.j = self.start + n * self.per, 0



def build(nc, a, out):
    with ExitStack() as ctx:
        def sem(name):
            return ctx.enter_context(nc.semaphore(name))

        at = [(nc.sbuf_base + 31) // 32 * 32]

        def sb(name, shape, dt=F32):
            size = int(np.prod(shape[1:])) * mybir.dt.size(dt)
            t = nc.alloc_sbuf_tensor_at(name, shape, dt, offset=at[0])
            at[0] += (size + 31) // 32 * 32
            return t

        def over(name, region_at, offset, shape, dt=F32):
            return nc.alloc_sbuf_tensor_at(name, shape, dt, offset=region_at + offset)

        stage = sb("stage", [P, NS, BW])
        whi = sb("whi", [P, 2, BW], F32R)
        wlo = sb("wlo", [P, 2, BW], F32R)
        h_at = at[0]
        h = sb("h", [P, KT, T])
        vec = sb("vec", [P, N_VEC])
        ident = sb("ident", [P, P])
        ones = sb("ones", [P, P])
        bfox = sb("bfox", [HEADS, 1])
        mkv = sb("mkv", [P, HEADS, T])
        small = sb("small", [P, 2, T])
        tmp = sb("tmp", [P, 2, T])
        rstd = sb("rstd", [P, T])
        acc = sb("acc", [P, T])
        cols = sb("cols", [P, 32])
        dummy = sb("dummy", [P, 2])
        conv_at = at[0]
        lmask = sb("lmask", [P, LEVELS, 2 * P], U8)
        mult = sb("mult", [P, 3 * P], BF16)
        bias_att = sb("bias_att", [P, 3 * P], BF16)
        rstd_mem = sb("rstd_mem", [P, T])
        upb = over("upb", conv_at, 0, [P, 2, T + 2])
        cy = over("cy", conv_at, 2080, [P, 2, T])
        gl = over("gl", conv_at, 4128, [P, T])
        at[0] = conv_at + 4128 + 1024
        a_at = at[0]
        act_a = sb("act_a", [P, KT, 2 * T], F32R)
        big_at = at[0]
        big = sb("big", [P, FT, 2 * T], F32R)
        KB = 1024

        mem_raw = over("mem_raw", big_at, 0, [P, KT, T])
        squares = over("squares", big_at, 64 * KB, [P, KT, T])
        xs_mix = big[:, 0:KT, :]
        xs_mem = big[:, KT:2 * KT, :]
        lmask_in = over("lmask_in", big_at, 80 * KB, [P, LEVELS, 2 * P], BF16)
        w1 = [64 * KB]

        def work1(name, shape):
            t = over(name, big_at, w1[0], shape)
            w1[0] += int(np.prod(shape[1:])) * 4
            assert w1[0] <= 88 * KB
            return t

        w0 = [0]

        def work0(name, shape):
            t = over(name, h_at, w0[0], shape)
            w0[0] += int(np.prod(shape[1:])) * 4
            assert w0[0] <= 16 * KB
            return t

        pfx = work1("pfx", [P, T])
        sfx = work1("sfx", [P, T])
        kk = work1("kk", [P, T])
        qq = work1("qq", [P, T])
        lev_in = work1("lev_in", [P, LEVELS, T])
        sT = work1("sT", [P, 3 * P])
        iT = work1("iT", [P, T])
        vtok = work1("vtok", [P, 2, P])
        aqT = work1("aqT", [P, T])
        akT = work1("akT", [P, T])
        avT = work1("avT", [P, T])
        avtok = work1("avtok", [P, 2, P])
        hfx = work0("hfx", [P, T])
        hqx = work0("hqx", [P, T])
        hgx = work0("hgx", [P, T])
        ef = work0("ef", [P, T])
        eq = work0("eq", [P, T])
        eg = work0("eg", [P, T])
        on1 = work0("on1", [P, T])
        osq = work0("osq", [P, T])
        osb = work0("osb", [P, T])
        var = work0("var", [P, T])
        sm = work0("sm", [P, 3 * P])
        pT = work0("pT", [P, 3 * P])
        mixed = over("mixed", big_at, 64 * KB, [P, KT, T])
        sq1 = over("sq1", big_at, 80 * KB, [P, T])
        t_res = over("t_res", big_at, 81 * KB, [P, 2, T])
        y = over("y", a_at, 0, [P, KT, T])
        p_raw = over("p_raw", a_at, 20 * KB, [P, 2, T])
        sq2 = over("sq2", a_at, 22 * KB, [P, T])
        t_res2 = over("t_res2", a_at, 23 * KB, [P, 2, T])
        xs_p = act_a[:, 8:10, :]
        xs_h = big[:, 0:KT, :]
        pe_out = over("pe_out", big_at, 32 * KB, [P, KT, T])
        pg_x = over("pg_x", big_at, 48 * KB, [P, 2, T])
        pg_s = over("pg_s", big_at, 50 * KB, [P, 2, T])
        sq3 = over("sq3", big_at, 52 * KB, [P, T])
        xs_y = big[:, 0:KT, :]
        xs_cv = big[:, 40:44, :]
        w2 = [32 * KB]

        def work2(name, shape):
            t = over(name, big_at, w2[0], shape)
            w2[0] += int(np.prod(shape[1:])) * 4
            assert w2[0] <= 80 * KB
            return t

        upad = work2("upad", [P, GROUPS, TAPS - 1 + T])
        uc = work2("uc", [P, GROUPS, T])
        usq = work2("usq", [P, GROUPS, T])
        cx = work2("cx", [P, 2, T])
        ce = work2("ce", [P, 2, T])
        mu = work2("mu", [P, T])
        bias_fox = work2("bias_fox", [P, 3 * P // 2])[:, :].bitcast(BF16)
        wfg = work2("wfg", [P, KT, HEADS])
        sg_c = work2("sg_c", [P, GROUPS, T])
        fqT = work2("fqT", [P, T])
        fkT = work2("fkT", [P, T])
        fvT = work2("fvT", [P, T])
        fgx = work2("fgx", [P, T])
        fge = work2("fge", [P, T])
        fvtok = work2("fvtok", [P, 2, P])
        fs = work2("fs", [P, 4 * P])
        fpT = work2("fpT", [P, 4 * P])
        fo = work2("fo", [P, T])
        mv_h = work2("mv_h", [P, T])
        zf = work2("zf", [HEADS, T])
        z1 = work2("z1", [HEADS, T])
        z2 = work2("z2", [HEADS, T])
        one8 = work2("one8", [HEADS, T])
        cc = work2("cc", [HEADS, T])
        cpos = work2("cpos", [HEADS, T])
        cneg = work2("cneg", [HEADS, T])
        sq4 = work2("sq4", [P, 2, T])
        h4 = over("h4", a_at, 0, [P, KT, T])
        o_out = over("o_out", a_at, 16 * KB, [P, KT, T])
        assert at[0] <= nc.sbuf_top, at[0] - nc.sbuf_top

        ps = ctx.enter_context(nc.psum_tensor("ps", [P, 2, 2 * T], F32))
        ps_lev = ctx.enter_context(nc.psum_tensor("ps_lev", [P, 2, 2, T], F32))
        ps_sc = ctx.enter_context(nc.psum_tensor("ps_sc", [P, 2 * T], F32))
        ps_t = ctx.enter_context(nc.psum_tensor("ps_t", [P, 2 * T], F32))
        ps_a = ctx.enter_context(nc.psum_tensor("ps_a", [P, 2 * T], F32))[:, 0:T]
        ps_b = ctx.enter_context(nc.psum_tensor("ps_b", [P, 2 * T], F32))[:, 0:T]

        S = {}

        def s(name):
            if name not in S:
                S[name] = sem(name)
            return S[name]

        once = {name: (kind, n + 1) for kind, names in (
            ("summed", ("x_summed", "mem_summed", "mixed_summed", "h1_summed", "y_summed", "h3_summed", "uc_summed",
                        "usq_summed", "h4_summed")),
            ("mean_square", ("x_ms", "mem_ms", "mixed_ms", "h1_ms", "y_ms", "h3_ms", "uc_ms", "h4_ms")),
            ("normed", ("x_norm", "mem_norm", "mixed_norm", "h1_norm", "y_norm", "h3_norm", "uc_norm", "h4_norm")),
            ("squares_summed", ("mixed_acc", "y_acc", "h3_acc", "h4_acc")),
            ("squared", ("x_sq", "mem_sq")),
            ("early_sums", ("x_sum", "mem_sum")),
        ) for n, name in enumerate(names)}

        def event(name):
            kind, n = once[name]
            return s(kind), n

        w_landed = [sem(f"w_landed{i}") for i in range(NS)]
        w_hi, w_lo, w_used = sem("w_hi"), sem("w_lo"), sem("w_used")
        part_made, small_ready, out_free = sem("part_made"), sem("small_ready"), sem("out_free")
        vector_step, scalar_step, pool_step = sem("vector_step"), sem("scalar_step"), sem("pool_step")
        for name in ("consts_in", "x_in", "mem_in", "x_back", "p_in", "out_done"):
            s(name)

        block = ctx.enter_context(nc.Block())

        def column(name, i, n=1):
            return vec[:, bass.ds(V[name] + i, n)]

        @block.sync
        def _(sp):
            for dst, src in ((vec, a["vec"]), (ident, a["ident"]), (ones, a["ones"]), (mult, a["mult"]),
                             (bias_att, a["bias_att"]), (lmask_in, a["lmask"]), (bfox, a["bfox"])):
                full = tuple(slice(None) for _ in dst.shape)
                sp.dma_start(dst[full], src).then_inc(s("consts_in"), 16)
            sp.dma_start(h[:, :, :], a["xT"]).then_inc(s("x_in"), 16)
            sp.dma_start(mem_raw[:, :, :], a["memT"]).then_inc(s("mem_in"), 16)

            def load(g, source, slot, first=False):
                if not first:
                    sp.wait_ge(w_lo, g - (NS - 1))
                width = source.shape[-1]
                sp.dma_start(stage[:, slot, 0:width], source).then_inc(w_landed[slot], 16)

            def load_run(start, count, source):
                n = count // NS
                with sp.Fori(0, n) as i:
                    for j in range(NS):
                        load(start + i * NS + j, source[i * NS + j], (start + j) % NS)
                for j in range(n * NS, count):
                    load(start + j, source[j], (start + j) % NS)

            for j in range(NS):
                load(j, a["w_a"][j], j, first=True)
            load_run(NS, G_OUT - NS, a["w_a"][NS:G_OUT])
            load_run(G_OUT, 8, a["w_a"][G_OUT:G_OUT + 8])
            sp.wait_ge(s("mix_done"), HEADS)
            sp.dma_start(h[:, :, :], a["xT"]).then_inc(s("x_back"), 16)
            load_run(G_OUT + 8, G_DOWN - G_OUT - 8, a["w_a"][G_OUT + 8:G_DOWN])
            load_run(G_DOWN, 4, a["w_down"][0:4])
            sp.wait_ge(w_used, G_DOWN)
            sp.dma_start(p_raw[:, :, :], a["pT"]).then_inc(s("p_in"), 16)
            load_run(G_DOWN + 4, G_PE - G_DOWN - 4, a["w_down"][4:])
            load_run(G_PE, G_CONV + 4 - G_PE, a["w_b"])
            sp.wait_ge(*event("h3_ms"))
            sp.dma_start(bias_fox, a["bias_fox"]).then_inc(s("fox_in"), 16)
            sp.dma_start(wfg[:, :, :], a["wfg"]).then_inc(s("fox_in"), 16)
            load_run(G_CONV + 4, N_BLOCKS - G_CONV - 4, a["w_b"][G_CONV + 4 - G_PE:])
            for c in range(4):
                sp.wait_ge(s("o_ready"), 4 * c + 4)
                sp.dma_start(out[:, 4 * c:4 * c + 4, :], o_out[:, 4 * c:4 * c + 4, :]).then_inc(s("out_done"), 16)
            sp.wait_ge(s("out_done"), 4 * 16)

        @block.scalar
        def _(act):
            chain = Chain(act, scalar_step)
            link = chain.link

            def hi(g, slot, first=False):
                act.wait_ge(w_landed[slot % NS], 16 * (g // NS + 1))
                if not first:
                    act.wait_ge(w_used, g - 1)
                act.activation(whi[:, slot % 2, :], stage[:, slot % NS, :], ACT.Copy).then_inc(w_hi, 1)

            def hi_at(start, i, per, j, first=False):
                act.wait_ge(w_landed[(start + j) % NS], i * (16 * per // NS) + 16 * ((start + j) // NS + 1))
                if not first:
                    act.wait_ge(w_used, i * per + (start + j - 1))
                act.activation(whi[:, (start + j) % 2, :], stage[:, (start + j) % NS, :], ACT.Copy).then_inc(w_hi, 1)

            def evac(u, b, ahead=0, made=None):
                act.wait_ge(w_used if made is None else part_made, u + ahead + 1 if made is None else made)
                act.wait_ge(out_free, u + 1)
                act.activation(small[:, b, :], ps[:, b, T:2 * T], ACT.Copy).then_inc(small_ready, 1)

            def inverse_root(t, waits, done):
                act.wait_ge(*waits)
                link(act.activation(t, t, ACT.Ln))
                act.activation(t, t, ACT.Exp, scale=-0.5).then_inc(done, 1)

            def norm(t, name):
                inverse_root(t, event(name + "_ms"), event(name + "_norm")[0])

            def split_hi(dst, src, done, scale=1.0):
                act.activation(dst, src, ACT.Copy, scale=scale).then_inc(s(done), 1)

            act.wait_ge(s("consts_in"), 7 * 16)
            act.wait_ge(s("x_in"), 16)
            act.activation(squares[:, :, :], h[:, :, :], ACT.Square).then_inc(event("x_sq")[0], 1)
            for k in range(KT):
                split_hi(act_a[:, k, 0:T], h[:, k, :], "xs_x_hi", column("ln_mix_pre", k))
            hi_at(G_MIX, 0, 8, 0, first=True)
            act.wait_ge(s("mem_in"), 16)
            act.wait_ge(*event("x_sum"))
            act.activation(squares[:, :, :], mem_raw[:, :, :], ACT.Square).then_inc(event("mem_sq")[0], 1)
            for k in range(KT):
                split_hi(xs_mem[:, k, 0:T], mem_raw[:, k, :], "xs_mem_hi", column("mem_norm_g_2", k))

            norm(rstd[:, :], "x")
            norm(rstd_mem[:, :], "mem")
            hi_at(G_MIX, 0, 8, 1, first=True)
            with act.Fori(0, HEADS) as i:
                chain.enter(i, 1)
                u = i * 8
                evac(u, 0)
                hi_at(G_MIX, i, 8, 2)
                act.wait_ge(s("hf_lin"), i + 1)
                act.activation(ef[:, :], hfx[:, :], ACT.Exp, scale=-1.0).then_inc(s("hf_exp"), 1)
                evac(u + 1, 1)
                hi_at(G_MIX, i, 8, 3)
                act.wait_ge(s("hq_lin"), i + 1)
                act.activation(eq[:, :], hqx[:, :], ACT.Exp, scale=-1.0).then_inc(s("hq_exp"), 1)
                evac(u + 2, 0)
                hi_at(G_MIX, i, 8, 4)
                evac(u + 3, 1)
                hi_at(G_MIX, i, 8, 5)
                act.wait_ge(s("i_turned"), i + 1)
                act.activation(vtok[:, :, :], ps_t[:, 0:T].rearrange("p (a b) -> p a b", a=2), ACT.Copy).then_inc(s("vtok_ready"), 1)
                evac(u + 4, 0)
                hi_at(G_MIX, i, 8, 6)
                act.wait_ge(s("lev_ready"), i * 5 + 5)
                act.activation(sT[:, P:2 * P], ps_lev[:, 0, 0, 0:P], ACT.Copy).then_inc(s("cross_ready"), 1)
                evac(u + 5, 1)
                hi_at(G_MIX, i, 8, 7)
                act.wait_ge(s("att_max"), i + 1)
                act.activation(sm[:, 0:P], sm[:, 0:P], ACT.Exp, bias=cols[:, 2:3]).then_inc(s("att_exp"), 1)
                act.activation(sm[:, P:3 * P], sm[:, P:3 * P], ACT.Exp, bias=cols[:, 3:4]).then_inc(s("att_exp"), 1)
                evac(u + 6, 0)
                hi_at(G_MIX, i, 8, 8)
                act.wait_ge(s("hg_lin"), i + 1)
                act.activation(eg[:, :], hgx[:, :], ACT.Exp, scale=-1.0).then_inc(s("hg_exp"), 1)
                act.wait_ge(s("av_turned"), i + 1)
                act.activation(avtok[:, :, :], ps_t[:, 0:T].rearrange("p (a b) -> p a b", a=2), ACT.Copy).then_inc(s("avtok_ready"), 1)
                act.wait_ge(s("hg_out"), i + 1)
                act.activation(osq[:, :], ps_a, ACT.Square).then_inc(s("osq_ready"), 1)
                evac(u + 7, 1)
                hi_at(G_MIX, i, 8, 9)
                act.wait_ge(s("p_turned"), i + 1)
                act.activation(pT[:, :], ps_t[:, 0:3 * P], ACT.Copy).then_inc(s("pT_ready"), 1)
                act.wait_ge(s("att_out"), i + 1)
                act.activation(xs_mix[:, bass.ds(HEADS + i, 1), 0:T], ps_b.unsqueeze(1), ACT.Copy).then_inc(s("att_hi"), 1)
                inverse_root(var[:, :], (s("var_ready"), i + 1), s("o_norm"))
                act.wait_ge(s("o_done"), i + 1)
                act.activation(xs_mix[:, bass.ds(i, 1), 0:T], osb[:, :].unsqueeze(1), ACT.Copy).then_inc(s("o_hi"), 1)
                chain.leave(HEADS)

            with act.Fori(0, 4) as i:
                for j in range(4):
                    evac(U_OUT + 4 * i + j, j % 2)
                    hi_at(G_OUT, i, 4, j + 2)
            norm(rstd[:, :], "mixed")
            for k in range(KT):
                act.wait_ge(s("h1_ready"), k + 1)
                split_hi(act_a[:, k, 0:T], h[:, k, :], "xs_u_hi", column("ln_ffn_pre", k))
                act.activation(mixed[:, k, :], h[:, k, :], ACT.Square).then_inc(s("h1_sq"), 1)

            norm(rstd[:, :], "h1")
            with act.Fori(0, FT // 2) as i:
                for q in range(2):
                    u = U_UP + 4 * i + 2 * q
                    pair = 2 * i + q
                    evac(u, 0)
                    hi_at(G_UP, i, 4, 2 * q + 2)
                    evac(u + 1, 1)
                    hi_at(G_UP, i, 4, 2 * q + 3)
                    act.wait_ge(s("gate_conv"), pair + 1)
                    act.activation(gl[:, :], cy[:, 0, :], ACT.Gelu_apprx_tanh).then_inc(s("gelu_done"), 1)
                    act.wait_ge(s("gv_done"), pair + 1)
                    act.activation(big[:, bass.ds(pair, 1), 0:T], cy[:, 1:2, :], ACT.Copy).then_inc(s("xs_g_hi"), 1)
            with act.Fori(0, KT // 2) as i:
                for j in range(8):
                    if j % 4 == 3:
                        act.wait_ge(w_used, G_DOWN + 8 * i + j + 1)
                        act.wait_ge(out_free, U_DOWN + 2 * i + j // 4 + 1)
                        act.activation(small[:, j // 4, :], ps[:, j // 4, T:2 * T], ACT.Copy).then_inc(small_ready, 1)
                    hi_at(G_DOWN, i, 8, j + 2)
            act.wait_ge(s("p_in"), 16)
            for k in range(2):
                split_hi(xs_p[:, k, 0:T], p_raw[:, k, :], "xs_p_hi")
            for blk in range(2):
                for j in range(8):
                    if j < 7:
                        evac(U_PE + 8 * blk + j, j % 2, made=7 * blk + j + 1)
                    else:
                        evac(U_PE + 8 * blk + j, j % 2, ahead=G_PE + blk - (U_PE + 8 * blk + j))
                hi(G_PE + 2 + blk, G_PE + 2 + blk)
                if blk == 0:
                    norm(rstd[:, :], "y")
            for k in range(KT):
                act.wait_ge(s("h2_ready"), k + 1)
                split_hi(xs_h[:, k, 0:T], h[:, k, :], "xs_h_hi")

            with act.Fori(0, 4) as i:
                for j in range(4):
                    u = U_PG + 4 * i + j
                    evac(u, j % 2, G_PG - U_PG)
                    hi_at(G_PG, i, 4, j + 2)
                    act.wait_ge(s("pg_ready"), 4 * i + j + 1)
                    act.activation(pg_s[:, j % 2, :], pg_x[:, j % 2, :], ACT.Sigmoid).then_inc(s("pg_sig"), 1)
                    act.wait_ge(s("h3_ready"), 4 * i + j + 1)
                    act.activation(act_a[:, bass.ds(4 * i + j, 1), 0:T], h[:, bass.ds(4 * i + j, 1), :], ACT.Copy,
                                   scale=column("norm_g_2", 4 * i + j)).then_inc(s("xs_n_hi"), 1)

            norm(rstd[:, :], "h3")
            with act.Fori(0, 2) as i:
                for q in range(2):
                    u = U_CONV + 4 * i + 2 * q
                    evac(u, 0, G_PG - U_PG)
                    hi_at(G_CONV, i, 4, 2 * q + 2)
                    evac(u + 1, 1, G_PG - U_PG)
                    hi_at(G_CONV, i, 4, 2 * q + 3)
                    act.wait_ge(s("cv_lin"), 2 * i + q + 1)
                    act.activation(ce[:, 0, :], cx[:, 1, :], ACT.Exp, scale=-1.0).then_inc(s("cv_exp"), 1)
            act.wait_ge(s("z_abs"), 1)
            act.activation(z1[:, :], z1[:, :], ACT.Exp, scale=-1.0).then_inc(s("z_exp"), 1)
            act.wait_ge(s("z_exp"), 1)
            act.activation(z1[:, :], z1[:, :], ACT.Ln, bias=1.0).then_inc(s("z_ln"), 1)

            with act.Fori(0, HEADS) as i:
                u = U_FOX + 4 * i
                evac(u, 0, G_PG - U_PG)
                hi_at(G_FOX, i, 4, 2)
                evac(u + 1, 1, G_PG - U_PG)
                hi_at(G_FOX, i, 4, 3)
                evac(u + 2, 0, G_PG - U_PG)
                hi_at(G_FOX, i, 4, 4)
                act.wait_ge(s("fox_max"), i + 1)
                act.activation(fs[:, 0:P], fs[:, 0:P], ACT.Exp, bias=cols[:, 10:11], accum_out=cols[:, 12:13]).then_inc(s("fox_exp"), 1)
                act.activation(fs[:, P:3 * P], fs[:, P:3 * P], ACT.Exp, bias=cols[:, 11:12], accum_out=cols[:, 13:14]).then_inc(s("fox_exp"), 1)
                evac(u + 3, 1, G_PG - U_PG)
                hi_at(G_FOX, i, 4, 5)
                act.wait_ge(s("fg_lin"), i + 1)
                act.activation(fge[:, :], fgx[:, :], ACT.Exp, scale=-1.0).then_inc(s("fg_exp"), 1)
                act.wait_ge(s("fv_turned"), i + 1)
                act.activation(fvtok[:, :, :], ps_b.rearrange("p (a b) -> p a b", a=2), ACT.Copy).then_inc(s("fvtok_ready"), 1)
                act.wait_ge(s("fp_turned"), i + 1)
                act.activation(fpT[:, 0:3 * P], ps_t[:, 0:3 * P], ACT.Copy).then_inc(s("fpT_ready"), 1)
                act.wait_ge(s("fo_done"), i + 1)
                act.activation(xs_y[:, bass.ds(GROUPS + i, 1), 0:T], fo[:, :].unsqueeze(1), ACT.Copy).then_inc(s("fo_hi"), 1)

            with act.Fori(0, 2) as i:
                for q in range(2):
                    u = U_MEM + 4 * i + 2 * q
                    n = 2 * i + q
                    act.wait_ge(s("mv_turned"), n)
                    act.activation(mv_h[:, :].unsqueeze(1), mkv[:, bass.ds(MEM_HEADS + n, 1), :], ACT.Copy).then_inc(s("mv_here"), 1)
                    evac(u, 0, G_PG - U_PG)
                    hi_at(G_MEM, i, 4, 2 * q + 2)
                    act.wait_ge(s("mem_max"), n + 1)
                    for t in range(2):
                        act.activation(fs[:, t * T:t * T + T], ps_sc[:, t * T:t * T + T], ACT.Exp, bias=cols[:, 20 + t:21 + t],
                                       accum_out=cols[:, 22 + t:23 + t]).then_inc(s("mem_exp"), 1)
                    evac(u + 1, 1, G_PG - U_PG)
                    hi_at(G_MEM, i, 4, 2 * q + 3)
                    act.wait_ge(s("mg_lin"), n + 1)
                    act.activation(fge[:, :], fgx[:, :], ACT.Exp, scale=-1.0).then_inc(s("mg_exp"), 1)
                    act.wait_ge(s("mv_turned"), n + 1)
                    act.activation(fvtok[:, :, :], ps_b.rearrange("p (a b) -> p a b", a=2), ACT.Copy).then_inc(s("mvtok_ready"), 1)
                    act.wait_ge(s("mp_turned"), n + 1)
                    act.activation(fpT[:, :], ps_t[:, :], ACT.Copy).then_inc(s("mpT_ready"), 1)
                    act.wait_ge(s("mo_done"), n + 1)
                    act.activation(xs_y[:, bass.ds(GROUPS + HEADS + n, 1), 0:T], fo[:, :].unsqueeze(1), ACT.Copy).then_inc(s("mo_hi"), 1)

            norm(mu[:, :], "uc")
            act.wait_ge(s("cl_ready"), 1)
            act.activation(usq[:, :, :], uc[:, :, :], ACT.Sigmoid).then_inc(s("cl_sig"), 1)
            for k in range(GROUPS):
                act.wait_ge(s("cs_ready"), 1)
                split_hi(xs_cv[:, k, 0:T], uc[:, k, :], "xs_cv_hi")
            for k in range(GROUPS):
                evac(U_CG + k, k % 2, G_CG - U_CG)
                hi(G_CG + k + 2, G_CG + k + 2)
                act.wait_ge(s("cg_lin"), k + 1)
                act.activation(ce[:, k % 2, :], sg_c[:, k, :], ACT.Exp, scale=-1.0).then_inc(s("cg_exp"), 1)
            for k in range(GROUPS):
                if k < GROUPS - 1:
                    evac(U_PW + k, k % 2, made=14 + k + 1)
                else:
                    evac(U_PW + k, k % 2, ahead=G_PW - U_PW - k)
                act.wait_ge(s("yc_ready"), k + 1)
                split_hi(xs_y[:, k, 0:T], cx[:, k % 2, :], "xs_yc_hi")
            hi(G_PW + 2, G_PW + 2)

            with act.Fori(0, 3) as i:
                for j in range(4):
                    evac(U_OUT2 + 4 * i + j, j % 2, G_OUT2 - U_OUT2)
                    hi_at(G_OUT2, i, 4, j + 2)
            for j in range(4):
                evac(U_OUT2 + 12 + j, j % 2, G_OUT2 - U_OUT2)
                if j < 2:
                    hi(G_OUT2 + 12 + j + 2, G_OUT2 + 12 + j + 2)
            norm(rstd[:, :], "h4")

        @block.vector
        def _(dve):
            chain = Chain(dve, vector_step)
            link = chain.link

            def lo(start, i, per, j):
                dve.wait_ge(w_hi, i * per + (start + j + 1))
                dve.tensor_tensor(wlo[:, (start + j) % 2, :], stage[:, (start + j) % NS, :],
                                  whi[:, (start + j) % 2, :].bitcast(F32), ALU.subtract).then_inc(w_lo, 1)

            def add(u, b, dst=None):
                dve.wait_ge(small_ready, u + 1)
                dve.tensor_tensor(tmp[:, b, :] if dst is None else dst, ps[:, b, 0:T], small[:, b, :],
                                  ALU.add).then_inc(out_free, 1)

            def scaled(u, b, dst, done, by=None, factor=None):
                dve.wait_ge(out_free, u + 3)
                by = rstd[:, :] if by is None else by
                if factor is None:
                    dve.tensor_tensor(dst, tmp[:, b, :], by, ALU.mult).then_inc(s(done), 1)
                else:
                    dve.scalar_tensor_tensor(out=dst, in0=tmp[:, b, :], scalar=factor, in1=by,
                                             op0=ALU.mult, op1=ALU.mult).then_inc(s(done), 1)

            def logistic(e, exp_done, n):
                dve.wait_ge(s(exp_done), n)
                link(dve.tensor_scalar(e, e, LARGE, 1.0, ALU.min, ALU.add))
                link(dve.reciprocal(e, e))

            def mean_square(src, n, done):
                dve.tensor_scalar(n, src, 1.0 / D, EPS, ALU.mult, ALU.add).then_inc(event(done)[0], 1)

            dve.memset(dummy[:, :], 0.0).then_inc(out_free, 2)
            dve.wait_ge(*event("x_sq"))
            dve.tensor_reduce(acc[:, :], squares[:, :, :].rearrange("p k t -> p t k"), AX_X, ALU.add).then_inc(event("x_sum")[0], 1)
            for k in range(KT):
                dve.wait_ge(s("xs_x_hi"), k + 1)
                dve.scalar_tensor_tensor(out=act_a[:, k, T:2 * T], in0=h[:, k, :], scalar=column("ln_mix_pre", k),
                                         in1=act_a[:, k, 0:T].bitcast(F32), op0=ALU.mult, op1=ALU.subtract)\
                   .then_inc(s("xs_x"), 1)
            lo(G_MIX, 0, 8, 0)
            dve.wait_ge(*event("x_summed"))
            mean_square(ps_a, rstd[:, :], "x_ms")
            dve.wait_ge(*event("mem_sq"))
            dve.tensor_reduce(acc[:, :], squares[:, :, :].rearrange("p k t -> p t k"), AX_X, ALU.add).then_inc(event("mem_sum")[0], 1)
            for k in range(KT):
                dve.wait_ge(s("xs_mem_hi"), k + 1)
                dve.scalar_tensor_tensor(out=xs_mem[:, k, T:2 * T], in0=mem_raw[:, k, :], scalar=column("mem_norm_g_2", k),
                                         in1=xs_mem[:, k, 0:T].bitcast(F32), op0=ALU.mult, op1=ALU.subtract)\
                   .then_inc(s("xs_mem"), 1)
            dve.wait_ge(*event("mem_summed"))
            mean_square(ps_b, rstd_mem[:, :], "mem_ms")
            link(dve.memset(sT[:, :], 0.0))
            lb, omlb, ex = cols[:, 16:24], cols[:, 24:32], cols[:, 8:16]
            link(dve.tensor_tensor(ex, column("lb", 0, HEADS), column("lb", 0, HEADS), ALU.subtract))
            link(dve.tensor_scalar(ex, ex, 1.0, None, ALU.add))
            link(dve.tensor_tensor(lb, ex, ex, ALU.subtract))
            link(dve.tensor_scalar(omlb, lb, -1.0, 1.0, ALU.mult, ALU.add))
            lo(G_MIX, 0, 8, 1)
            dve.wait_ge(*event("x_norm"))
            dve.wait_ge(*event("mem_norm"))
            dve.wait_ge(s("lmask_ready"), 1)

            with dve.Fori(0, HEADS) as i:
                chain.enter(i, 17)
                u = i * 8
                add(u, 0)
                lo(G_MIX, i, 8, 2)
                scaled(u, 0, hfx[:, :], "hf_lin")
                add(u + 1, 1)
                lo(G_MIX, i, 8, 3)
                scaled(u + 1, 1, hqx[:, :], "hq_lin")
                logistic(ef[:, :], "hf_exp", i + 1)
                dve.wait_ge(s("lev_in_ready"), i * LEVELS)
                dve.wait_ge(s("lev_ready"), i * 5)
                link(dve.tensor_scalar(pfx[:, :], ef[:, :], cols[:, bass.ds(24 + i, 1)], cols[:, bass.ds(16 + i, 1)],
                                       ALU.mult, ALU.add))
                dve.tensor_scalar(kk[:, :], pfx[:, :], -1.0, 1.0, ALU.mult, ALU.add).then_inc(s("fk_ready"), 1)
                add(u + 2, 0)
                lo(G_MIX, i, 8, 4)
                scaled(u + 2, 0, iT[:, :], "i_ready")
                logistic(eq[:, :], "hq_exp", i + 1)
                dve.tensor_tensor(qq[:, :], hqx[:, :], eq[:, :], ALU.mult).then_inc(s("q_ready"), 1)
                add(u + 3, 1)
                lo(G_MIX, i, 8, 5)
                dve.wait_ge(s("sc_ready"), i)
                scaled(u + 3, 1, aqT[:, :], "aq_ready", factor=SCALE)
                add(u + 4, 0)
                lo(G_MIX, i, 8, 6)
                scaled(u + 4, 0, akT[:, :], "ak_ready")
                dve.wait_ge(s("hg_out"), i)
                diag = sT[:, :].rearrange("p (c t) -> p c t", c=3)[:, 0:3:2, :]
                for n in range(LEVELS):
                    if n % 2 == 0:
                        dve.wait_ge(s("lev_ready"), i * 5 + n // 2 + 1)
                    dve.wait_ge(s("lev_used"), i * LEVELS + n)
                    dve.memset(dummy[:, 0:1], 0.0)
                    dve.copy_predicated(diag, lmask[:, n, :].rearrange("p (c t) -> p c t", c=2),
                                        ps_lev[:, n // 2 % 2, n % 2, :].rearrange("p (c t) -> p c t", c=2)).then_inc(s("lev_used"), 1)
                add(u + 5, 1)
                lo(G_MIX, i, 8, 7)
                scaled(u + 5, 1, avT[:, :], "av_ready")
                dve.wait_ge(s("sc_ready"), i + 1)
                dve.wait_ge(s("p_turned"), i)
                link(dve.tensor_tensor(sm[:, :], ps_sc[:, 0:3 * P], bias_att[:, :], ALU.add))
                link(dve.tensor_reduce(cols[:, 0:1], sm[:, 0:P], AX_X, ALU.max))
                link(dve.tensor_reduce(cols[:, 1:2], sm[:, P:3 * P], AX_X, ALU.max))
                dve.tensor_scalar(cols[:, 2:4], cols[:, 0:2], -1.0, None, ALU.mult).then_inc(s("att_max"), 1)
                add(u + 6, 0)
                lo(G_MIX, i, 8, 8)
                scaled(u + 6, 0, hgx[:, :], "hg_lin")
                dve.wait_ge(s("att_exp"), 2 * i + 2)
                link(dve.tensor_tensor(sm[:, :], sm[:, :], mult[:, :], ALU.mult))
                link(dve.tensor_reduce(cols[:, 4:5], sm[:, 0:P], AX_X, ALU.add))
                link(dve.tensor_reduce(cols[:, 5:6], sm[:, P:3 * P], AX_X, ALU.add))
                link(dve.reciprocal(cols[:, 6:8], cols[:, 4:6]))
                dve.tensor_scalar(sm[:, 0:P], sm[:, 0:P], cols[:, 6:7], None, ALU.mult).then_inc(s("p_ready"), 1)
                dve.tensor_scalar(sm[:, P:3 * P], sm[:, P:3 * P], cols[:, 7:8], None, ALU.mult).then_inc(s("p_ready"), 1)
                logistic(eg[:, :], "hg_exp", i + 1)
                link(dve.tensor_tensor(eg[:, :], eg[:, :], hgx[:, :], ALU.mult))
                dve.wait_ge(s("osq_ready"), i + 1)
                link(dve.tensor_scalar(on1[:, :], ps_a, column("hgrn_norm", i), None, ALU.mult))
                link(dve.tensor_tensor(on1[:, :], on1[:, :], eg[:, :], ALU.mult))
                dve.wait_ge(s("o_summed"), i + 1)
                dve.tensor_scalar(var[:, :], ps_lev[:, 1, 0, :], 1.0 / P, EPS, ALU.mult, ALU.add).then_inc(s("var_ready"), 1)
                add(u + 7, 1)
                lo(G_MIX, i, 8, 9)
                dve.wait_ge(out_free, u + 10)
                dve.tensor_tensor(mkv[:, bass.ds(i, 1), :], tmp[:, 1:2, :], rstd_mem[:, :].unsqueeze(1), ALU.mult)\
                   .then_inc(s("mkv_ready"), 1)
                dve.wait_ge(s("o_norm"), i + 1)
                dve.wait_ge(s("o_hi"), i)
                dve.tensor_tensor(osb[:, :], on1[:, :], var[:, :], ALU.mult).then_inc(s("o_done"), 1)
                dve.wait_ge(s("att_hi"), i + 1)
                dve.tensor_tensor(xs_mix[:, bass.ds(HEADS + i, 1), T:2 * T], ps_b.unsqueeze(1),
                                  xs_mix[:, bass.ds(HEADS + i, 1), 0:T].bitcast(F32), ALU.subtract).then_inc(s("att_split"), 1)
                dve.wait_ge(s("o_hi"), i + 1)
                dve.tensor_tensor(xs_mix[:, bass.ds(i, 1), T:2 * T], osb[:, :].unsqueeze(1),
                                  xs_mix[:, bass.ds(i, 1), 0:T].bitcast(F32), ALU.subtract).then_inc(s("mix_done"), 1)
                chain.leave(HEADS)

            with dve.Fori(0, 4) as i:
                for j in range(4):
                    add(U_OUT + 4 * i + j, j % 2, dst=mixed[:, bass.ds(4 * i + j, 1), :].squeeze(1))
                    lo(G_OUT, i, 4, j + 2)
            dve.wait_ge(*event("mixed_summed"))
            mean_square(ps_a, rstd[:, :], "mixed_ms")
            dve.wait_ge(s("x_back"), 16)
            dve.wait_ge(*event("mixed_norm"))

            def low_u(k):
                dve.wait_ge(s("xs_u_hi"), k + 1)
                dve.scalar_tensor_tensor(out=act_a[:, k, T:2 * T], in0=h[:, k, :], scalar=column("ln_ffn_pre", k),
                                         in1=act_a[:, k, 0:T].bitcast(F32), op0=ALU.mult, op1=ALU.subtract)\
                   .then_inc(s("xs_u"), 1)

            for k in range(KT):
                link(dve.tensor_tensor(t_res[:, k % 2, :], mixed[:, k, :], rstd[:, :], ALU.mult))
                dve.scalar_tensor_tensor(out=h[:, k, :], in0=t_res[:, k % 2, :], scalar=column("ln_mix_post", k),
                                         in1=h[:, k, :], op0=ALU.mult, op1=ALU.add).then_inc(s("h1_ready"), 1)
                if k:
                    low_u(k - 1)
            low_u(KT - 1)
            link(dve.memset(upb[:, :, 0:2], 0.0))
            dve.wait_ge(*event("h1_summed"))
            mean_square(ps_b, rstd[:, :], "h1_ms")

            def conv(block, b, done):
                w = [vec[:, bass.ds(V["conv"] + 4 * block + c, 1)] for c in range(4)]
                dve.wait_ge(s("up_ready"), block + 1)
                link(dve.tensor_scalar(cy[:, b, :], upb[:, b, 2:T + 2], w[2], w[3], ALU.mult, ALU.add))
                link(dve.scalar_tensor_tensor(out=cy[:, b, :], in0=upb[:, b, 1:T + 1], scalar=w[1], in1=cy[:, b, :],
                                              op0=ALU.mult, op1=ALU.add))
                dve.scalar_tensor_tensor(out=cy[:, b, :], in0=upb[:, b, 0:T], scalar=w[0], in1=cy[:, b, :],
                                         op0=ALU.mult, op1=ALU.add).then_inc(s(done), 1)

            with dve.Fori(0, FT // 2) as i:
                chain.enter(i, 8)
                for q in range(2):
                    u = U_UP + 4 * i + 2 * q
                    pair = 2 * i + q
                    dve.wait_ge(s("up_ready"), 2 * pair)
                    add(u, 0)
                    lo(G_UP, i, 4, 2 * q + 2)
                    add(u + 1, 1)
                    lo(G_UP, i, 4, 2 * q + 3)
                    dve.wait_ge(s("xs_g_hi"), pair)
                    conv(2 * pair, 0, "gate_conv")
                    conv(2 * pair + 1, 1, "val_conv")
                    dve.wait_ge(s("gelu_done"), pair + 1)
                    dve.wait_ge(s("val_conv"), pair + 1)
                    dve.tensor_tensor(cy[:, 1, :], cy[:, 1, :], gl[:, :], ALU.mult).then_inc(s("gv_done"), 1)
                    dve.wait_ge(s("xs_g_hi"), pair + 1)
                    dve.tensor_tensor(big[:, bass.ds(pair, 1), T:2 * T], cy[:, 1:2, :],
                                      big[:, bass.ds(pair, 1), 0:T].bitcast(F32), ALU.subtract).then_inc(s("xs_g"), 1)
                chain.leave(FT // 2)
            with dve.Fori(0, KT // 2) as i:
                for j in range(8):
                    if j % 4 == 3:
                        add(U_DOWN + 2 * i + j // 4, j // 4, dst=y[:, bass.ds(2 * i + j // 4, 1), :].squeeze(1))
                    lo(G_DOWN, i, 8, j + 2)
            for k in range(2):
                dve.wait_ge(s("xs_p_hi"), k + 1)
                dve.tensor_tensor(xs_p[:, k, T:2 * T], p_raw[:, k, :], xs_p[:, k, 0:T].bitcast(F32),
                                  ALU.subtract).then_inc(s("xs_p"), 1)
            for blk in range(2):
                for j in range(8):
                    add(U_PE + 8 * blk + j, j % 2, dst=pe_out[:, 8 * blk + j, :])
                lo(G_PE, 0, 0, blk + 2)
                if blk == 0:
                    dve.wait_ge(*event("y_summed"))
                    mean_square(ps_a, rstd[:, :], "y_ms")
            dve.wait_ge(*event("y_norm"))

            def low_h(k):
                dve.wait_ge(s("xs_h_hi"), k + 1)
                dve.tensor_tensor(xs_h[:, k, T:2 * T], h[:, k, :], xs_h[:, k, 0:T].bitcast(F32),
                                  ALU.subtract).then_inc(s("xs_h"), 1)

            for k in range(KT):
                link(dve.tensor_tensor(t_res2[:, k % 2, :], y[:, k, :], rstd[:, :], ALU.mult))
                dve.scalar_tensor_tensor(out=h[:, k, :], in0=t_res2[:, k % 2, :], scalar=column("ln_ffn_post", k),
                                         in1=h[:, k, :], op0=ALU.mult, op1=ALU.add).then_inc(s("h2_ready"), 1)
                if k:
                    low_h(k - 1)
            low_h(KT - 1)

            with dve.Fori(0, 4) as i:
                chain.enter(i, 4)
                for j in range(4):
                    u = U_PG + 4 * i + j
                    k = 4 * i + j
                    add(u, j % 2, dst=pg_x[:, j % 2, :])
                    lo(G_PG, i, 4, j + 2)
                    dve.wait_ge(out_free, u + 3)
                    dve.tensor_scalar(dummy[:, 0:1], pg_x[:, j % 2, 0:1], 1.0, None, ALU.mult).then_inc(s("pg_ready"), 1)
                    dve.wait_ge(s("pg_sig"), k + 1)
                    link(dve.tensor_tensor(pg_s[:, j % 2:j % 2 + 1, :], pg_s[:, j % 2:j % 2 + 1, :], pe_out[:, bass.ds(k, 1), :], ALU.mult))
                    dve.tensor_tensor(h[:, bass.ds(k, 1), :], h[:, bass.ds(k, 1), :], pg_s[:, j % 2:j % 2 + 1, :], ALU.add)\
                       .then_inc(s("h3_ready"), 1)
                    dve.wait_ge(s("xs_n_hi"), k + 1)
                    dve.scalar_tensor_tensor(out=act_a[:, bass.ds(k, 1), T:2 * T], in0=h[:, bass.ds(k, 1), :],
                                             scalar=column("norm_g_2", k), in1=act_a[:, bass.ds(k, 1), 0:T].bitcast(F32),
                                             op0=ALU.mult, op1=ALU.subtract).then_inc(s("xs_n"), 1)
                chain.leave(4)
            dve.wait_ge(*event("h3_summed"))
            mean_square(ps_b, rstd[:, :], "h3_ms")
            link(dve.memset(upad[:, :, :], 0.0))
            link(dve.memset(one8[:, :], 1.0))
            dve.wait_ge(*event("h3_norm"))

            dve.wait_ge(s("fox_in"), 32)
            dve.tensor_tensor(wfg[:, :, :], wfg[:, :, :],
                              column("norm_g_2", 0, KT).unsqueeze(2).to_broadcast([P, KT, HEADS]), ALU.mult).then_inc(s("wfg_ready"), 1)
            with dve.Fori(0, 2) as i:
                chain.enter(i, 4)
                for q in range(2):
                    u = U_CONV + 4 * i + 2 * q
                    n = 2 * i + q
                    add(u, 0)
                    lo(G_CONV, i, 4, 2 * q + 2)
                    scaled(u, 0, cx[:, 0, :], "ca_lin")
                    add(u + 1, 1)
                    lo(G_CONV, i, 4, 2 * q + 3)
                    scaled(u + 1, 1, cx[:, 1, :], "cv_lin")
                    logistic(ce[:, 0, :], "cv_exp", n + 1)
                    dve.wait_ge(s("ca_lin"), n + 1)
                    dve.tensor_tensor(upad[:, bass.ds(n, 1), TAPS - 1:], cx[:, 0:1, :], ce[:, 0:1, :], ALU.mult).then_inc(s("u_ready"), 1)
                chain.leave(2)

            dve.wait_ge(s("fl_ready"), 1)
            link(dve.tensor_tensor(zf[:, :], ps_t[0:HEADS, 0:T], rstd[0:HEADS, :], ALU.mult))
            link(dve.tensor_scalar(zf[:, :], zf[:, :], bfox[:, 0:1], None, ALU.add))
            link(dve.tensor_scalar(z1[:, :], zf[:, :], -1.0, None, ALU.mult))
            dve.tensor_tensor(z1[:, :], zf[:, :], z1[:, :], ALU.max).then_inc(s("z_abs"), 1)
            link(dve.tensor_scalar(zf[:, :], zf[:, :], 0.0, None, ALU.min))
            dve.wait_ge(s("z_ln"), 1)
            link(dve.tensor_tensor(z2[:, :], zf[:, :], z1[:, :], ALU.subtract))
            link(dve.tensor_tensor_scan(cc[:, :], one8[:, :], z2[:, :], 0.0, ALU.mult, ALU.add))

            with dve.Fori(0, HEADS) as i:
                chain.enter(i, 7)
                u = U_FOX + 4 * i
                add(u, 0)
                lo(G_FOX, i, 4, 2)
                dve.wait_ge(s("fsc_ready"), i)
                scaled(u, 0, fqT[:, :], "fq_ready", factor=SCALE)
                dve.tensor_scalar(cpos[:, :], cc[:, :], ident[0:HEADS, bass.ds(i, 1)], None, ALU.mult).then_inc(s("c_ready"), 1)
                dve.tensor_scalar(cneg[:, :], cc[:, :], ident[0:HEADS, bass.ds(i, 1)], -1.0, ALU.mult, ALU.mult).then_inc(s("c_ready"), 1)
                add(u + 1, 1)
                lo(G_FOX, i, 4, 3)
                scaled(u + 1, 1, fkT[:, :], "fk2_ready")
                add(u + 2, 0)
                lo(G_FOX, i, 4, 4)
                scaled(u + 2, 0, fvT[:, :], "fv_ready")
                dve.wait_ge(s("fsc_ready"), i + 1)
                dve.wait_ge(s("fp_turned"), i)
                link(dve.tensor_tensor(fs[:, 0:3 * P], ps_sc[:, 0:3 * P], bias_fox, ALU.add))
                link(dve.tensor_reduce(cols[:, 8:9], fs[:, 0:P], AX_X, ALU.max))
                link(dve.tensor_reduce(cols[:, 9:10], fs[:, P:3 * P], AX_X, ALU.max))
                dve.tensor_scalar(cols[:, 10:12], cols[:, 8:10], -1.0, None, ALU.mult).then_inc(s("fox_max"), 1)
                add(u + 3, 1)
                lo(G_FOX, i, 4, 5)
                scaled(u + 3, 1, fgx[:, :], "fg_lin")
                dve.wait_ge(s("fox_exp"), 2 * i + 2)
                link(dve.reciprocal(cols[:, 14:16], cols[:, 12:14]))
                dve.tensor_scalar(fs[:, 0:P], fs[:, 0:P], cols[:, 14:15], None, ALU.mult).then_inc(s("fp_ready"), 1)
                dve.tensor_scalar(fs[:, P:3 * P], fs[:, P:3 * P], cols[:, 15:16], None, ALU.mult).then_inc(s("fp_ready"), 1)
                logistic(fge[:, :], "fg_exp", i + 1)
                link(dve.tensor_tensor(fge[:, :], fge[:, :], fgx[:, :], ALU.mult))
                dve.wait_ge(s("fo_ready"), i + 1)
                dve.wait_ge(s("fo_hi"), i)
                dve.tensor_tensor(fo[:, :], ps_a, fge[:, :], ALU.mult).then_inc(s("fo_done"), 1)
                dve.wait_ge(s("fo_hi"), i + 1)
                dve.tensor_tensor(xs_y[:, bass.ds(GROUPS + i, 1), T:2 * T], fo[:, :].unsqueeze(1),
                                  xs_y[:, bass.ds(GROUPS + i, 1), 0:T].bitcast(F32), ALU.subtract).then_inc(s("fo_split"), 1)
                chain.leave(HEADS)

            dve.wait_ge(*event("uc_summed"))
            link(dve.tensor_scalar(mu[:, :], ps_b, 1.0 / (GROUPS * P), None, ALU.mult))
            for k in range(GROUPS):
                link(dve.tensor_tensor(uc[:, k, :], uc[:, k, :], mu[:, :], ALU.subtract))
            dve.tensor_tensor(usq[:, :, :], uc[:, :, :], uc[:, :, :], ALU.mult).then_inc(s("usq_ready"), 1)

            with dve.Fori(0, 2) as i:
                chain.enter(i, 10)
                for q in range(2):
                    u = U_MEM + 4 * i + 2 * q
                    n = 2 * i + q
                    add(u, 0)
                    lo(G_MEM, i, 4, 2 * q + 2)
                    scaled(u, 0, fqT[:, :], "mq_ready", factor=SCALE)
                    dve.wait_ge(s("msc_ready"), n + 1)
                    link(dve.tensor_reduce(cols[:, 18:20], ps_sc[:, :].rearrange("p (c t) -> p c t", c=2), AX_X, ALU.max))
                    dve.tensor_scalar(cols[:, 20:22], cols[:, 18:20], -1.0, None, ALU.mult).then_inc(s("mem_max"), 1)
                    add(u + 1, 1)
                    lo(G_MEM, i, 4, 2 * q + 3)
                    scaled(u + 1, 1, fgx[:, :], "mg_lin")
                    dve.wait_ge(s("mem_exp"), 2 * n + 2)
                    link(dve.reciprocal(cols[:, 24:26], cols[:, 22:24]))
                    for t in range(2):
                        dve.tensor_scalar(fs[:, t * T:t * T + T], fs[:, t * T:t * T + T], cols[:, 24 + t:25 + t], None,
                                          ALU.mult).then_inc(s("mp_ready"), 1)
                    logistic(fge[:, :], "mg_exp", n + 1)
                    link(dve.tensor_tensor(fge[:, :], fge[:, :], fgx[:, :], ALU.mult))
                    dve.wait_ge(s("mo_ready"), n + 1)
                    dve.tensor_tensor(fo[:, :], ps_a, fge[:, :], ALU.mult).then_inc(s("mo_done"), 1)
                    dve.wait_ge(s("mo_hi"), n + 1)
                    dve.tensor_tensor(xs_y[:, bass.ds(GROUPS + HEADS + n, 1), T:2 * T], fo[:, :].unsqueeze(1),
                                      xs_y[:, bass.ds(GROUPS + HEADS + n, 1), 0:T].bitcast(F32), ALU.subtract).then_inc(s("mo_split"), 1)
                chain.leave(2)

            dve.wait_ge(*event("usq_summed"))
            dve.tensor_scalar(mu[:, :], ps_b, 1.0 / (GROUPS * P), EPS, ALU.mult, ALU.add).then_inc(event("uc_ms")[0], 1)
            dve.wait_ge(*event("uc_norm"))
            for k in range(GROUPS):
                link(dve.tensor_tensor(uc[:, k, :], uc[:, k, :], mu[:, :], ALU.mult))
                ins = dve.tensor_scalar(uc[:, k, :], uc[:, k, :], column("conv_ln_g", k), column("conv_ln_b", k),
                                        ALU.mult, ALU.add)
                if k < GROUPS - 1:
                    link(ins)
                else:
                    ins.then_inc(s("cl_ready"), 1)
            dve.wait_ge(s("cl_sig"), 1)
            dve.tensor_tensor(uc[:, :, :], uc[:, :, :], usq[:, :, :], ALU.mult).then_inc(s("cs_ready"), 1)
            for k in range(GROUPS):
                dve.wait_ge(s("xs_cv_hi"), k + 1)
                dve.tensor_tensor(xs_cv[:, k, T:2 * T], uc[:, k, :], xs_cv[:, k, 0:T].bitcast(F32),
                                  ALU.subtract).then_inc(s("xs_cv"), 1)
            for k in range(GROUPS):
                add(U_CG + k, k % 2)
                lo(G_CG, 0, 0, k + 2)
                scaled(U_CG + k, k % 2, sg_c[:, k, :], "cg_lin")
                logistic(ce[:, k % 2, :], "cg_exp", k + 1)
                link(dve.tensor_tensor(sg_c[:, k, :], sg_c[:, k, :], ce[:, k % 2, :], ALU.mult))
            for k in range(GROUPS):
                add(U_PW + k, k % 2)
                dve.wait_ge(out_free, U_PW + k + 3)
                dve.tensor_tensor(cx[:, k % 2, :], tmp[:, k % 2, :], sg_c[:, k, :], ALU.mult).then_inc(s("yc_ready"), 1)
                dve.wait_ge(s("xs_yc_hi"), k + 1)
                dve.tensor_tensor(xs_y[:, k, T:2 * T], cx[:, k % 2, :], xs_y[:, k, 0:T].bitcast(F32),
                                  ALU.subtract).then_inc(s("xs_yc"), 1)
            lo(G_PW, 0, 0, 2)

            def out2(i, j, ahead):
                u = U_OUT2 + 4 * i + j
                add(u, j % 2)
                if ahead:
                    lo(G_OUT2, i, 4, j + 2)
                dve.wait_ge(out_free, u + 3)
                k = 4 * i + j
                dve.tensor_tensor(h4[:, bass.ds(k, 1), :], tmp[:, j % 2:j % 2 + 1, :], h[:, bass.ds(k, 1), :],
                                  ALU.add).then_inc(s("h4_ready"), 1)

            with dve.Fori(0, 3) as i:
                for j in range(4):
                    out2(i, j, True)
            for j in range(4):
                out2(3, j, j < 2)
            dve.wait_ge(*event("h4_summed"))
            mean_square(ps_a, rstd[:, :], "h4_ms")
            dve.wait_ge(*event("h4_norm"))
            for k in range(KT):
                dve.scalar_tensor_tensor(out=o_out[:, k, :], in0=h4[:, k, :], scalar=column("final_g", k),
                                         in1=rstd[:, :], op0=ALU.mult, op1=ALU.mult).then_inc(s("o_ready"), 1)

        @block.gpsimd
        def _(pool):
            chain = Chain(pool, pool_step)
            link = chain.link


            pool.wait_ge(s("consts_in"), 7 * 16)
            pool.tensor_copy(lmask[:, :, :], lmask_in[:, :, :]).then_inc(s("lmask_ready"), 1)
            with pool.Fori(0, HEADS) as i:
                chain.enter(i, 23)
                pool.wait_ge(s("fk_ready"), i + 1)
                pool.wait_ge(s("q_ready"), i + 1)
                pool.wait_ge(s("lev_ready"), i * 5)
                for L in range(LEVELS):
                    m = 2 ** L

                    def halves(t):
                        v = t.rearrange("p (b two m) -> p b two m", two=2, m=m)
                        return v[:, :, 0, :], v[:, :, 1, :]

                    shape = [P, T // (2 * m), m]
                    (x0, x1), (p0, p1), (s0, s1) = halves(lev_in[:, L, :]), halves(pfx[:, :]), halves(sfx[:, :])
                    (k0, _), (_, q1) = halves(kk[:, :]), halves(qq[:, :])
                    link(pool.tensor_tensor(x1, q1, p1, ALU.mult))
                    if L == 0:
                        both = ones[:, :].unsqueeze(1).to_broadcast([P, 2, P])
                        link(pool.tensor_tensor(sfx[:, :].rearrange("p (a b) -> p a b", a=2), both, both, ALU.mult))
                    pool.tensor_tensor(x0, k0, s0, ALU.mult).then_inc(s("lev_in_ready"), 1)
                    if L < LEVELS - 1:
                        pool.wait_ge(s("lev_in_ready"), i * LEVELS + L + 1)
                        link(pool.tensor_tensor(s0, s0, p1[:, :, m - 1:m].to_broadcast(shape), ALU.mult))
                        link(pool.tensor_tensor(p1, p1, p0[:, :, m - 1:m].to_broadcast(shape), ALU.mult))
                chain.leave(HEADS)

            def sum_squares(src, sq):
                link(pool.tensor_tensor(sq, src, src, ALU.mult))
                link(pool.tensor_tensor(acc[:, :], acc[:, :], sq.squeeze(1) if len(sq.shape) == 3 else sq, ALU.add))

            pool.wait_ge(*event("mem_summed"))
            link(pool.memset(acc[:, :], 0.0))
            with pool.Fori(0, KT) as i:
                chain.enter(i, 2)
                pool.wait_ge(out_free, U_OUT + i + 3)
                sum_squares(mixed[:, bass.ds(i, 1), :], sq1[:, :].unsqueeze(1))
                chain.leave(KT)
            pool.tensor_copy(dummy[:, 1:2], acc[:, 0:1]).then_inc(event("mixed_acc")[0], 1)
            pool.wait_ge(*event("h1_norm"))
            with pool.Fori(0, FT // 2) as i:
                for q in range(4):
                    n = 4 * i + q
                    pool.wait_ge(out_free, U_UP + n + 3)
                    pool.wait_ge(s("gate_conv" if q % 2 == 0 else "val_conv"), 2 * i + q // 2)
                    pool.tensor_tensor(upb[:, q % 2, 2:T + 2], tmp[:, q % 2, :], rstd[:, :], ALU.mult).then_inc(s("up_ready"), 1)
            link(pool.memset(acc[:, :], 0.0))
            with pool.Fori(0, KT) as i:
                chain.enter(i, 2)
                pool.wait_ge(out_free, U_DOWN + i + 3)
                sum_squares(y[:, bass.ds(i, 1), :], sq2[:, :].unsqueeze(1))
                chain.leave(KT)
            pool.tensor_copy(dummy[:, 1:2], acc[:, 0:1]).then_inc(event("y_acc")[0], 1)
            pool.wait_ge(*event("y_summed"))
            link(pool.memset(acc[:, :], 0.0))
            with pool.Fori(0, KT) as i:
                chain.enter(i, 2)
                pool.wait_ge(s("h3_ready"), i + 1)
                sum_squares(h[:, bass.ds(i, 1), :], sq3[:, :].unsqueeze(1))
                chain.leave(KT)
            pool.tensor_copy(dummy[:, 1:2], acc[:, 0:1]).then_inc(event("h3_acc")[0], 1)

            pool.wait_ge(s("u_ready"), GROUPS)
            taps = vec[:, V["taps"]:V["taps"] + GROUPS * TAPS].rearrange("p (k t) -> p k t", k=GROUPS)
            every = [P, GROUPS, T]

            def tap_product(dst, tap):
                return pool.tensor_tensor(dst, upad[:, :, bass.ds(tap, T)],
                                          taps[:, :, bass.ds(tap, 1)].to_broadcast(every), ALU.mult)

            link(tap_product(uc[:, :, :], 0))
            pool.tensor_tensor(uc[:, :, :], uc[:, :, :], column("conv_b_2", 0, GROUPS).unsqueeze(2).to_broadcast(every),
                               ALU.add).then_inc(s("tap_done"), 1)
            with pool.Fori(0, (TAPS - 1) // 2) as i:
                for j, made in enumerate((usq, sg_c)):
                    pool.wait_ge(s("tap_done"), 2 * i + j)
                    tap_product(made[:, :, :], 2 * i + j + 1).then_inc(s("tap_product"), 1)
                    pool.wait_ge(s("tap_product"), 2 * i + j + 1)
                    pool.wait_ge(s("tap_done"), 2 * i + j + 1)
                    pool.tensor_tensor(uc[:, :, :], uc[:, :, :], made[:, :, :], ALU.add).then_inc(s("tap_done"), 1)
            pool.wait_ge(*event("h3_ms"))
            link(pool.memset(acc[:, :], 0.0))
            with pool.Fori(0, KT) as i:
                chain.enter(i, 2)
                pool.wait_ge(s("h4_ready"), i + 1)
                sum_squares(h4[:, bass.ds(i, 1), :], sq4[:, 0:1, :])
                chain.leave(KT)
            pool.tensor_copy(dummy[:, 1:2], acc[:, 0:1]).then_inc(event("h4_acc")[0], 1)

        @block.tensor
        def _(pe):
            def product(slot, c, act, bank, start, stop):
                pe.matmul(ps[:, bank, :], whi[:, slot, c * P:(c + 1) * P], act, start=start, stop=False)
                return pe.matmul(ps[:, bank, T:2 * T], wlo[:, slot, c * P:(c + 1) * P], act[:, 0:T],
                                 start=False, stop=stop)

            def whole(g, u, slot, bank, xs, order=range(KT)):
                pe.wait_ge(w_lo, g + 1)
                pe.wait_ge(out_free, u + 1)
                order = list(order)
                for c in order:
                    ins = product(slot, c, xs[:, c, :], bank, c == order[0], c == order[-1])
                ins.then_inc(w_used, 1)

            def column_sums(dst, srcs, waits, done):
                for n, src in enumerate(srcs):
                    pe.wait_ge(*waits(n))
                    ins = pe.matmul(dst, ones[:, :], src, start=n == 0, stop=n == len(srcs) - 1)
                ins.then_inc(event(done)[0], 1)

            def turn(dst, src, done, inc=1):
                ins = pe.transpose(dst, src, ident[:, :])
                if inc:
                    ins.then_inc(s(done), 1)

            def masked_scores(q, k, terms):
                for t, (c0, c1) in enumerate(((0, P), (P, 3 * P))):
                    rows, n = slice(t * P, t * P + P), c1 - c0
                    for m, (l, r) in enumerate(terms(rows, n)):
                        pe.matmul(ps_sc[:, c0:c1], l, r, start=m == 0, stop=False)
                    ins = pe.matmul(ps_sc[:, c0:c1], q[:, rows], k[:, 0:n], start=not terms(rows, n), stop=True)
                return ins

            def weighted(dst, v, pt):
                pe.matmul(dst, v[:, 0, :], pt[:, 0:T], start=True, stop=False)
                return pe.matmul(dst[:, P:T], v[:, 1, :], pt[:, T:3 * P], start=False, stop=True)

            pe.wait_ge(s("consts_in"), 7 * 16)
            column_sums(ps_a, [acc[:, :]], lambda n: event("x_sum"), "x_summed")
            column_sums(ps_b, [acc[:, :]], lambda n: event("mem_sum"), "mem_summed")
            pe.wait_ge(s("xs_x"), KT)
            pe.wait_ge(s("xs_mem"), KT)

            with pe.Fori(0, HEADS) as i:
                g = i * 8
                for j in range(4):
                    whole(g + j, g + j, j % 2, j % 2, act_a)
                pe.wait_ge(s("i_ready"), i + 1)
                pe.wait_ge(s("pT_ready"), i)
                turn(ps_t[:, 0:P], iT[:, 0:P], None, 0)
                turn(ps_t[:, P:T], iT[:, P:T], "i_turned")
                whole(g + 4, g + 4, 0, 0, act_a)
                pe.wait_ge(s("fk_ready"), i + 1)
                pe.wait_ge(s("q_ready"), i + 1)
                pe.wait_ge(s("lev_used"), i * LEVELS)
                pe.wait_ge(s("cross_ready"), i)
                pe.wait_ge(s("var_ready"), i)
                for n in range(LEVELS + 1):
                    if n >= 4 and n % 2 == 0:
                        pe.wait_ge(s("lev_used"), i * LEVELS + n - 2)
                    if n:
                        pe.wait_ge(s("lev_in_ready"), i * LEVELS + n)
                    keys, queries = (kk, qq) if n == 0 else (lev_in[:, n - 1, :],) * 2
                    if n < LEVELS:
                        for c in range(2):
                            tile = slice(c * P, c * P + P)
                            ins = pe.matmul(ps_lev[:, n // 2 % 2, n % 2, tile], keys[:, tile], queries[:, tile],
                                            start=True, stop=True)
                    else:
                        ins = pe.matmul(ps_lev[:, 0, 0, 0:P], keys[:, 0:P], queries[:, P:T], start=True, stop=True)
                    if n % 2 or n == LEVELS:
                        ins.then_inc(s("lev_ready"), 1)
                whole(g + 5, g + 5, 1, 1, act_a)
                pe.wait_ge(s("aq_ready"), i + 1)
                pe.wait_ge(s("ak_ready"), i + 1)
                pe.wait_ge(s("att_max"), i)
                masked_scores(aqT, akT, lambda rows, n: ()).then_inc(s("sc_ready"), 1)
                whole(g + 6, g + 6, 0, 0, act_a)
                pe.wait_ge(s("av_ready"), i + 1)
                pe.wait_ge(s("vtok_ready"), i + 1)
                turn(ps_t[:, 0:P], avT[:, 0:P], None, 0)
                turn(ps_t[:, P:T], avT[:, P:T], "av_turned")
                pe.wait_ge(s("lev_used"), (i + 1) * LEVELS)
                pe.wait_ge(s("cross_ready"), i + 1)
                pe.wait_ge(s("vtok_ready"), i + 1)
                weighted(ps_a, vtok, sT).then_inc(s("hg_out"), 1)
                whole(g + 7, g + 7, 1, 1, xs_mem)
                pe.wait_ge(s("osq_ready"), i + 1)
                pe.matmul(ps_lev[:, 1, 0, :], ones[:, :], osq[:, :], start=True, stop=True).then_inc(s("o_summed"), 1)
                pe.wait_ge(s("p_ready"), 2 * i + 2)
                pe.wait_ge(s("avtok_ready"), i + 1)
                for c in range(3):
                    turn(ps_t[:, c * P:(c + 1) * P], sm[:, c * P:(c + 1) * P], "p_turned", c == 2)
                pe.wait_ge(s("pT_ready"), i + 1)
                pe.wait_ge(s("avtok_ready"), i + 1)
                pe.wait_ge(s("att_split"), i)
                weighted(ps_b, avtok, pT).then_inc(s("att_out"), 1)

            with pe.Fori(0, 4) as i:
                for j in range(4):
                    if j == 0:
                        pe.wait_ge(s("mix_done"), HEADS)
                        pe.wait_ge(s("att_split"), HEADS)
                    whole(G_OUT + 4 * i + j, U_OUT + 4 * i + j, j % 2, j % 2, xs_mix)
            column_sums(ps_a, [acc[:, :]], lambda n: event("mixed_acc"), "mixed_summed")
            column_sums(ps_b, [mixed[:, k, :] for k in range(KT)], lambda n: (s("h1_sq"), n + 1), "h1_summed")

            with pe.Fori(0, FT // 2) as i:
                for j in range(4):
                    if j == 0:
                        pe.wait_ge(s("xs_u"), KT)
                    whole(G_UP + 4 * i + j, U_UP + 4 * i + j, j % 2, j % 2, act_a)
            with pe.Fori(0, KT // 2) as i:
                for j in range(8):
                    part, bank = j % 4, j // 4
                    pe.wait_ge(w_lo, G_DOWN + 8 * i + j + 1)
                    if part == 0:
                        pe.wait_ge(out_free, U_DOWN + 2 * i + bank + 1)
                    if j < 4:
                        pe.wait_ge(s("xs_g"), DOWN_CELLS * (part + 1))
                    for c in range(DOWN_CELLS):
                        k = DOWN_CELLS * part + c
                        ins = product(j % 2, c, big[:, k, :], bank, k == 0, k == FT - 1)
                    ins.then_inc(w_used, 1)

            def parts(g, u0, slot, n_out, per, xs):
                pe.wait_ge(w_lo, g + 1)
                for o in range(n_out):
                    pe.wait_ge(out_free, u0 + o + 1)
                    for c in range(per):
                        ins = product(slot, o * per + c, xs[:, c, :], o % 2, c == 0, c == per - 1)
                    ins.then_inc(part_made if o < n_out - 1 else w_used, 1)

            pe.wait_ge(s("xs_p"), 2)
            parts(G_PE, U_PE, 0, 8, 2, xs_p)
            column_sums(ps_a, [acc[:, :]], lambda n: event("y_acc"), "y_summed")
            parts(G_PE + 1, U_PE + 8, 1, 8, 2, xs_p)
            with pe.Fori(0, 4) as i:
                for j in range(4):
                    if j == 0:
                        pe.wait_ge(s("xs_h"), KT)
                    whole(G_PG + 4 * i + j, U_PG + 4 * i + j, j % 2, j % 2, xs_h)
            column_sums(ps_b, [acc[:, :]], lambda n: event("h3_acc"), "h3_summed")

            with pe.Fori(0, 2) as i:
                for j in range(4):
                    if j == 0:
                        pe.wait_ge(s("xs_n"), KT)
                    whole(G_CONV + 4 * i + j, U_CONV + 4 * i + j, j % 2, j % 2, act_a)
            pe.wait_ge(s("wfg_ready"), 1)
            for k in range(KT):
                ins = pe.matmul(ps_t[0:HEADS, 0:T], wfg[:, k, :], h[:, k, :], start=k == 0, stop=k == KT - 1)
            ins.then_inc(s("fl_ready"), 1)
            with pe.Fori(0, HEADS) as i:
                g, u = G_FOX + 4 * i, U_FOX + 4 * i
                for j in range(3):
                    whole(g + j, u + j, j % 2, j % 2, act_a)
                pe.wait_ge(s("c_ready"), 2 * i + 2)
                pe.wait_ge(s("fq_ready"), i + 1)
                pe.wait_ge(s("fk2_ready"), i + 1)
                pe.wait_ge(s("fox_max"), i)
                masked_scores(fqT, fkT, lambda rows, n: ((cpos[:, rows], one8[:, 0:n]), (one8[:, 0:P], cneg[:, 0:n])))\
                    .then_inc(s("fsc_ready"), 1)
                whole(g + 3, u + 3, 1, 1, act_a)
                pe.wait_ge(s("fv_ready"), i + 1)
                pe.wait_ge(s("fvtok_ready"), i)
                turn(ps_b[:, 0:P], fvT[:, 0:P], None, 0)
                turn(ps_b[:, P:T], fvT[:, P:T], "fv_turned")
                pe.wait_ge(s("fp_ready"), 2 * i + 2)
                pe.wait_ge(s("fpT_ready"), i)
                for c in range(3):
                    turn(ps_t[:, c * P:(c + 1) * P], fs[:, c * P:(c + 1) * P], "fp_turned", c == 2)
                pe.wait_ge(s("fvtok_ready"), i + 1)
                pe.wait_ge(s("fpT_ready"), i + 1)
                pe.wait_ge(s("fo_done"), i)
                weighted(ps_a, fvtok, fpT).then_inc(s("fo_ready"), 1)
            column_sums(ps_b, [uc[:, k, :] for k in range(GROUPS)],
                        lambda n: (s("tap_done"), TAPS), "uc_summed")
            with pe.Fori(0, 2) as i:
                for q in range(2):
                    g, u, n = G_MEM + 4 * i + 2 * q, U_MEM + 4 * i + 2 * q, 2 * i + q
                    whole(g, u, 0, 0, act_a)
                    pe.wait_ge(s("mv_here"), n + 1)
                    pe.wait_ge(s("mvtok_ready"), n)
                    pe.wait_ge(s("usq_ready"), 1)
                    turn(ps_b[:, 0:P], mv_h[:, 0:P], None, 0)
                    turn(ps_b[:, P:T], mv_h[:, P:T], "mv_turned")
                    pe.wait_ge(s("mq_ready"), n + 1)
                    pe.wait_ge(s("mem_exp"), 2 * n)
                    for t in range(2):
                        ins = pe.matmul(ps_sc[:, t * T:t * T + T], fqT[:, t * P:t * P + P],
                                        mkv[:, bass.ds(n, 1), :].squeeze(1), start=True, stop=True)
                    ins.then_inc(s("msc_ready"), 1)
                    whole(g + 1, u + 1, 1, 1, act_a)
                    pe.wait_ge(s("mp_ready"), 2 * n + 2)
                    pe.wait_ge(s("mpT_ready"), n)
                    for t in range(2):
                        for m in range(2):
                            turn(ps_t[:, m * T + t * P:m * T + t * P + P], fs[:, t * T + m * P:t * T + m * P + P],
                                 "mp_turned", t and m)
                    pe.wait_ge(s("mvtok_ready"), n + 1)
                    pe.wait_ge(s("mpT_ready"), n + 1)
                    pe.wait_ge(s("mo_done"), n)
                    pe.matmul(ps_a, fvtok[:, 0, :], fpT[:, 0:T], start=True, stop=False)
                    pe.matmul(ps_a, fvtok[:, 1, :], fpT[:, T:2 * T], start=False, stop=True).then_inc(s("mo_ready"), 1)
            column_sums(ps_b, [usq[:, k, :] for k in range(GROUPS)], lambda n: (s("usq_ready"), 1), "usq_summed")
            for k in range(GROUPS):
                whole(G_CG + k, U_CG + k, k % 2, k % 2, act_a)
            pe.wait_ge(s("xs_cv"), GROUPS)
            parts(G_PW, U_PW, 0, GROUPS, GROUPS, xs_cv)

            pe.wait_ge(s("fo_split"), HEADS)
            pe.wait_ge(s("mo_split"), MEM_HEADS)
            pe.wait_ge(s("xs_yc"), GROUPS)
            with pe.Fori(0, 4) as i:
                for j in range(4):
                    whole(G_OUT2 + 4 * i + j, U_OUT2 + 4 * i + j, (G_OUT2 + j) % 2, j % 2, xs_y)
            column_sums(ps_a, [acc[:, :]], lambda n: event("h4_acc"), "h4_summed")


def kernel(**inputs):
    import concourse.bacc as bacc
    from concourse.bass_utils import run_bass_kernel_spmd

    f32, b16 = np.float32, mybir.dt.np(BF16)
    get = {n: np.asarray(x) for n, x in inputs.items()}

    def features(x):
        return np.ascontiguousarray(x.T.reshape(-1, P, x.shape[0]).transpose(1, 0, 2))

    def vector(x):
        return x.reshape(-1, P).T

    def blocks(w):
        k, n = w.shape
        return w.reshape(k // P, P, n // P, P).transpose(2, 1, 0, 3).reshape(n // P, P, k)

    w_in, w_in2 = get["w_in"][0], get["w_in_2"][0]
    hq, hf, hi, hg, aq, ak, av = (blocks(w) for w in np.split(w_in, 7, axis=1))
    mkv = blocks(get["w_mem_kv_2"][0])
    mix = np.stack([hf, hq, hi, aq, ak, av, hg, mkv], axis=1).reshape(G_OUT, P, BW)
    up = blocks(get["w_up"][0])
    up = np.stack([up[:FT], up[FT:]], axis=1).reshape(2 * FT, P, BW)
    w_a = np.concatenate([mix, blocks(get["w_out"][0]), up])
    w_down = get["w_down"][0].reshape(4, DOWN_CELLS, P, KT, P).transpose(3, 0, 2, 1, 4).reshape(4 * KT, P, DOWN_CELLS * P)
    w_pe = blocks(get["w_pe"][0]).reshape(2, 8, P, 2, P).transpose(0, 2, 1, 3, 4).reshape(2, P, BW)
    c = GROUPS * P
    fw = HEADS * P
    at = np.cumsum([0, c, c, c, fw, fw, fw, HEADS, fw, c, c])
    cv_a, cv_b, cv_g, fq, fk, fv, fl, fg, mq, mg = (w_in2[:, a:b] for a, b in zip(at[:-1], at[1:]))
    conv = np.stack([blocks(cv_a), blocks(cv_b)], axis=1).reshape(2 * GROUPS, P, BW)
    fox = np.stack([blocks(fq), blocks(fk), blocks(fv), blocks(fg)], axis=1).reshape(4 * HEADS, P, BW)
    mem = np.stack([blocks(mq), blocks(mg)], axis=1).reshape(2 * MEM_HEADS, P, BW)
    pw = blocks(get["w_conv_pw_2"][0]).transpose(1, 0, 2).reshape(1, P, BW)
    w_b = np.concatenate([w_pe, blocks(get["w_pg"][0]), conv, fox, mem, blocks(cv_g), pw, blocks(get["w_out_2"][0])])
    wfg = np.ascontiguousarray(fl.reshape(KT, P, HEADS).transpose(1, 0, 2))

    cw = np.stack([vector(x) for x in (*get["conv_w"][0], get["conv_b"][0])], axis=2)
    cw = np.stack([cw[:, :FT], cw[:, FT:]], axis=2).reshape(P, 8 * FT)
    taps = np.stack([vector(x) for x in get["conv_w_2"][0]], axis=2).reshape(P, GROUPS * TAPS)
    vec = np.concatenate([
        vector(get["ln_mix_pre"]), vector(get["lb_logits"]), vector(get["hgrn_norm"]), vector(get["ln_mix_post"]),
        vector(get["ln_ffn_pre"]), cw, vector(get["ln_ffn_post"]), vector(get["norm_g_2"]), vector(get["mem_norm_g_2"]),
        taps, vector(get["conv_b_2"]), vector(get["conv_ln_g_2"]), vector(get["conv_ln_b_2"]), vector(get["final_g_2"])],
        axis=1)

    t, k = np.arange(T)[:, None], np.arange(T)[None, :]

    def tiles(m):
        return np.ascontiguousarray(np.concatenate([m[:P, :P], m[P:, :]], axis=1))

    dist = t - k
    count = sum(((dist >= 0) & (dist <= w) & (dist % d == 0)).astype(f32) for w, d in ((128, 1), (512, 4), (2048, 16)))
    one = np.arange(P)
    lmask = [one[:, None] == one[None, :]]
    for level in range(LEVELS - 1):
        b = one // 2 ** level
        lmask.append((b[:, None] % 2 == 0) & (b[None, :] == b[:, None] + 1))
    lmask = np.stack([np.concatenate([m, m], axis=1) for m in lmask], axis=1).astype(b16)

    arrays = {
        "xT": features(get["x"][0]), "memT": features(get["mem_2"][0]), "pT": features(get["p"][0, 0]),
        "w_a": w_a, "w_down": w_down, "w_b": w_b, "wfg": wfg, "bfox": get["b_f_2"].reshape(HEADS, 1), "vec": vec,
        "ident": np.eye(P, dtype=f32), "ones": np.ones((P, P), f32), "mult": tiles(count).astype(b16),
        "bias_att": tiles(np.where(count > 0, 0.0, MASKED)).astype(b16),
        "bias_fox": tiles(np.where(dist >= 0, 0.0, MASKED)).astype(b16), "lmask": lmask,
    }
    nc = bacc.Bacc("TRN2", target_bir_lowering=False, num_devices=1, dynamic_dma_scratch_size=1024)
    drams, sent = {}, {}
    for name, x in arrays.items():
        sent[f"in_{name}"] = np.ascontiguousarray(x)
        drams[name] = nc.dram_tensor(f"in_{name}", x.shape, mybir.dt.from_np(x.dtype), kind="ExternalInput").ap()
    out = nc.dram_tensor("out", (P, KT, T), F32, kind="ExternalOutput").ap()
    build(nc, drams, out)
    r = run_bass_kernel_spmd(nc, [sent], core_ids=[0])
    got = r.results[0]["out"]
    return np.ascontiguousarray(got.transpose(1, 0, 2).reshape(D, T).T).reshape(1, T, D)
```

```python
from contextlib import ExitStack

import numpy as np

import concourse.bass as bass
from concourse import mybir

F32 = mybir.dt.float32
F32R = mybir.dt.float32r
BF16 = mybir.dt.bfloat16
U8 = mybir.dt.uint8
ALU = mybir.AluOpType
ACT = mybir.ActivationFunctionType
AX_X = mybir.AxisListType.X

P = 128
T = 256
D = 2048
KT = D // P
HEADS = 8
MEM_HEADS = 4
GROUPS = 4
TAPS = 31
FF = 5632
FT = FF // P
DOWN_CELLS = 11
BW = KT * P
NS = 4
EPS = 1e-6
SCALE = float(P) ** -0.5
LEVELS = 8
QUARTERS = 4
MASKED = -1e30
LARGE = 1e38

G_MIX, U_MIX = 0, 0
G_OUT, U_OUT = 64, 64
G_UP, U_UP = 80, 80
G_DOWN, U_DOWN = 168, 168
G_PE, U_PE = 232, 184
G_PG, U_PG = 234, 200
G_CONV, U_CONV = 250, 216
G_FOX, U_FOX = 258, 224
G_MEM, U_MEM = 290, 256
G_CG, U_CG = 298, 264
G_PW, U_PW = 302, 268
G_OUT2, U_OUT2 = 303, 272
N_BLOCKS = 319

V = {}


def _vector_columns():
    at = 0
    for name, n in (("ln_mix_pre", KT), ("lb", HEADS), ("hgrn_norm", HEADS), ("ln_mix_post", KT), ("ln_ffn_pre", KT),
                    ("conv", 4 * 2 * FT), ("ln_ffn_post", KT), ("norm_g_2", KT), ("mem_norm_g_2", KT),
                    ("taps", GROUPS * TAPS), ("conv_b_2", GROUPS), ("conv_ln_g", GROUPS), ("conv_ln_b", GROUPS),
                    ("final_g", KT)):
        V[name] = at
        at += n
    return at


N_VEC = _vector_columns()


class Chain:

    def __init__(self, eng, sem):
        self.eng, self.sem, self.base, self.j = eng, sem, 0, 0

    def link(self, ins):
        self.j += 1
        ins.then_inc(self.sem, 1)
        self.eng.wait_ge(self.sem, self.base + self.j)

    def enter(self, i, per):
        self.start, self.per = self.base + self.j, per
        self.base, self.j = self.start + i * per, 0

    def leave(self, n):
        assert self.j == self.per, f"{self.sem}: {self.j} steps in the loop's body, {self.per} stated"
        self.base, self.j = self.start + n * self.per, 0



def build(nc, a, out):
    with ExitStack() as ctx:
        def sem(name):
            return ctx.enter_context(nc.semaphore(name))

        at = [(nc.sbuf_base + 31) // 32 * 32]

        def sb(name, shape, dt=F32):
            size = int(np.prod(shape[1:])) * mybir.dt.size(dt)
            t = nc.alloc_sbuf_tensor_at(name, shape, dt, offset=at[0])
            at[0] += (size + 31) // 32 * 32
            return t

        def over(name, region_at, offset, shape, dt=F32):
            return nc.alloc_sbuf_tensor_at(name, shape, dt, offset=region_at + offset)

        stage_at = at[0]
        stage = sb("stage", [P, NS, BW])
        wlo = over("wlo", stage_at, 0, [P, NS, BW], F32R)
        whi = sb("whi", [P, NS, BW], F32R)
        h_at = at[0]
        h = sb("h", [P, KT, T])
        vec = sb("vec", [P, N_VEC])
        ident = sb("ident", [P, P])
        ones = sb("ones", [P, P])
        bfox = sb("bfox", [HEADS, 1])
        mkv = sb("mkv", [P, HEADS, T])
        small = sb("small", [P, 2, T])
        tmp = sb("tmp", [P, 2, T])
        rstd = sb("rstd", [P, T])
        acc = sb("acc", [P, T])
        cols = sb("cols", [P, 32])
        dummy = sb("dummy", [P, 2])
        conv_at = at[0]
        lmask = sb("lmask", [P, LEVELS, 2 * P], U8)
        mult = sb("mult", [P, 3 * P], BF16)
        bias_att = sb("bias_att", [P, 3 * P], BF16)
        upb = over("upb", conv_at, 0, [P, 2, T + 2])
        cy = over("cy", conv_at, 2080, [P, 2, T])
        gl = over("gl", conv_at, 4128, [P, T])
        at[0] = conv_at + 4128 + 1024
        a_at = at[0]
        act_a = sb("act_a", [P, KT, 2 * T], F32R)
        big_at = at[0]
        big = sb("big", [P, FT, 2 * T], F32R)
        KB = 1024

        mem_raw = over("mem_raw", big_at, 0, [P, KT, T])
        squares = over("squares", big_at, 64 * KB, [P, KT, T])
        xs_mix = big[:, 0:KT, :]
        xs_mem = big[:, KT:2 * KT, :]
        lmask_in = over("lmask_in", big_at, 80 * KB, [P, LEVELS, 2 * P], BF16)
        w1 = [64 * KB]

        def work1(name, shape):
            t = over(name, big_at, w1[0], shape)
            w1[0] += int(np.prod(shape[1:])) * 4
            assert w1[0] <= 86 * KB
            return t

        w0 = [0]

        def work0(name, shape):
            t = over(name, h_at, w0[0], shape)
            w0[0] += int(np.prod(shape[1:])) * 4
            assert w0[0] <= 16 * KB
            return t

        pfx = work1("pfx", [P, T])
        sfx = work1("sfx", [P, T])
        kk = work1("kk", [P, T])
        qq = work1("qq", [P, T])
        lev_in = work1("lev_in", [P, LEVELS, T])
        sT = work1("sT", [P, 3 * P])
        iT = work1("iT", [P, T])
        vtok = work1("vtok", [P, 2, P])
        aqT = work1("aqT", [P, T])
        akT = work1("akT", [P, T])
        avT = work1("avT", [P, T])
        avtok = work1("avtok", [P, 2, P])
        hfx = work0("hfx", [P, T])
        hqx = work0("hqx", [P, T])
        hgx = work0("hgx", [P, T])
        ef = work0("ef", [P, T])
        eq = work0("eq", [P, T])
        eg = work0("eg", [P, T])
        on1 = work0("on1", [P, T])
        osq = work0("osq", [P, T])
        osb = work0("osb", [P, T])
        var = work0("var", [P, T])
        sm = work0("sm", [P, 3 * P])
        pT = work0("pT", [P, 3 * P])
        mixed = over("mixed", big_at, 64 * KB, [P, KT, T])
        sq1 = over("sq1", big_at, 80 * KB, [P, T])
        rstd_mem = over("rstd_mem", big_at, 86 * KB, [P, T])
        mem_again = over("mem_again", a_at, 0, [P, KT, T])
        y = over("y", a_at, 0, [P, KT, T])
        p_raw = over("p_raw", a_at, 20 * KB, [P, 2, T])
        sq2 = over("sq2", a_at, 22 * KB, [P, T])
        xs_p = act_a[:, 8:10, :]
        xs_h = big[:, 0:KT, :]
        pe_out = over("pe_out", big_at, 32 * KB, [P, KT, T])
        pg_x = over("pg_x", big_at, 48 * KB, [P, 2, T])
        pg_s = over("pg_s", big_at, 50 * KB, [P, 2, T])
        sq3 = over("sq3", big_at, 52 * KB, [P, T])
        xs_y = big[:, 0:KT, :]
        xs_cv = big[:, 40:44, :]
        w2 = [32 * KB]

        def work2(name, shape):
            t = over(name, big_at, w2[0], shape)
            w2[0] += int(np.prod(shape[1:])) * 4
            assert w2[0] <= 80 * KB
            return t

        upad = work2("upad", [P, GROUPS, TAPS - 1 + T])
        uc = work2("uc", [P, GROUPS, T])
        usq = work2("usq", [P, GROUPS, T])
        cx = work2("cx", [P, 2, T])
        ce = work2("ce", [P, 2, T])
        mu = work2("mu", [P, T])
        bias_fox = work2("bias_fox", [P, 3 * P // 2])[:, :].bitcast(BF16)
        wfg = work2("wfg", [P, KT, HEADS])
        sg_c = work2("sg_c", [P, GROUPS, T])
        fqT = work2("fqT", [P, T])
        fkT = work2("fkT", [P, T])
        fvT = work2("fvT", [P, T])
        fgx = work2("fgx", [P, T])
        fge = work2("fge", [P, T])
        fvtok = work2("fvtok", [P, 2, P])
        fs = work2("fs", [P, 4 * P])
        fpT = work2("fpT", [P, 4 * P])
        fo = work2("fo", [P, T])
        mv_h = work2("mv_h", [P, T])
        zf = work2("zf", [HEADS, T])
        z1 = work2("z1", [HEADS, T])
        z2 = work2("z2", [HEADS, T])
        one8 = work2("one8", [HEADS, T])
        cc = work2("cc", [HEADS, T])
        cpos = work2("cpos", [HEADS, T])
        cneg = work2("cneg", [HEADS, T])
        sq4 = work2("sq4", [P, 2, T])
        h4 = over("h4", a_at, 0, [P, KT, T])
        o_out = over("o_out", a_at, 16 * KB, [P, KT, T])
        assert at[0] <= nc.sbuf_top, at[0] - nc.sbuf_top

        ps = ctx.enter_context(nc.psum_tensor("ps", [P, 2, 2 * T], F32))
        ps_lev = ctx.enter_context(nc.psum_tensor("ps_lev", [P, 2, 2, T], F32))
        ps_sc = ctx.enter_context(nc.psum_tensor("ps_sc", [P, 2 * T], F32))
        ps_t = ctx.enter_context(nc.psum_tensor("ps_t", [P, 2 * T], F32))
        bank_a = ctx.enter_context(nc.psum_tensor("bank_a", [P, 2 * T], F32))
        ps_a, ps_cross = bank_a[:, 0:T], bank_a[:, T:T + P]
        ps_b = ctx.enter_context(nc.psum_tensor("ps_b", [P, 2 * T], F32))[:, 0:T]

        S = {}

        def s(name):
            if name not in S:
                S[name] = sem(name)
            return S[name]

        once = {name: (kind, n + 1) for kind, names in (
            ("summed", ("x_summed", "mixed_summed", "mem_summed", "h1_summed", "y_summed", "h3_summed", "uc_summed",
                        "usq_summed", "h4_summed")),
            ("mean_square", ("x_ms", "mixed_ms", "mem_ms", "h1_ms", "y_ms", "h3_ms", "uc_ms", "h4_ms")),
            ("normed", ("x_norm", "mixed_norm", "mem_norm", "h1_norm", "y_norm", "h3_norm", "uc_norm", "h4_norm")),
            ("squares_added", ("x_sum", "mem_sum", "h1_sum")),
        ) for n, name in enumerate(names)}

        def event(name):
            kind, n = once[name]
            return s(kind), n

        steps = {name: (kind, n * count) for kind, count, names in (
            ("square_added", KT, ("mixed_acc", "y_acc", "h3_acc", "h4_acc")),
            ("gain_put", KT, ("mixed_gain", "y_gain", "h4_gain")),
            ("norm_put", QUARTERS, ("mixed_scaled", "y_scaled")),
            ("residual_put", QUARTERS - 1, ("h1_ready", "h2_ready")),
            ("tile_high", KT, ("xs_x_hi", "xs_mem_hi", "xs_u_hi")),
        ) for n, name in enumerate(names)}

        def step(name, n):
            kind, before = steps[name]
            return s(kind), n + before

        w_landed = [sem(f"w_landed{i}") for i in range(NS)]
        w_hi, w_lo, w_used = sem("w_hi"), sem("w_lo"), sem("w_used")
        part_made, small_ready, out_free = sem("part_made"), sem("small_ready"), sem("out_free")
        vector_step, scalar_step, pool_step = sem("vector_step"), sem("scalar_step"), sem("pool_step")

        def wait(eng, name, n):
            if not (isinstance(n, int) and n == 0):
                eng.wait_ge(s(name), n)

        block = ctx.enter_context(nc.Block())

        def quarter(c):
            return slice(c * KT // QUARTERS, (c + 1) * KT // QUARTERS)

        def column(name, i, n=1):
            return vec[:, bass.ds(V[name] + i, n)]

        @block.sync
        def _(sp):
            def load(g, source, slot, first=False):
                if not first:
                    sp.wait_ge(w_used, g - (NS - 1))
                width = source.shape[-1]
                sp.dma_start(stage[:, slot, 0:width], source).then_inc(w_landed[slot], 16)

            def load_run(start, count, source):
                n = count // NS
                with sp.Fori(0, n) as i:
                    for j in range(NS):
                        load(start + i * NS + j, source[i * NS + j], (start + j) % NS)
                for j in range(n * NS, count):
                    load(start + j, source[j], (start + j) % NS)

            def constant(dst, name, done="consts_in"):
                full = tuple(slice(None) for _ in dst.shape)
                sp.dma_start(dst[full], a[name]).then_inc(s(done), 16)

            load(0, a["w_a"][0], 0, first=True)
            constant(vec, "vec", "vec_in")
            for c in range(QUARTERS):
                sp.dma_start(h[:, quarter(c), :], a["xT"][:, quarter(c), :]).then_inc(s(f"x_in{c}"), 16)
            for j in range(1, NS):
                load(j, a["w_a"][j], j, first=True)
                if j == 2:
                    for dst, name in ((ident, "ident"), (ones, "ones"), (mult, "mult"), (bias_att, "bias_att"),
                                      (lmask_in, "lmask"), (bfox, "bfox")):
                        constant(dst, name)
            constant(mem_raw, "memT", "mem_in")
            load_run(NS, G_OUT - NS, a["w_a"][NS:G_OUT])
            load_run(G_OUT, NS, a["w_a"][G_OUT:G_OUT + NS])
            sp.wait_ge(s("mix_done"), HEADS)
            for c in range(2 * QUARTERS):
                load(G_OUT + NS + c, a["w_a"][G_OUT + NS + c], (G_OUT + c) % NS)
                dst, src, done = (mem_again, "memT", "mem_back") if c < QUARTERS else (h, "xT", "x_back")
                q = quarter(c % QUARTERS)
                sp.dma_start(dst[:, q, :], a[src][:, q, :]).then_inc(s(done), 16)
            load_run(G_OUT + 3 * NS, G_DOWN - G_OUT - 3 * NS, a["w_a"][G_OUT + 3 * NS:G_DOWN])
            load_run(G_DOWN, 4, a["w_down"][0:4])
            sp.wait_ge(w_used, G_DOWN)
            sp.dma_start(p_raw[:, :, :], a["pT"]).then_inc(s("p_in"), 16)
            load_run(G_DOWN + 4, G_PE - G_DOWN - 4, a["w_down"][4:])
            load_run(G_PE, G_CONV + 4 - G_PE, a["w_b"])
            sp.wait_ge(s("h3_ready"), KT)
            sp.dma_start(bias_fox, a["bias_fox"]).then_inc(s("fox_in"), 16)
            sp.dma_start(wfg[:, :, :], a["wfg"]).then_inc(s("fox_in"), 16)
            load_run(G_CONV + 4, N_BLOCKS - G_CONV - 4, a["w_b"][G_CONV + 4 - G_PE:])
            for c in range(QUARTERS):
                sp.wait_ge(s("o_ready"), c + 1)
                sp.dma_start(out[:, quarter(c), :], o_out[:, quarter(c), :]).then_inc(s("out_done"), 16)
            sp.wait_ge(s("out_done"), QUARTERS * 16)

        @block.scalar
        def _(act):
            chain = Chain(act, scalar_step)
            link = chain.link

            def hi(start, i, per, j, cells=KT):
                act.wait_ge(w_landed[(start + j) % NS], i * (16 * per // NS) + 16 * ((start + j) // NS + 1))
                slot = (start + j) % NS
                act.activation(whi[:, slot, 0:cells * P], stage[:, slot, 0:cells * P], ACT.Copy).then_inc(w_hi, 1)

            def evac(u, b, ahead=0, made=None):
                act.wait_ge(w_used if made is None else part_made, u + ahead + 1 if made is None else made)
                act.wait_ge(out_free, u + 1)
                act.activation(small[:, b, :], ps[:, b, T:2 * T], ACT.Copy).then_inc(small_ready, 1)

            def inverse_root(t, waits, done):
                act.wait_ge(*waits)
                link(act.activation(t, t, ACT.Ln))
                act.activation(t, t, ACT.Exp, scale=-0.5).then_inc(done, 1)

            def norm(t, name):
                inverse_root(t, event(name + "_ms"), event(name + "_norm")[0])

            def split_hi(dst, src, done, scale=1.0):
                act.activation(dst, src, ACT.Copy, scale=scale).then_inc(step(done, 0)[0] if done in steps else s(done), 1)

            hi(G_MIX, 0, 8, 0)
            act.wait_ge(s("vec_in"), 16)
            for k in range(KT):
                if k % (KT // QUARTERS) == 0:
                    act.wait_ge(s(f"x_in{k * QUARTERS // KT}"), 16)
                split_hi(act_a[:, k, 0:T], h[:, k, :], "xs_x_hi", column("ln_mix_pre", k))
            hi(G_MIX, 0, 8, 1)
            hi(G_MIX, 0, 8, 2)
            evac(0, 0)
            hi(G_MIX, 0, 8, 3)
            evac(1, 1)
            hi(G_MIX, 0, 8, 4)
            norm(rstd[:, :], "x")

            def mem_hi(half):
                for k in range(half * KT // 2, (half + 1) * KT // 2):
                    split_hi(xs_mem[:, k, 0:T], mem_raw[:, k, :], "xs_mem_hi", column("mem_norm_g_2", k))

            def attention_turned(n):
                wait(act, "p_turned", n + 1)
                act.activation(pT[:, :], ps_t[:, 0:3 * P], ACT.Copy).then_inc(s("pT_ready"), 1)

            def attention_out(n):
                wait(act, "att_out", n + 1)
                act.activation(xs_mix[:, bass.ds(HEADS + n, 1), 0:T], ps_b.unsqueeze(1), ACT.Copy).then_inc(s("att_hi"), 1)

            def recurrence_out(n):
                wait(act, "o_done", n + 1)
                act.activation(xs_mix[:, bass.ds(n, 1), 0:T], osb[:, :].unsqueeze(1), ACT.Copy).then_inc(s("o_hi"), 1)

            def mixers_head(i, before=None):
                u = i * 8
                if before is not None:
                    evac(u, 0)
                    hi(G_MIX, i, 8, 3)
                wait(act, "hf_lin", i + 1)
                act.activation(ef[:, :], hfx[:, :], ACT.Exp, scale=-1.0).then_inc(s("hf_exp"), 1)
                if before is not None:
                    attention_turned(before)
                    evac(u + 1, 1)
                    hi(G_MIX, i, 8, 4)
                wait(act, "hq_lin", i + 1)
                act.activation(eq[:, :], hqx[:, :], ACT.Exp, scale=-1.0).then_inc(s("hq_exp"), 1)
                if before is None:
                    act.wait_ge(s("mem_in"), 16)
                    mem_hi(0)
                else:
                    attention_out(before)
                evac(u + 2, 0)
                hi(G_MIX, i, 8, 5)
                if before is not None:
                    inverse_root(var[:, :], (s("var_ready"), before + 1), s("o_norm"))
                evac(u + 3, 1)
                hi(G_MIX, i, 8, 6)
                if before is not None:
                    recurrence_out(before)
                evac(u + 4, 0)
                hi(G_MIX, i, 8, 7)
                wait(act, "i_turned", i + 1)
                act.activation(vtok[:, :, :], ps_t[:, 0:T].rearrange("p (a b) -> p a b", a=2), ACT.Copy).then_inc(s("vtok_ready"), 1)
                if before is None:
                    mem_hi(1)
                evac(u + 5, 1)
                hi(G_MIX, i, 8, 8)
                wait(act, "lev_ready", i * 5 + 5)
                act.activation(sT[:, P:2 * P], ps_cross, ACT.Copy).then_inc(s("cross_ready"), 1)
                wait(act, "att_max", i + 1)
                act.activation(sm[:, 0:P], sm[:, 0:P], ACT.Exp, bias=cols[:, 2:3]).then_inc(s("att_exp"), 1)
                act.activation(sm[:, P:3 * P], sm[:, P:3 * P], ACT.Exp, bias=cols[:, 3:4]).then_inc(s("att_exp"), 1)
                evac(u + 6, 0)
                hi(G_MIX, i, 8, 9)
                wait(act, "av_turned", i + 1)
                act.activation(avtok[:, :, :], ps_t[:, 0:T].rearrange("p (a b) -> p a b", a=2), ACT.Copy).then_inc(s("avtok_ready"), 1)
                wait(act, "hg_lin", i + 1)
                act.activation(eg[:, :], hgx[:, :], ACT.Exp, scale=-1.0).then_inc(s("hg_exp"), 1)
                evac(u + 7, 1)
                hi(G_MIX, i, 8, 10)
                wait(act, "hg_out", i + 1)
                act.activation(osq[:, :], ps_a, ACT.Square).then_inc(s("osq_ready"), 1)

            mixers_head(0)
            with act.Fori(0, HEADS - 1) as n:
                chain.enter(n, 1)
                mixers_head(n + 1, n)
                chain.leave(HEADS - 1)
            attention_turned(HEADS - 1)
            inverse_root(var[:, :], (s("var_ready"), HEADS), s("o_norm"))
            attention_out(HEADS - 1)
            recurrence_out(HEADS - 1)

            for j in range(4):
                evac(U_OUT + j, j % 2)
                hi(G_OUT, 0, 0, j + 3)
            with act.Fori(0, 3) as i:
                for j in range(4):
                    evac(U_OUT + 4 + 4 * i + j, j % 2)
                    hi(G_OUT + 4, i, 4, j + 3)
            norm(rstd[:, :], "mixed")
            for c in range(QUARTERS + 1):
                if c < QUARTERS:
                    act.wait_ge(*step("h1_ready", c + 1) if c < QUARTERS - 1 else (s("h1_last"), 1))
                    for k in range(KT)[quarter(c)]:
                        split_hi(act_a[:, k, 0:T], h[:, k, :], "xs_u_hi", column("ln_ffn_pre", k))
                if c:
                    act.activation(mixed[:, quarter(c - 1), :], h[:, quarter(c - 1), :], ACT.Square).then_inc(s("h1_sq"), 1)

            def first_tap(block, b):
                w = [vec[:, bass.ds(V["conv"] + 4 * block + c, 1)] for c in (2, 3)]
                act.wait_ge(s("up_ready"), block + 1)
                act.activation(cy[:, b, :], upb[:, b, 2:T + 2], ACT.Identity, scale=w[0], bias=w[1])\
                   .then_inc(s("tap_made"), 1)

            def split_gated(pair):
                act.wait_ge(s("gv_done"), pair + 1)
                act.activation(big[:, bass.ds(pair, 1), 0:T], cy[:, 1:2, :], ACT.Copy).then_inc(s("xs_g_hi"), 1)

            def mlp_pairs(i, first=False, last=False):
                for q in range(2):
                    u = U_UP + 4 * i + 2 * q
                    pair = 2 * i + q
                    evac(u, 0)
                    hi(G_UP, i, 4, 2 * q + 3, DOWN_CELLS if last and q else KT)
                    if first and not q:
                        evac(u + 1, 1)
                        hi(G_UP, i, 4, 4)
                        norm(rstd[:, :], "h1")
                        first_tap(2 * pair, 0)
                    else:
                        split_gated(pair - 1)
                        first_tap(2 * pair, 0)
                        evac(u + 1, 1)
                        hi(G_UP, i, 4, 2 * q + 4, DOWN_CELLS if last else KT)
                    first_tap(2 * pair + 1, 1)
                    act.wait_ge(s("gate_conv"), pair + 1)
                    act.activation(gl[:, :], cy[:, 0, :], ACT.Gelu_apprx_tanh).then_inc(s("gelu_done"), 1)

            norm(rstd_mem[:, :], "mem")
            mlp_pairs(0, first=True)
            with act.Fori(0, FT // 2 - 2) as n:
                mlp_pairs(n + 1)
            mlp_pairs(FT // 2 - 1, last=True)
            split_gated(FT - 1)

            def down_pair(i, last=False):
                for j in range(8):
                    if j % 4 == 3:
                        act.wait_ge(w_used, G_DOWN + 8 * i + j + 1)
                        act.wait_ge(out_free, U_DOWN + 2 * i + j // 4 + 1)
                        act.activation(small[:, j // 4, :], ps[:, j // 4, T:2 * T], ACT.Copy).then_inc(small_ready, 1)
                    hi(G_DOWN, i, 8, j + 3, KT if last and j + 3 >= 8 else DOWN_CELLS)

            with act.Fori(0, KT // 2 - 1) as i:
                down_pair(i)
            act.wait_ge(s("p_in"), 16)
            for k in range(2):
                split_hi(xs_p[:, k, 0:T], p_raw[:, k, :], "xs_p_hi")
            down_pair(KT // 2 - 1, last=True)

            def pe_evac(blk, j):
                u = U_PE + 8 * blk + j
                if j < 7:
                    evac(u, j % 2, made=7 * blk + j + 1)
                else:
                    evac(u, j % 2, ahead=G_PE + blk - u)

            for j in range(8):
                pe_evac(0, j)
                if j == 3:
                    norm(rstd[:, :], "y")
            hi(G_PE, 0, 0, 3)

            def split_h2(c):
                act.wait_ge(*step("h2_ready", c + 1) if c < QUARTERS - 1 else (s("h2_last"), 1))
                act.activation(xs_h[:, quarter(c), 0:T], h[:, quarter(c), :], ACT.Copy).then_inc(s("xs_h_hi"), 1)

            for c in range(QUARTERS):
                pe_evac(1, 2 * c)
                pe_evac(1, 2 * c + 1)
                if c:
                    split_h2(c - 1)
            split_h2(QUARTERS - 1)
            hi(G_PE, 0, 0, 4)

            act.activation(dummy[:, 0:1], rstd[:, 0:1], ACT.Sigmoid)
            def split_h3(k):
                act.wait_ge(s("h3_ready"), k + 1)
                act.activation(act_a[:, bass.ds(k, 1), 0:T], h[:, bass.ds(k, 1), :], ACT.Copy,
                               scale=column("norm_g_2", k)).then_inc(s("xs_n_hi"), 1)

            def gate_blocks(i, first=False):
                for j in range(4):
                    k = 4 * i + j
                    evac(U_PG + k, j % 2, G_PG - U_PG)
                    hi(G_PG, i, 4, j + 3)
                    act.wait_ge(out_free, U_PG + k + 3)
                    act.activation(pg_s[:, j % 2, :], pg_x[:, j % 2, :], ACT.Sigmoid).then_inc(s("pg_sig"), 1)
                    if j or not first:
                        split_h3(k - 1)

            gate_blocks(0, first=True)
            with act.Fori(0, 3) as n:
                gate_blocks(n + 1)
            split_h3(KT - 1)

            for n in range(GROUPS):
                u = U_CONV + 2 * n
                evac(u, 0, G_PG - U_PG)
                hi(G_CONV, 0, 0, 2 * n + 3)
                evac(u + 1, 1, G_PG - U_PG)
                hi(G_CONV, 0, 0, 2 * n + 4)
                if n == 0:
                    norm(rstd[:, :], "h3")
                act.wait_ge(s("cv_lin"), n + 1)
                act.activation(ce[:, 0, :], cx[:, 1, :], ACT.Exp, scale=-1.0).then_inc(s("cv_exp"), 1)
            act.wait_ge(s("z_abs"), 1)
            act.activation(z1[:, :], z1[:, :], ACT.Exp, scale=-1.0).then_inc(s("z_exp"), 1)
            act.wait_ge(s("z_exp"), 1)
            act.activation(z1[:, :], z1[:, :], ACT.Ln, bias=1.0).then_inc(s("z_ln"), 1)

            def fox_turned(n):
                wait(act, "fp_turned", n + 1)
                act.activation(fpT[:, 0:3 * P], ps_t[:, 0:3 * P], ACT.Copy).then_inc(s("fpT_ready"), 1)

            def fox_out(n):
                wait(act, "fo_done", n + 1)
                act.activation(xs_y[:, bass.ds(GROUPS + n, 1), 0:T], fo[:, :].unsqueeze(1), ACT.Copy).then_inc(s("fo_hi"), 1)

            def fox_head(i, before=None):
                u = U_FOX + 4 * i
                evac(u, 0, G_PG - U_PG)
                hi(G_FOX, i, 4, 3)
                if before is not None:
                    fox_turned(before)
                evac(u + 1, 1, G_PG - U_PG)
                hi(G_FOX, i, 4, 4)
                evac(u + 2, 0, G_PG - U_PG)
                hi(G_FOX, i, 4, 5)
                if before is not None:
                    fox_out(before)
                wait(act, "fox_max", i + 1)
                act.activation(fs[:, 0:P], fs[:, 0:P], ACT.Exp, bias=cols[:, 10:11], accum_out=cols[:, 12:13]).then_inc(s("fox_exp"), 1)
                act.activation(fs[:, P:3 * P], fs[:, P:3 * P], ACT.Exp, bias=cols[:, 11:12], accum_out=cols[:, 13:14]).then_inc(s("fox_exp"), 1)
                evac(u + 3, 1, G_PG - U_PG)
                hi(G_FOX, i, 4, 6)
                wait(act, "fg_lin", i + 1)
                act.activation(fge[:, :], fgx[:, :], ACT.Exp, scale=-1.0).then_inc(s("fg_exp"), 1)
                wait(act, "fv_turned", i + 1)
                act.activation(fvtok[:, :, :], ps_b.rearrange("p (a b) -> p a b", a=2), ACT.Copy).then_inc(s("fvtok_ready"), 1)

            fox_head(0)
            with act.Fori(0, HEADS - 1) as n:
                fox_head(n + 1, n)

            def memory_turned(n):
                act.wait_ge(s("mp_turned"), n + 1)
                act.activation(fpT[:, :], ps_t[:, :], ACT.Copy).then_inc(s("mpT_ready"), 1)

            def memory_out(n):
                act.wait_ge(s("mo_done"), n + 1)
                act.activation(xs_y[:, GROUPS + HEADS + n, 0:T], fo[:, :], ACT.Copy).then_inc(s("mo_hi"), 1)

            for n in range(MEM_HEADS):
                u = U_MEM + 2 * n
                evac(u, 0, G_PG - U_PG)
                hi(G_MEM, 0, 0, 2 * n + 3)
                memory_turned(n - 1) if n else fox_turned(HEADS - 1)
                if n == 1:
                    norm(mu[:, :], "uc")
                if n == 3:
                    act.wait_ge(s("cl_ready"), GROUPS)
                    act.activation(usq[:, :, :], uc[:, :, :], ACT.Sigmoid).then_inc(s("cl_sig"), 1)
                evac(u + 1, 1, G_PG - U_PG)
                hi(G_MEM, 0, 0, 2 * n + 4)
                memory_out(n - 1) if n else fox_out(HEADS - 1)
                act.wait_ge(s("mem_max"), n + 1)
                for t in range(2):
                    act.activation(fs[:, t * T:t * T + T], ps_sc[:, t * T:t * T + T], ACT.Exp, bias=cols[:, 20 + t:21 + t],
                                   accum_out=cols[:, 22 + t:23 + t]).then_inc(s("mem_exp"), 1)
                act.wait_ge(s("mg_lin"), n + 1)
                act.activation(fge[:, :], fgx[:, :], ACT.Exp, scale=-1.0).then_inc(s("mg_exp"), 1)
                act.wait_ge(s("mv_turned"), n + 1)
                act.activation(fvtok[:, :, :], ps_b.rearrange("p (a b) -> p a b", a=2), ACT.Copy).then_inc(s("mvtok_ready"), 1)

            for k in range(GROUPS):
                evac(U_CG + k, k % 2, G_CG - U_CG)
                hi(G_CG, 0, 0, k + 3)
                if k == 0:
                    memory_turned(MEM_HEADS - 1)
                    act.wait_ge(s("cs_ready"), 1)
                    act.activation(xs_cv[:, :, 0:T], uc[:, :, :], ACT.Copy).then_inc(s("xs_cv_hi"), 1)
                if k == 1:
                    memory_out(MEM_HEADS - 1)
                act.wait_ge(s("cg_lin"), k + 1)
                act.activation(ce[:, k % 2, :], sg_c[:, k, :], ACT.Exp, scale=-1.0).then_inc(s("cg_exp"), 1)
            for k in range(GROUPS + 1):
                if k < GROUPS - 1:
                    evac(U_PW + k, k % 2, made=14 + k + 1)
                elif k < GROUPS:
                    evac(U_PW + k, k % 2, ahead=G_PW - U_PW - k)
                if k:
                    act.wait_ge(s("yc_ready"), k)
                    split_hi(xs_y[:, k - 1, 0:T], cx[:, (k - 1) % 2, :], "xs_yc_hi")
            hi(G_PW, 0, 0, 3)

            with act.Fori(0, 3) as i:
                for j in range(4):
                    evac(U_OUT2 + 4 * i + j, j % 2, G_OUT2 - U_OUT2)
                    hi(G_OUT2, i, 4, j + 3)
            for j in range(4):
                evac(U_OUT2 + 12 + j, j % 2, G_OUT2 - U_OUT2)
                if j < 1:
                    hi(G_OUT2, 0, 0, 12 + j + 3)
            norm(rstd[:, :], "h4")

        @block.vector
        def _(dve):
            chain = Chain(dve, vector_step)
            link = chain.link

            def lo(start, i, per, j, cells=KT):
                dve.wait_ge(w_hi, i * per + (start + j + 1))
                slot = (start + j) % NS
                part = slice(0, cells * P)
                dve.tensor_tensor(wlo[:, slot, part], stage[:, slot, part], whi[:, slot, part].bitcast(F32),
                                  ALU.subtract).then_inc(w_lo, 1)

            def add(u, b, dst=None):
                dve.wait_ge(small_ready, u + 1)
                dve.tensor_tensor(tmp[:, b, :] if dst is None else dst, ps[:, b, 0:T], small[:, b, :],
                                  ALU.add).then_inc(out_free, 1)

            def scaled(u, b, dst, done, by=None, factor=None):
                dve.wait_ge(out_free, u + 3)
                by = rstd[:, :] if by is None else by
                if factor is None:
                    dve.tensor_tensor(dst, tmp[:, b, :], by, ALU.mult).then_inc(s(done), 1)
                else:
                    dve.scalar_tensor_tensor(out=dst, in0=tmp[:, b, :], scalar=factor, in1=by,
                                             op0=ALU.mult, op1=ALU.mult).then_inc(s(done), 1)

            def logistic(e, exp_done, n):
                dve.wait_ge(s(exp_done), n)
                link(dve.tensor_scalar(e, e, LARGE, 1.0, ALU.min, ALU.add))
                link(dve.reciprocal(e, e))

            def mean_square(src, n, done):
                dve.tensor_scalar(n, src, 1.0 / D, EPS, ALU.mult, ALU.add).then_inc(event(done)[0], 1)

            dve.memset(dummy[:, :], 0.0).then_inc(out_free, 2)
            lo(G_MIX, 0, 8, 0)
            dve.wait_ge(s("vec_in"), 16)
            for k in range(KT):
                dve.wait_ge(*step("xs_x_hi", k + 1))
                dve.scalar_tensor_tensor(out=act_a[:, k, T:2 * T], in0=h[:, k, :], scalar=column("ln_mix_pre", k),
                                         in1=act_a[:, k, 0:T].bitcast(F32), op0=ALU.mult, op1=ALU.subtract)\
                   .then_inc(s("xs_x"), 1)
            lo(G_MIX, 0, 8, 1)
            lo(G_MIX, 0, 8, 2)
            lb, omlb, ex = cols[:, 16:24], cols[:, 24:32], cols[:, 8:16]
            link(dve.tensor_tensor(ex, column("lb", 0, HEADS), column("lb", 0, HEADS), ALU.subtract))
            link(dve.tensor_scalar(ex, ex, 1.0, None, ALU.add))
            link(dve.tensor_tensor(lb, ex, ex, ALU.subtract))
            link(dve.tensor_scalar(omlb, lb, -1.0, 1.0, ALU.mult, ALU.add))
            dve.wait_ge(s("consts_in"), 6 * 16)
            link(dve.tensor_copy(lmask[:, :, :], lmask_in[:, :, :]))
            add(0, 0)
            lo(G_MIX, 0, 8, 3)
            add(1, 1)
            lo(G_MIX, 0, 8, 4)
            dve.wait_ge(*event("x_summed"))
            mean_square(ps_a, rstd[:, :], "x_ms")
            link(dve.memset(sT[:, :], 0.0))
            dve.wait_ge(*event("x_norm"))

            def mem_lo(half):
                for k in range(half * KT // 2, (half + 1) * KT // 2):
                    dve.wait_ge(*step("xs_mem_hi", k + 1))
                    dve.scalar_tensor_tensor(out=xs_mem[:, k, T:2 * T], in0=mem_raw[:, k, :],
                                             scalar=column("mem_norm_g_2", k), in1=xs_mem[:, k, 0:T].bitcast(F32),
                                             op0=ALU.mult, op1=ALU.subtract).then_inc(s("xs_mem"), 1)

            def recurrence_gated(n):
                wait(dve, "osq_ready", n + 1)
                link(dve.scalar_tensor_tensor(out=on1[:, :], in0=ps_a, scalar=column("hgrn_norm", n), in1=eg[:, :],
                                              op0=ALU.mult, op1=ALU.mult))
                wait(dve, "o_summed", n + 1)
                dve.tensor_scalar(var[:, :], ps_lev[:, 1, 0, :], 1.0 / P, EPS, ALU.mult, ALU.add).then_inc(s("var_ready"), 1)

            def attention_split(n):
                wait(dve, "att_hi", n + 1)
                dve.tensor_tensor(xs_mix[:, bass.ds(HEADS + n, 1), T:2 * T], ps_b.unsqueeze(1),
                                  xs_mix[:, bass.ds(HEADS + n, 1), 0:T].bitcast(F32), ALU.subtract).then_inc(s("att_split"), 1)

            def recurrence_normed(n):
                wait(dve, "o_norm", n + 1)
                dve.tensor_tensor(osb[:, :], on1[:, :], var[:, :], ALU.mult).then_inc(s("o_done"), 1)

            def recurrence_split(n):
                wait(dve, "o_hi", n + 1)
                dve.tensor_tensor(xs_mix[:, bass.ds(n, 1), T:2 * T], osb[:, :].unsqueeze(1),
                                  xs_mix[:, bass.ds(n, 1), 0:T].bitcast(F32), ALU.subtract).then_inc(s("mix_done"), 1)

            diag = sT[:, :].rearrange("p (c t) -> p c t", c=3)[:, 0:3:2, :]

            def place_levels(i, levels):
                for n in levels:
                    if n % 2 == 0:
                        wait(dve, "lev_ready", i * 5 + n // 2 + 1)
                    wait(dve, "lev_used", i * LEVELS + n)
                    dve.memset(dummy[:, 0:1], 0.0)
                    dve.copy_predicated(diag, lmask[:, n, :].rearrange("p (c t) -> p c t", c=2),
                                        ps_lev[:, n // 2 % 2, n % 2, :].rearrange("p (c t) -> p c t", c=2)).then_inc(s("lev_used"), 1)

            def mixers_head(i, before=None):
                u = i * 8
                if before is None:
                    scaled(u, 0, hfx[:, :], "hf_lin")
                    scaled(u + 1, 1, hqx[:, :], "hq_lin")
                else:
                    add(u, 0)
                    scaled(u, 0, hfx[:, :], "hf_lin")
                    lo(G_MIX, i, 8, 3)
                    recurrence_gated(before)
                logistic(ef[:, :], "hf_exp", i + 1)
                wait(dve, "lev_in_ready", i * LEVELS)
                wait(dve, "lev_ready", i * 5)
                link(dve.tensor_scalar(pfx[:, :], ef[:, :], cols[:, bass.ds(24 + i, 1)], cols[:, bass.ds(16 + i, 1)],
                                       ALU.mult, ALU.add))
                dve.tensor_scalar(kk[:, :], pfx[:, :], -1.0, 1.0, ALU.mult, ALU.add).then_inc(s("fk_ready"), 1)
                if before is not None:
                    add(u + 1, 1)
                    scaled(u + 1, 1, hqx[:, :], "hq_lin")
                    lo(G_MIX, i, 8, 4)
                logistic(eq[:, :], "hq_exp", i + 1)
                dve.tensor_tensor(qq[:, :], hqx[:, :], eq[:, :], ALU.mult).then_inc(s("q_ready"), 1)
                if before is not None:
                    attention_split(before)
                add(u + 2, 0)
                lo(G_MIX, i, 8, 5)
                scaled(u + 2, 0, iT[:, :], "i_ready")
                if before is None:
                    mem_lo(0)
                add(u + 3, 1)
                lo(G_MIX, i, 8, 6)
                scaled(u + 3, 1, aqT[:, :], "aq_ready", factor=SCALE)
                if before is not None:
                    recurrence_normed(before)
                add(u + 4, 0)
                lo(G_MIX, i, 8, 7)
                scaled(u + 4, 0, akT[:, :], "ak_ready")
                if before is not None:
                    recurrence_split(before)
                place_levels(i, range(4))
                if before is None:
                    mem_lo(1)
                add(u + 5, 1)
                lo(G_MIX, i, 8, 8)
                scaled(u + 5, 1, avT[:, :], "av_ready")
                wait(dve, "sc_ready", i + 1)
                wait(dve, "p_turned", i)
                link(dve.tensor_tensor(sm[:, :], ps_sc[:, 0:3 * P], bias_att[:, :], ALU.add))
                link(dve.tensor_reduce(cols[:, 0:1], sm[:, 0:P], AX_X, ALU.max))
                link(dve.tensor_reduce(cols[:, 1:2], sm[:, P:3 * P], AX_X, ALU.max))
                dve.tensor_scalar(cols[:, 2:4], cols[:, 0:2], -1.0, None, ALU.mult).then_inc(s("att_max"), 1)
                place_levels(i, range(4, LEVELS))
                add(u + 6, 0)
                lo(G_MIX, i, 8, 9)
                scaled(u + 6, 0, hgx[:, :], "hg_lin")
                wait(dve, "att_exp", 2 * i + 2)
                link(dve.tensor_tensor(sm[:, :], sm[:, :], mult[:, :], ALU.mult))
                link(dve.tensor_reduce(cols[:, 4:5], sm[:, 0:P], AX_X, ALU.add))
                link(dve.tensor_reduce(cols[:, 5:6], sm[:, P:3 * P], AX_X, ALU.add))
                link(dve.reciprocal(cols[:, 6:8], cols[:, 4:6]))
                dve.tensor_scalar(sm[:, 0:P], sm[:, 0:P], cols[:, 6:7], None, ALU.mult).then_inc(s("p_ready"), 1)
                dve.tensor_scalar(sm[:, P:3 * P], sm[:, P:3 * P], cols[:, 7:8], None, ALU.mult).then_inc(s("p_ready"), 1)
                add(u + 7, 1, dst=mkv[:, bass.ds(i, 1), :].squeeze(1))
                lo(G_MIX, i, 8, 10)
                logistic(eg[:, :], "hg_exp", i + 1)
                link(dve.tensor_tensor(eg[:, :], eg[:, :], hgx[:, :], ALU.mult))

            mixers_head(0)
            with dve.Fori(0, HEADS - 1) as n:
                chain.enter(n, 16)
                mixers_head(n + 1, n)
                chain.leave(HEADS - 1)
            recurrence_gated(HEADS - 1)
            attention_split(HEADS - 1)
            recurrence_normed(HEADS - 1)
            recurrence_split(HEADS - 1)

            for j in range(4):
                add(U_OUT + j, j % 2, dst=mixed[:, j, :])
                lo(G_OUT, 0, 0, j + 3)
            with dve.Fori(0, 3) as i:
                for j in range(4):
                    add(U_OUT + 4 + 4 * i + j, j % 2, dst=mixed[:, bass.ds(4 + 4 * i + j, 1), :].squeeze(1))
                    lo(G_OUT + 4, i, 4, j + 3)
            dve.wait_ge(*event("mixed_summed"))
            mean_square(ps_a, rstd[:, :], "mixed_ms")
            dve.wait_ge(*step("mixed_gain", KT))
            dve.wait_ge(*event("mixed_norm"))
            by_norm = rstd[:, :].unsqueeze(1).to_broadcast([P, KT // QUARTERS, T])
            for c in range(QUARTERS):
                dve.tensor_tensor(mixed[:, quarter(c), :], mixed[:, quarter(c), :], by_norm, ALU.mult).then_inc(step("mixed_scaled", 0)[0], 1)
            last = quarter(QUARTERS - 1)
            dve.wait_ge(s("x_back"), QUARTERS * 16)
            dve.wait_ge(*step("mixed_scaled", QUARTERS))
            dve.tensor_tensor(h[:, last, :], h[:, last, :], mixed[:, last, :], ALU.add).then_inc(s("h1_last"), 1)
            for k in range(KT):
                dve.wait_ge(*step("xs_u_hi", k + 1))
                dve.scalar_tensor_tensor(out=act_a[:, k, T:2 * T], in0=h[:, k, :], scalar=column("ln_ffn_pre", k),
                                         in1=act_a[:, k, 0:T].bitcast(F32), op0=ALU.mult, op1=ALU.subtract)\
                   .then_inc(s("xs_u"), 1)
            dve.wait_ge(s("h1_sq"), QUARTERS)
            n = KT
            while n > 2:
                n //= 2
                link(dve.tensor_tensor(mixed[:, 0:n, :], mixed[:, 0:n, :], mixed[:, n:2 * n, :], ALU.add))
            dve.tensor_tensor(acc[:, :], mixed[:, 0, :], mixed[:, 1, :], ALU.add).then_inc(event("h1_sum")[0], 1)
            dve.wait_ge(*event("mem_summed"))
            mean_square(ps_sc[:, 0:T], rstd_mem[:, :], "mem_ms")
            link(dve.memset(upb[:, :, 0:2], 0.0))

            def conv(block, b, done):
                w = [vec[:, bass.ds(V["conv"] + 4 * block + c, 1)] for c in range(2)]
                dve.wait_ge(s("tap_made"), block + 1)
                link(dve.scalar_tensor_tensor(out=cy[:, b, :], in0=upb[:, b, 1:T + 1], scalar=w[1], in1=cy[:, b, :],
                                              op0=ALU.mult, op1=ALU.add))
                dve.scalar_tensor_tensor(out=cy[:, b, :], in0=upb[:, b, 0:T], scalar=w[0], in1=cy[:, b, :],
                                         op0=ALU.mult, op1=ALU.add).then_inc(s(done), 1)

            def gate(pair):
                conv(2 * pair + 1, 1, "val_conv")
                dve.wait_ge(s("gelu_done"), pair + 1)
                dve.wait_ge(s("val_conv"), pair + 1)
                dve.tensor_tensor(cy[:, 1, :], cy[:, 1, :], gl[:, :], ALU.mult).then_inc(s("gv_done"), 1)

            def split_gated(pair):
                dve.wait_ge(s("xs_g_hi"), pair + 1)
                dve.tensor_tensor(big[:, bass.ds(pair, 1), T:2 * T], cy[:, 1:2, :],
                                  big[:, bass.ds(pair, 1), 0:T].bitcast(F32), ALU.subtract).then_inc(s("xs_g"), 1)

            def mlp_pairs(i, first=False, last=False):
                for q in range(2):
                    u = U_UP + 4 * i + 2 * q
                    pair = 2 * i + q
                    add(u, 0)
                    if first and not q:
                        lo(G_UP, i, 4, 3)
                        add(u + 1, 1)
                        lo(G_UP, i, 4, 4)
                        dve.wait_ge(*event("h1_summed"))
                        mean_square(ps_b, rstd[:, :], "h1_ms")
                        conv(2 * pair, 0, "gate_conv")
                    else:
                        gate(pair - 1)
                        lo(G_UP, i, 4, 2 * q + 3, DOWN_CELLS if last and q else KT)
                        split_gated(pair - 1)
                        add(u + 1, 1)
                        conv(2 * pair, 0, "gate_conv")
                        lo(G_UP, i, 4, 2 * q + 4, DOWN_CELLS if last else KT)

            mlp_pairs(0, first=True)
            with dve.Fori(0, FT // 2 - 2) as n:
                chain.enter(n, 4)
                mlp_pairs(n + 1)
                chain.leave(FT // 2 - 2)
            mlp_pairs(FT // 2 - 1, last=True)
            gate(FT - 1)
            split_gated(FT - 1)

            def down_pair(i, last=False):
                for j in range(8):
                    if j % 4 == 3:
                        add(U_DOWN + 2 * i + j // 4, j // 4, dst=y[:, bass.ds(2 * i + j // 4, 1), :].squeeze(1))
                    lo(G_DOWN, i, 8, j + 3, KT if last and j + 3 >= 8 else DOWN_CELLS)

            with dve.Fori(0, KT // 2 - 1) as i:
                down_pair(i)
            for k in range(2):
                dve.wait_ge(s("xs_p_hi"), k + 1)
                dve.tensor_tensor(xs_p[:, k, T:2 * T], p_raw[:, k, :], xs_p[:, k, 0:T].bitcast(F32),
                                  ALU.subtract).then_inc(s("xs_p"), 1)
            down_pair(KT // 2 - 1, last=True)
            def pe_add(blk, j):
                add(U_PE + 8 * blk + j, j % 2, dst=pe_out[:, 8 * blk + j, :])

            for j in range(8):
                pe_add(0, j)
                if j == 3:
                    dve.wait_ge(*event("y_summed"))
                    mean_square(ps_a, rstd[:, :], "y_ms")
            lo(G_PE, 0, 0, 3)
            dve.wait_ge(*step("y_gain", KT))
            dve.wait_ge(*event("y_norm"))
            for c in range(QUARTERS):
                dve.tensor_tensor(y[:, quarter(c), :], y[:, quarter(c), :], by_norm, ALU.mult).then_inc(step("y_scaled", 0)[0], 1)
                pe_add(1, 2 * c)
                pe_add(1, 2 * c + 1)
            dve.wait_ge(*step("y_scaled", QUARTERS))
            dve.tensor_tensor(h[:, last, :], h[:, last, :], y[:, last, :], ALU.add).then_inc(s("h2_last"), 1)
            for c in range(QUARTERS):
                dve.wait_ge(s("xs_h_hi"), c + 1)
                dve.tensor_tensor(xs_h[:, quarter(c), T:2 * T], h[:, quarter(c), :],
                                  xs_h[:, quarter(c), 0:T].bitcast(F32), ALU.subtract).then_inc(s("xs_h"), 1)
            lo(G_PE, 0, 0, 4)

            def gated(k, b):
                dve.wait_ge(s("pg_sig"), k + 1)
                link(dve.tensor_tensor(pg_s[:, b:b + 1, :], pg_s[:, b:b + 1, :], pe_out[:, bass.ds(k, 1), :], ALU.mult))
                dve.tensor_tensor(h[:, bass.ds(k, 1), :], h[:, bass.ds(k, 1), :], pg_s[:, b:b + 1, :], ALU.add)\
                   .then_inc(s("h3_ready"), 1)

            def split_h3(k):
                dve.wait_ge(s("xs_n_hi"), k + 1)
                dve.scalar_tensor_tensor(out=act_a[:, bass.ds(k, 1), T:2 * T], in0=h[:, bass.ds(k, 1), :],
                                         scalar=column("norm_g_2", k), in1=act_a[:, bass.ds(k, 1), 0:T].bitcast(F32),
                                         op0=ALU.mult, op1=ALU.subtract).then_inc(s("xs_n"), 1)

            def gate_blocks(i, first=False):
                for j in range(4):
                    k = 4 * i + j
                    add(U_PG + k, j % 2, dst=pg_x[:, j % 2, :])
                    if j or not first:
                        gated(k - 1, (j - 1) % 2)
                    lo(G_PG, i, 4, j + 3)
                    if j or not first:
                        split_h3(k - 1)

            gate_blocks(0, first=True)
            with dve.Fori(0, 3) as n:
                chain.enter(n, 4)
                gate_blocks(n + 1)
                chain.leave(3)
            gated(KT - 1, 1)
            split_h3(KT - 1)
            link(dve.memset(upad[:, :, :], 0.0))
            link(dve.memset(one8[:, :], 1.0))
            for n in range(GROUPS):
                u = U_CONV + 2 * n
                add(u, 0)
                lo(G_CONV, 0, 0, 2 * n + 3)
                if n == 0:
                    add(u + 1, 1)
                    lo(G_CONV, 0, 0, 2 * n + 4)
                    dve.wait_ge(*event("h3_summed"))
                    mean_square(ps_b, rstd[:, :], "h3_ms")
                    dve.wait_ge(s("fox_in"), 32)
                    dve.tensor_tensor(wfg[:, :, :], wfg[:, :, :],
                                      column("norm_g_2", 0, KT).unsqueeze(2).to_broadcast([P, KT, HEADS]), ALU.mult).then_inc(s("wfg_ready"), 1)
                    dve.wait_ge(*event("h3_norm"))
                scaled(u, 0, cx[:, 0, :], "ca_lin")
                if n:
                    add(u + 1, 1)
                    lo(G_CONV, 0, 0, 2 * n + 4)
                scaled(u + 1, 1, cx[:, 1, :], "cv_lin")
                logistic(ce[:, 0, :], "cv_exp", n + 1)
                dve.wait_ge(s("ca_lin"), n + 1)
                dve.tensor_tensor(upad[:, n, TAPS - 1:], cx[:, 0, :], ce[:, 0, :], ALU.mult).then_inc(s("u_ready"), 1)

            dve.wait_ge(s("fl_ready"), 1)
            link(dve.tensor_tensor(zf[:, :], ps_t[0:HEADS, 0:T], rstd[0:HEADS, :], ALU.mult))
            link(dve.tensor_scalar(zf[:, :], zf[:, :], bfox[:, 0:1], None, ALU.add))
            link(dve.tensor_scalar(z1[:, :], zf[:, :], -1.0, None, ALU.mult))
            dve.tensor_tensor(z1[:, :], zf[:, :], z1[:, :], ALU.max).then_inc(s("z_abs"), 1)
            link(dve.tensor_scalar(zf[:, :], zf[:, :], 0.0, None, ALU.min))
            dve.wait_ge(s("z_ln"), 1)
            link(dve.tensor_tensor(z2[:, :], zf[:, :], z1[:, :], ALU.subtract))
            link(dve.tensor_tensor_scan(cc[:, :], one8[:, :], z2[:, :], 0.0, ALU.mult, ALU.add))

            def fox_gated(n):
                wait(dve, "fo_ready", n + 1)
                dve.tensor_tensor(fo[:, :], ps_a, fge[:, :], ALU.mult).then_inc(s("fo_done"), 1)

            def fox_split(n):
                wait(dve, "fo_hi", n + 1)
                dve.tensor_tensor(xs_y[:, bass.ds(GROUPS + n, 1), T:2 * T], fo[:, :].unsqueeze(1),
                                  xs_y[:, bass.ds(GROUPS + n, 1), 0:T].bitcast(F32), ALU.subtract).then_inc(s("fo_split"), 1)

            def fox_head(i, before=None):
                u = U_FOX + 4 * i
                add(u, 0)
                lo(G_FOX, i, 4, 3)
                wait(dve, "fsc_ready", i)
                scaled(u, 0, fqT[:, :], "fq_ready", factor=SCALE)
                dve.tensor_scalar(cpos[:, :], cc[:, :], ident[0:HEADS, bass.ds(i, 1)], None, ALU.mult).then_inc(s("c_ready"), 1)
                dve.tensor_scalar(cneg[:, :], cc[:, :], ident[0:HEADS, bass.ds(i, 1)], -1.0, ALU.mult, ALU.mult).then_inc(s("c_ready"), 1)
                add(u + 1, 1)
                lo(G_FOX, i, 4, 4)
                scaled(u + 1, 1, fkT[:, :], "fk2_ready")
                add(u + 2, 0)
                lo(G_FOX, i, 4, 5)
                scaled(u + 2, 0, fvT[:, :], "fv_ready")
                if before is not None:
                    fox_gated(before)
                wait(dve, "fsc_ready", i + 1)
                wait(dve, "fp_turned", i)
                link(dve.tensor_tensor(fs[:, 0:3 * P], ps_sc[:, 0:3 * P], bias_fox, ALU.add))
                link(dve.tensor_reduce(cols[:, 8:9], fs[:, 0:P], AX_X, ALU.max))
                link(dve.tensor_reduce(cols[:, 9:10], fs[:, P:3 * P], AX_X, ALU.max))
                dve.tensor_scalar(cols[:, 10:12], cols[:, 8:10], -1.0, None, ALU.mult).then_inc(s("fox_max"), 1)
                if before is not None:
                    fox_split(before)
                add(u + 3, 1)
                wait(dve, "fox_exp", 2 * i + 2)
                link(dve.reciprocal(cols[:, 14:16], cols[:, 12:14]))
                dve.tensor_scalar(fs[:, 0:P], fs[:, 0:P], cols[:, 14:15], None, ALU.mult).then_inc(s("fp_ready"), 1)
                dve.tensor_scalar(fs[:, P:3 * P], fs[:, P:3 * P], cols[:, 15:16], None, ALU.mult).then_inc(s("fp_ready"), 1)
                lo(G_FOX, i, 4, 6)
                scaled(u + 3, 1, fgx[:, :], "fg_lin")
                logistic(fge[:, :], "fg_exp", i + 1)
                link(dve.tensor_tensor(fge[:, :], fge[:, :], fgx[:, :], ALU.mult))

            fox_head(0)
            with dve.Fori(0, HEADS - 1) as n:
                chain.enter(n, 7)
                fox_head(n + 1, n)
                chain.leave(HEADS - 1)

            uc_mean = ps_lev[:, 0, 0, :]
            uc_square = ps_lev[:, 1, 0, :]
            by_mean = mu[:, :].unsqueeze(1).to_broadcast([P, GROUPS, T])

            def memory_gated(n):
                dve.wait_ge(s("mo_ready"), n + 1)
                dve.tensor_tensor(fo[:, :], ps_a, fge[:, :], ALU.mult).then_inc(s("mo_done"), 1)

            def memory_split(n):
                dve.wait_ge(s("mo_hi"), n + 1)
                dve.tensor_tensor(xs_y[:, GROUPS + HEADS + n, T:2 * T], fo[:, :],
                                  xs_y[:, GROUPS + HEADS + n, 0:T].bitcast(F32), ALU.subtract).then_inc(s("mo_split"), 1)

            for n in range(MEM_HEADS):
                u = U_MEM + 2 * n
                if n == 0:
                    dve.wait_ge(*event("uc_summed"))
                    link(dve.tensor_scalar(mu[:, :], uc_mean, 1.0 / (GROUPS * P), None, ALU.mult))
                    link(dve.tensor_tensor(uc[:, :, :], uc[:, :, :], by_mean, ALU.subtract))
                    dve.tensor_tensor(usq[:, :, :], uc[:, :, :], uc[:, :, :], ALU.mult).then_inc(s("usq_ready"), 1)
                if n == 1:
                    dve.wait_ge(*event("usq_summed"))
                    dve.tensor_scalar(mu[:, :], uc_square, 1.0 / (GROUPS * P), EPS, ALU.mult, ALU.add).then_inc(event("uc_ms")[0], 1)
                add(u, 0)
                lo(G_MEM, 0, 0, 2 * n + 3)
                scaled(u, 0, fqT[:, :], "mq_ready", factor=SCALE)
                if n == 2:
                    dve.wait_ge(*event("uc_norm"))
                    link(dve.tensor_tensor(uc[:, :, :], uc[:, :, :], by_mean, ALU.mult))
                    for k in range(GROUPS):
                        dve.tensor_scalar(uc[:, k, :], uc[:, k, :], column("conv_ln_g", k), column("conv_ln_b", k),
                                          ALU.mult, ALU.add).then_inc(s("cl_ready"), 1)
                add(u + 1, 1)
                lo(G_MEM, 0, 0, 2 * n + 4)
                memory_gated(n - 1) if n else fox_gated(HEADS - 1)
                dve.wait_ge(s("msc_ready"), n + 1)
                link(dve.tensor_reduce(cols[:, 18:20], ps_sc[:, :].rearrange("p (c t) -> p c t", c=2), AX_X, ALU.max))
                dve.tensor_scalar(cols[:, 20:22], cols[:, 18:20], -1.0, None, ALU.mult).then_inc(s("mem_max"), 1)
                scaled(u + 1, 1, fgx[:, :], "mg_lin")
                memory_split(n - 1) if n else fox_split(HEADS - 1)
                dve.wait_ge(s("mem_exp"), 2 * n + 2)
                link(dve.reciprocal(cols[:, 24:26], cols[:, 22:24]))
                for t in range(2):
                    dve.tensor_scalar(fs[:, t * T:t * T + T], fs[:, t * T:t * T + T], cols[:, 24 + t:25 + t], None,
                                      ALU.mult).then_inc(s("mp_ready"), 1)
                logistic(fge[:, :], "mg_exp", n + 1)
                link(dve.tensor_tensor(fge[:, :], fge[:, :], fgx[:, :], ALU.mult))
            dve.wait_ge(s("cl_sig"), 1)
            dve.tensor_tensor(uc[:, :, :], uc[:, :, :], usq[:, :, :], ALU.mult).then_inc(s("cs_ready"), 1)

            for k in range(GROUPS):
                add(U_CG + k, k % 2)
                lo(G_CG, 0, 0, k + 3)
                if k == 1:
                    memory_gated(MEM_HEADS - 1)
                    dve.wait_ge(s("xs_cv_hi"), 1)
                    dve.tensor_tensor(xs_cv[:, :, T:2 * T], uc[:, :, :], xs_cv[:, :, 0:T].bitcast(F32),
                                      ALU.subtract).then_inc(s("xs_cv"), 1)
                scaled(U_CG + k, k % 2, sg_c[:, k, :], "cg_lin")
                if k == 1:
                    memory_split(MEM_HEADS - 1)
                logistic(ce[:, k % 2, :], "cg_exp", k + 1)
                link(dve.tensor_tensor(sg_c[:, k, :], sg_c[:, k, :], ce[:, k % 2, :], ALU.mult))
            for k in range(GROUPS + 1):
                if k < GROUPS:
                    add(U_PW + k, k % 2)
                    dve.wait_ge(out_free, U_PW + k + 3)
                    dve.tensor_tensor(cx[:, k % 2, :], tmp[:, k % 2, :], sg_c[:, k, :], ALU.mult).then_inc(s("yc_ready"), 1)
                if k:
                    dve.wait_ge(s("xs_yc_hi"), k)
                    dve.tensor_tensor(xs_y[:, k - 1, T:2 * T], cx[:, (k - 1) % 2, :], xs_y[:, k - 1, 0:T].bitcast(F32),
                                      ALU.subtract).then_inc(s("xs_yc"), 1)
            lo(G_PW, 0, 0, 3)

            def out2(i, j, ahead):
                u = U_OUT2 + 4 * i + j
                add(u, j % 2)
                if ahead:
                    lo(G_OUT2, i, 4, j + 3)
                dve.wait_ge(out_free, u + 3)
                k = 4 * i + j
                dve.tensor_tensor(h4[:, bass.ds(k, 1), :], tmp[:, j % 2:j % 2 + 1, :], h[:, bass.ds(k, 1), :],
                                  ALU.add).then_inc(s("h4_ready"), 1)

            with dve.Fori(0, 3) as i:
                for j in range(4):
                    out2(i, j, True)
            for j in range(4):
                out2(3, j, j < 1)
            dve.wait_ge(*event("h4_summed"))
            mean_square(ps_a, rstd[:, :], "h4_ms")
            dve.wait_ge(*event("h4_norm"))
            dve.wait_ge(*step("h4_gain", KT))
            for c in range(QUARTERS):
                dve.tensor_tensor(o_out[:, quarter(c), :], h4[:, quarter(c), :], by_norm, ALU.mult).then_inc(s("o_ready"), 1)

        @block.gpsimd
        def _(pool):
            chain = Chain(pool, pool_step)
            link = chain.link


            def halve(t, n, dst, done):
                while n > 2:
                    n //= 2
                    link(pool.tensor_tensor(t[:, 0:n, :], t[:, 0:n, :], t[:, n:2 * n, :], ALU.add))
                pool.tensor_tensor(dst, t[:, 0, :], t[:, 1, :], ALU.add).then_inc(event(done)[0], 1)

            for c in range(QUARTERS):
                pool.wait_ge(s(f"x_in{c}"), 16)
                link(pool.tensor_tensor(squares[:, quarter(c), :], h[:, quarter(c), :], h[:, quarter(c), :], ALU.mult))
            halve(squares, KT, acc[:, :], "x_sum")

            def decays(i):
                wait(pool, "fk_ready", i + 1)
                wait(pool, "q_ready", i + 1)
                wait(pool, "lev_ready", i * 5)
                for L in range(LEVELS):
                    m = 2 ** L

                    def halves(t):
                        v = t.rearrange("p (b two m) -> p b two m", two=2, m=m)
                        return v[:, :, 0, :], v[:, :, 1, :]

                    shape = [P, T // (2 * m), m]
                    (x0, x1), (p0, p1), (s0, s1) = halves(lev_in[:, L, :]), halves(pfx[:, :]), halves(sfx[:, :])
                    (k0, _), (_, q1) = halves(kk[:, :]), halves(qq[:, :])
                    link(pool.tensor_tensor(x1, q1, p1, ALU.mult))
                    if L == 0:
                        both = ones[:, :].unsqueeze(1).to_broadcast([P, 2, P])
                        link(pool.tensor_tensor(sfx[:, :].rearrange("p (a b) -> p a b", a=2), both, both, ALU.mult))
                    pool.tensor_tensor(x0, k0, s0, ALU.mult).then_inc(s("lev_in_ready"), 1)
                    if L < LEVELS - 1:
                        pool.wait_ge(s("lev_in_ready"), i * LEVELS + L + 1)
                        link(pool.tensor_tensor(s0, s0, p1[:, :, m - 1:m].to_broadcast(shape), ALU.mult))
                        link(pool.tensor_tensor(p1, p1, p0[:, :, m - 1:m].to_broadcast(shape), ALU.mult))

            decays(0)
            with pool.Fori(0, HEADS - 1) as n:
                chain.enter(n, 23)
                decays(n + 1)
                chain.leave(HEADS - 1)

            def squares_and_gain(count, tile, sq, ready, done, gain):
                link(pool.memset(acc[:, :], 0.0))
                total = acc[:, :].unsqueeze(1)
                with pool.Fori(0, count) as i:
                    chain.enter(i, 1)
                    ready(i)
                    link(pool.tensor_tensor(sq, tile(i), tile(i), ALU.mult))
                    pool.tensor_tensor(total, total, sq, ALU.add).then_inc(step(done + "_acc", 0)[0], 1)
                    if gain is not None:
                        g = column(gain, i).unsqueeze(2).to_broadcast([P, 1, T])
                        pool.tensor_tensor(tile(i), tile(i), g, ALU.mult).then_inc(step(done + "_gain", 0)[0], 1)
                    pool.wait_ge(*step(done + "_acc", i + 1))
                    chain.leave(count)

            pool.wait_ge(s("mem_back"), QUARTERS * 16)
            link(pool.tensor_tensor(mem_again[:, :, :], mem_again[:, :, :], mem_again[:, :, :], ALU.mult))
            halve(mem_again, KT, rstd_mem[:, :], "mem_sum")
            squares_and_gain(KT, lambda i: mixed[:, bass.ds(i, 1), :], sq1[:, :].unsqueeze(1),
                             lambda i: pool.wait_ge(out_free, U_OUT + i + 3), "mixed", "ln_mix_post")
            pool.wait_ge(s("x_back"), QUARTERS * 16)
            for c in range(QUARTERS - 1):
                pool.wait_ge(*step("mixed_scaled", c + 1))
                pool.tensor_tensor(h[:, quarter(c), :], h[:, quarter(c), :], mixed[:, quarter(c), :], ALU.add)\
                    .then_inc(step("h1_ready", 0)[0], 1)
            pool.wait_ge(*event("h1_norm"))
            def token_norm(i):
                for q in range(4):
                    n = 4 * i + q
                    pool.wait_ge(out_free, U_UP + n + 3)
                    wait(pool, "gate_conv" if q % 2 == 0 else "val_conv", 2 * i + q // 2)
                    pool.tensor_tensor(upb[:, q % 2, 2:T + 2], tmp[:, q % 2, :], rstd[:, :], ALU.mult).then_inc(s("up_ready"), 1)

            token_norm(0)
            pool.wait_ge(*event("mem_norm"))
            pool.tensor_tensor(mkv[:, :, :], mkv[:, :, :], rstd_mem[:, :].unsqueeze(1).to_broadcast([P, HEADS, T]),
                               ALU.mult).then_inc(s("mkv_ready"), 1)
            with pool.Fori(0, FT // 2 - 1) as n:
                token_norm(n + 1)
            squares_and_gain(KT, lambda i: y[:, bass.ds(i, 1), :], sq2[:, :].unsqueeze(1),
                             lambda i: pool.wait_ge(out_free, U_DOWN + i + 3), "y", "ln_ffn_post")
            for c in range(QUARTERS - 1):
                pool.wait_ge(*step("y_scaled", c + 1))
                pool.tensor_tensor(h[:, quarter(c), :], h[:, quarter(c), :], y[:, quarter(c), :], ALU.add)\
                    .then_inc(step("h2_ready", 0)[0], 1)
            squares_and_gain(KT, lambda i: h[:, bass.ds(i, 1), :], sq3[:, :].unsqueeze(1),
                             lambda i: pool.wait_ge(s("h3_ready"), i + 1), "h3", None)

            pool.wait_ge(s("u_ready"), GROUPS)
            taps = vec[:, V["taps"]:V["taps"] + GROUPS * TAPS].rearrange("p (k t) -> p k t", k=GROUPS)
            every = [P, GROUPS, T]

            def tap_product(dst, tap):
                return pool.tensor_tensor(dst, upad[:, :, bass.ds(tap, T)],
                                          taps[:, :, bass.ds(tap, 1)].to_broadcast(every), ALU.mult)

            tap_product(uc[:, :, :], 0).then_inc(s("tap_done"), 1)
            pool.wait_ge(s("tap_done"), 1)
            pool.tensor_tensor(uc[:, :, :], uc[:, :, :], column("conv_b_2", 0, GROUPS).unsqueeze(2).to_broadcast(every),
                               ALU.add).then_inc(s("tap_done"), 1)
            with pool.Fori(0, (TAPS - 1) // 2) as i:
                chain.enter(i, 2)
                for j, made in enumerate((usq, sg_c)):
                    pool.wait_ge(s("tap_done"), 2 * i + j + 1)
                    link(tap_product(made[:, :, :], 2 * i + j + 1))
                    pool.wait_ge(s("tap_done"), 2 * i + j + 2)
                    pool.tensor_tensor(uc[:, :, :], uc[:, :, :], made[:, :, :], ALU.add).then_inc(s("tap_done"), 1)
                chain.leave((TAPS - 1) // 2)
            pool.wait_ge(*event("h3_ms"))
            squares_and_gain(KT, lambda i: h4[:, bass.ds(i, 1), :], sq4[:, 0:1, :],
                             lambda i: pool.wait_ge(s("h4_ready"), i + 1), "h4", "final_g")

        @block.tensor
        def _(pe):
            def product(slot, c, act, bank, start, stop):
                pe.matmul(ps[:, bank, :], whi[:, slot, c * P:(c + 1) * P], act, start=start, stop=False)
                return pe.matmul(ps[:, bank, T:2 * T], wlo[:, slot, c * P:(c + 1) * P], act[:, 0:T],
                                 start=False, stop=stop)

            def cells(slot, bank, xs, order, opens=True, closes=True, ready=None):
                for n, c in enumerate(order):
                    if ready is not None:
                        ready(c)
                    ins = product(slot, c, xs[:, c, :], bank, opens and n == 0, closes and n == len(order) - 1)
                return ins

            def await_block(start, i, per, j, u):
                pe.wait_ge(w_lo, i * per + (start + j + 1))
                pe.wait_ge(out_free, u + 1)

            def whole(start, i, per, j, u, bank, xs, order=tuple(range(KT)), ready=None):
                await_block(start, i, per, j, u)
                cells((start + j) % NS, bank, xs, order, ready=ready).then_inc(w_used, 1)

            def column_sums(dst, srcs, waits, done):
                for n, src in enumerate(srcs):
                    pe.wait_ge(*waits(n))
                    ins = pe.matmul(dst, ones[:, :], src, start=n == 0, stop=n == len(srcs) - 1)
                ins.then_inc(event(done)[0], 1)

            def turn(dst, src, done, inc=1):
                ins = pe.transpose(dst, src, ident[:, :])
                if inc:
                    ins.then_inc(s(done), 1)

            def masked_scores(q, k, terms):
                for t, (c0, c1) in enumerate(((0, P), (P, 3 * P))):
                    rows, n = slice(t * P, t * P + P), c1 - c0
                    for m, (l, r) in enumerate(terms(rows, n)):
                        pe.matmul(ps_sc[:, c0:c1], l, r, start=m == 0, stop=False)
                    ins = pe.matmul(ps_sc[:, c0:c1], q[:, rows], k[:, 0:n], start=not terms(rows, n), stop=True)
                return ins

            def weighted(dst, v, pt):
                pe.matmul(dst, v[:, 0, :], pt[:, 0:T], start=True, stop=False)
                return pe.matmul(dst[:, P:T], v[:, 1, :], pt[:, T:3 * P], start=False, stop=True)

            def recurrence_summed(n):
                wait(pe, "osq_ready", n + 1)
                wait(pe, "lev_used", (n + 1) * LEVELS)
                pe.matmul(ps_lev[:, 1, 0, :], ones[:, :], osq[:, :], start=True, stop=True).then_inc(s("o_summed"), 1)

            def attention_turned(n):
                wait(pe, "p_ready", 2 * n + 2)
                wait(pe, "avtok_ready", n + 1)
                for c in range(3):
                    turn(ps_t[:, c * P:(c + 1) * P], sm[:, c * P:(c + 1) * P], "p_turned", c == 2)

            def attention_out(n):
                wait(pe, "pT_ready", n + 1)
                weighted(ps_b, avtok, pT).then_inc(s("att_out"), 1)

            def levels(i, which):
                for n in which:
                    if 4 <= n < LEVELS and n % 2 == 0:
                        wait(pe, "lev_used", i * LEVELS + n - 2)
                    if n:
                        wait(pe, "lev_in_ready", i * LEVELS + n)
                    keys, queries = (kk, qq) if n == 0 else (lev_in[:, n - 1, :],) * 2
                    if n < LEVELS:
                        for c in range(2):
                            tile = slice(c * P, c * P + P)
                            ins = pe.matmul(ps_lev[:, n // 2 % 2, n % 2, tile], keys[:, tile], queries[:, tile],
                                            start=True, stop=True)
                    else:
                        ins = pe.matmul(ps_cross, keys[:, 0:P], queries[:, P:T], start=True, stop=True)
                    if n % 2 or n == LEVELS:
                        ins.then_inc(s("lev_ready"), 1)

            def mixers_head(i, before=None):
                first = before is None
                u = i * 8
                whole(G_MIX, i, 8, 0, u, 0, act_a, ready=(lambda c: pe.wait_ge(s("xs_x"), c + 1)) if first else None)
                if not first:
                    recurrence_summed(before)
                    attention_turned(before)
                whole(G_MIX, i, 8, 1, u + 1, 1, act_a)
                if not first:
                    attention_out(before)
                whole(G_MIX, i, 8, 2, u + 2, 0, act_a)
                if first:
                    pe.wait_ge(s("consts_in"), 6 * 16)
                    column_sums(ps_a, [acc[:, :]], lambda n: event("x_sum"), "x_summed")
                whole(G_MIX, i, 8, 3, u + 3, 1, act_a)
                whole(G_MIX, i, 8, 4, u + 4, 0, act_a)
                wait(pe, "i_ready", i + 1)
                turn(ps_t[:, 0:P], iT[:, 0:P], None, 0)
                turn(ps_t[:, P:T], iT[:, P:T], "i_turned")
                wait(pe, "fk_ready", i + 1)
                wait(pe, "q_ready", i + 1)
                wait(pe, "var_ready", i)
                levels(i, range(4))
                whole(G_MIX, i, 8, 5, u + 5, 1, act_a)
                wait(pe, "aq_ready", i + 1)
                wait(pe, "ak_ready", i + 1)
                wait(pe, "att_max", i)
                masked_scores(aqT, akT, lambda rows, n: ()).then_inc(s("sc_ready"), 1)
                levels(i, range(4, LEVELS + 1))
                whole(G_MIX, i, 8, 6, u + 6, 0, act_a)
                wait(pe, "av_ready", i + 1)
                wait(pe, "vtok_ready", i + 1)
                turn(ps_t[:, 0:P], avT[:, 0:P], None, 0)
                turn(ps_t[:, P:T], avT[:, P:T], "av_turned")
                whole(G_MIX, i, 8, 7, u + 7, 1, xs_mem, ready=(lambda c: pe.wait_ge(s("xs_mem"), c + 1)) if first else None)
                wait(pe, "lev_used", (i + 1) * LEVELS)
                wait(pe, "cross_ready", i + 1)
                weighted(ps_a, vtok, sT).then_inc(s("hg_out"), 1)

            mixers_head(0)
            with pe.Fori(0, HEADS - 1) as n:
                mixers_head(n + 1, n)

            late = (HEADS - 1, 2 * HEADS - 1)
            early = [c for c in range(KT) if c not in late]
            recurrence_summed(HEADS - 1)
            attention_turned(HEADS - 1)
            pe.wait_ge(s("mix_done"), HEADS - 1)
            await_block(G_OUT, 0, 0, 0, U_OUT)
            cells(G_OUT % NS, 0, xs_mix, early, closes=False)
            attention_out(HEADS - 1)
            await_block(G_OUT, 0, 0, 1, U_OUT + 1)
            cells((G_OUT + 1) % NS, 1, xs_mix, early, closes=False)
            pe.wait_ge(s("att_split"), HEADS)
            pe.wait_ge(s("mix_done"), HEADS)
            for j in range(2):
                cells((G_OUT + j) % NS, j, xs_mix, late, opens=False).then_inc(w_used, 1)
            for j in range(2, 4):
                whole(G_OUT, 0, 0, j, U_OUT + j, j % 2, xs_mix)
            with pe.Fori(0, 3) as i:
                for j in range(4):
                    whole(G_OUT + 4, i, 4, j, U_OUT + 4 + 4 * i + j, j % 2, xs_mix)
            column_sums(ps_a, [acc[:, :]], lambda n: step("mixed_acc", KT), "mixed_summed")
            column_sums(ps_sc[:, 0:T], [rstd_mem[:, :]], lambda n: event("mem_sum"), "mem_summed")

            for j in range(4):
                whole(G_UP, 0, 0, j, U_UP + j, j % 2, act_a, ready=None if j else lambda c: pe.wait_ge(s("xs_u"), c + 1))
                if j == 1:
                    column_sums(ps_b, [acc[:, :]], lambda n: event("h1_sum"), "h1_summed")
            with pe.Fori(0, FT // 2 - 1) as i:
                for j in range(4):
                    whole(G_UP + 4, i, 4, j, U_UP + 4 + 4 * i + j, j % 2, act_a)
            with pe.Fori(0, KT // 2) as i:
                for j in range(8):
                    part, bank = j % 4, j // 4
                    pe.wait_ge(w_lo, G_DOWN + 8 * i + j + 1)
                    if part == 0:
                        pe.wait_ge(out_free, U_DOWN + 2 * i + bank + 1)
                    if j < 4:
                        pe.wait_ge(s("xs_g"), DOWN_CELLS * (part + 1))
                    for c in range(DOWN_CELLS):
                        k = DOWN_CELLS * part + c
                        ins = product((G_DOWN + j) % NS, c, big[:, k, :], bank, k == 0, k == FT - 1)
                    ins.then_inc(w_used, 1)

            def parts(g, u0, outs, last, per, xs):
                pe.wait_ge(w_lo, g + 1)
                for o in outs:
                    pe.wait_ge(out_free, u0 + o + 1)
                    for c in range(per):
                        ins = product(g % NS, o * per + c, xs[:, c, :], o % 2, c == 0, c == per - 1)
                    ins.then_inc(w_used if o == last else part_made, 1)

            pe.wait_ge(s("xs_p"), 2)
            parts(G_PE, U_PE, range(4), 7, 2, xs_p)
            column_sums(ps_a, [acc[:, :]], lambda n: step("y_acc", KT), "y_summed")
            parts(G_PE, U_PE, range(4, 8), 7, 2, xs_p)
            parts(G_PE + 1, U_PE + 8, range(8), 7, 2, xs_p)
            for j in range(4):
                whole(G_PG, 0, 0, j, U_PG + j, j % 2, xs_h,
                      ready=None if j else lambda c: pe.wait_ge(s("xs_h"), c * QUARTERS // KT + 1))
            with pe.Fori(0, 3) as i:
                for j in range(4):
                    whole(G_PG + 4, i, 4, j, U_PG + 4 + 4 * i + j, j % 2, xs_h)

            for j in range(2 * GROUPS):
                whole(G_CONV, 0, 0, j, U_CONV + j, j % 2, act_a, ready=None if j else lambda c: pe.wait_ge(s("xs_n"), c + 1))
                if j == 1:
                    column_sums(ps_b, [acc[:, :]], lambda n: step("h3_acc", KT), "h3_summed")
            pe.wait_ge(s("wfg_ready"), 1)
            for k in range(KT):
                ins = pe.matmul(ps_t[0:HEADS, 0:T], wfg[:, k, :], h[:, k, :], start=k == 0, stop=k == KT - 1)
            ins.then_inc(s("fl_ready"), 1)

            def fox_turned(n):
                wait(pe, "fp_ready", 2 * n + 2)
                for c in range(3):
                    turn(ps_t[:, c * P:(c + 1) * P], fs[:, c * P:(c + 1) * P], "fp_turned", c == 2)

            def fox_out(n):
                wait(pe, "fvtok_ready", n + 1)
                wait(pe, "fpT_ready", n + 1)
                weighted(ps_a, fvtok, fpT).then_inc(s("fo_ready"), 1)

            def fox_head(i, before=None):
                u = U_FOX + 4 * i
                whole(G_FOX, i, 4, 0, u, 0, act_a)
                if before is not None:
                    fox_turned(before)
                whole(G_FOX, i, 4, 1, u + 1, 1, act_a)
                if before is not None:
                    fox_out(before)
                whole(G_FOX, i, 4, 2, u + 2, 0, act_a)
                wait(pe, "c_ready", 2 * i + 2)
                wait(pe, "fq_ready", i + 1)
                wait(pe, "fk2_ready", i + 1)
                wait(pe, "fox_max", i)
                masked_scores(fqT, fkT, lambda rows, n: ((cpos[:, rows], one8[:, 0:n]), (one8[:, 0:P], cneg[:, 0:n])))\
                    .then_inc(s("fsc_ready"), 1)
                whole(G_FOX, i, 4, 3, u + 3, 1, act_a)
                wait(pe, "fv_ready", i + 1)
                turn(ps_b[:, 0:P], fvT[:, 0:P], None, 0)
                turn(ps_b[:, P:T], fvT[:, P:T], "fv_turned")

            fox_head(0)
            with pe.Fori(0, HEADS - 1) as n:
                fox_head(n + 1, n)

            def memory_turned(n):
                pe.wait_ge(s("mp_ready"), 2 * n + 2)
                for t in range(2):
                    for m in range(2):
                        turn(ps_t[:, m * T + t * P:m * T + t * P + P], fs[:, t * T + m * P:t * T + m * P + P],
                             "mp_turned", t and m)

            def memory_out(n):
                pe.wait_ge(s("mvtok_ready"), n + 1)
                pe.wait_ge(s("mpT_ready"), n + 1)
                wait(pe, "mo_done", n)
                pe.matmul(ps_a, fvtok[:, 0, :], fpT[:, 0:T], start=True, stop=False)
                pe.matmul(ps_a, fvtok[:, 1, :], fpT[:, T:2 * T], start=False, stop=True).then_inc(s("mo_ready"), 1)

            column_sums(ps_lev[:, 0, 0, :], [uc[:, k, :] for k in range(GROUPS)], lambda n: (s("tap_done"), TAPS + 1), "uc_summed")
            pe.wait_ge(s("mkv_ready"), 1)
            for n in range(MEM_HEADS):
                u = U_MEM + 2 * n
                whole(G_MEM, 0, 0, 2 * n, u, 0, act_a)
                memory_turned(n - 1) if n else fox_turned(HEADS - 1)
                whole(G_MEM, 0, 0, 2 * n + 1, u + 1, 1, act_a)
                memory_out(n - 1) if n else fox_out(HEADS - 1)
                pe.wait_ge(s("mq_ready"), n + 1)
                for t in range(2):
                    ins = pe.matmul(ps_sc[:, t * T:t * T + T], fqT[:, t * P:t * P + P], mkv[:, n, :], start=True, stop=True)
                ins.then_inc(s("msc_ready"), 1)
                turn(ps_b[:, 0:P], mkv[:, MEM_HEADS + n, 0:P], None, 0)
                turn(ps_b[:, P:T], mkv[:, MEM_HEADS + n, P:T], "mv_turned")
                if n == 0:
                    column_sums(ps_lev[:, 1, 0, :], [usq[:, k, :] for k in range(GROUPS)], lambda n: (s("usq_ready"), 1), "usq_summed")
            for k in range(GROUPS):
                whole(G_CG, 0, 0, k, U_CG + k, k % 2, act_a)
                if k == 0:
                    memory_turned(MEM_HEADS - 1)
                if k == 1:
                    memory_out(MEM_HEADS - 1)
            pe.wait_ge(s("xs_cv"), 1)
            parts(G_PW, U_PW, range(GROUPS), GROUPS - 1, GROUPS, xs_cv)

            pe.wait_ge(s("fo_split"), HEADS)
            pe.wait_ge(s("mo_split"), MEM_HEADS)
            order = tuple(range(GROUPS, KT)) + tuple(range(GROUPS))
            with pe.Fori(0, 4) as i:
                for j in range(4):
                    whole(G_OUT2, i, 4, j, U_OUT2 + 4 * i + j, j % 2, xs_y, order,
                          ready=None if j else lambda c: c == 0 and pe.wait_ge(s("xs_yc"), GROUPS))
            column_sums(ps_a, [acc[:, :]], lambda n: step("h4_acc", KT), "h4_summed")


def kernel(**inputs):
    import concourse.bacc as bacc
    from concourse.bass_utils import run_bass_kernel_spmd

    f32, b16 = np.float32, mybir.dt.np(BF16)
    get = {n: np.asarray(x) for n, x in inputs.items()}

    def features(x):
        return np.ascontiguousarray(x.T.reshape(-1, P, x.shape[0]).transpose(1, 0, 2))

    def vector(x):
        return x.reshape(-1, P).T

    def blocks(w):
        k, n = w.shape
        return w.reshape(k // P, P, n // P, P).transpose(2, 1, 0, 3).reshape(n // P, P, k)

    w_in, w_in2 = get["w_in"][0], get["w_in_2"][0]
    hq, hf, hi, hg, aq, ak, av = (blocks(w) for w in np.split(w_in, 7, axis=1))
    mkv = blocks(get["w_mem_kv_2"][0])
    mix = np.stack([hf, hq, hi, aq, ak, av, hg, mkv], axis=1).reshape(G_OUT, P, BW)
    up = blocks(get["w_up"][0])
    up = np.stack([up[:FT], up[FT:]], axis=1).reshape(2 * FT, P, BW)
    w_a = np.concatenate([mix, blocks(get["w_out"][0]), up])
    w_down = get["w_down"][0].reshape(4, DOWN_CELLS, P, KT, P).transpose(3, 0, 2, 1, 4).reshape(4 * KT, P, DOWN_CELLS * P)
    w_pe = blocks(get["w_pe"][0]).reshape(2, 8, P, 2, P).transpose(0, 2, 1, 3, 4).reshape(2, P, BW)
    c = GROUPS * P
    fw = HEADS * P
    at = np.cumsum([0, c, c, c, fw, fw, fw, HEADS, fw, c, c])
    cv_a, cv_b, cv_g, fq, fk, fv, fl, fg, mq, mg = (w_in2[:, a:b] for a, b in zip(at[:-1], at[1:]))
    conv = np.stack([blocks(cv_a), blocks(cv_b)], axis=1).reshape(2 * GROUPS, P, BW)
    fox = np.stack([blocks(fq), blocks(fk), blocks(fv), blocks(fg)], axis=1).reshape(4 * HEADS, P, BW)
    mem = np.stack([blocks(mq), blocks(mg)], axis=1).reshape(2 * MEM_HEADS, P, BW)
    pw = blocks(get["w_conv_pw_2"][0]).transpose(1, 0, 2).reshape(1, P, BW)
    w_b = np.concatenate([w_pe, blocks(get["w_pg"][0]), conv, fox, mem, blocks(cv_g), pw, blocks(get["w_out_2"][0])])
    wfg = np.ascontiguousarray(fl.reshape(KT, P, HEADS).transpose(1, 0, 2))

    cw = np.stack([vector(x) for x in (*get["conv_w"][0], get["conv_b"][0])], axis=2)
    cw = np.stack([cw[:, :FT], cw[:, FT:]], axis=2).reshape(P, 8 * FT)
    taps = np.stack([vector(x) for x in get["conv_w_2"][0]], axis=2).reshape(P, GROUPS * TAPS)
    vec = np.concatenate([
        vector(get["ln_mix_pre"]), vector(get["lb_logits"]), vector(get["hgrn_norm"]), vector(get["ln_mix_post"]),
        vector(get["ln_ffn_pre"]), cw, vector(get["ln_ffn_post"]), vector(get["norm_g_2"]), vector(get["mem_norm_g_2"]),
        taps, vector(get["conv_b_2"]), vector(get["conv_ln_g_2"]), vector(get["conv_ln_b_2"]), vector(get["final_g_2"])],
        axis=1)

    t, k = np.arange(T)[:, None], np.arange(T)[None, :]

    def tiles(m):
        return np.ascontiguousarray(np.concatenate([m[:P, :P], m[P:, :]], axis=1))

    dist = t - k
    count = sum(((dist >= 0) & (dist <= w) & (dist % d == 0)).astype(f32) for w, d in ((128, 1), (512, 4), (2048, 16)))
    one = np.arange(P)
    lmask = [one[:, None] == one[None, :]]
    for level in range(LEVELS - 1):
        b = one // 2 ** level
        lmask.append((b[:, None] % 2 == 0) & (b[None, :] == b[:, None] + 1))
    lmask = np.stack([np.concatenate([m, m], axis=1) for m in lmask], axis=1).astype(b16)

    arrays = {
        "xT": features(get["x"][0]), "memT": features(get["mem_2"][0]), "pT": features(get["p"][0, 0]),
        "w_a": w_a, "w_down": w_down, "w_b": w_b, "wfg": wfg, "bfox": get["b_f_2"].reshape(HEADS, 1), "vec": vec,
        "ident": np.eye(P, dtype=f32), "ones": np.ones((P, P), f32), "mult": tiles(count).astype(b16),
        "bias_att": tiles(np.where(count > 0, 0.0, MASKED)).astype(b16),
        "bias_fox": tiles(np.where(dist >= 0, 0.0, MASKED)).astype(b16), "lmask": lmask,
    }
    nc = bacc.Bacc("TRN2", target_bir_lowering=False, num_devices=1, dynamic_dma_scratch_size=1024)
    drams, sent = {}, {}
    for name, x in arrays.items():
        sent[f"in_{name}"] = np.ascontiguousarray(x)
        drams[name] = nc.dram_tensor(f"in_{name}", x.shape, mybir.dt.from_np(x.dtype), kind="ExternalInput").ap()
    out = nc.dram_tensor("out", (P, KT, T), F32, kind="ExternalOutput").ap()
    build(nc, drams, out)
    r = run_bass_kernel_spmd(nc, [sent], core_ids=[0])
    got = r.results[0]["out"]
    return np.ascontiguousarray(got.transpose(1, 0, 2).reshape(D, T).T).reshape(1, T, D)
```

```python
from contextlib import ExitStack

import numpy as np

import concourse.bass as bass
from concourse import mybir

F32 = mybir.dt.float32
F32R = mybir.dt.float32r
BF16 = mybir.dt.bfloat16
U8 = mybir.dt.uint8
ALU = mybir.AluOpType
ACT = mybir.ActivationFunctionType
AX_X = mybir.AxisListType.X

P = 128
T = 256
D = 2048
KT = D // P
HEADS = 8
MEM_HEADS = 4
GROUPS = 4
TAPS = 31
FF = 5632
FT = FF // P
DOWN_CELLS = 11
BW = KT * P
NS = 4
EPS = 1e-6
SCALE = float(P) ** -0.5
LEVELS = 8
PARTS = 3
FOX_ROWS = 2 * PARTS * HEADS
QUARTERS = 4
MASKED = -1e30
LARGE = 1e38

G_MIX, U_MIX = 0, 0
G_OUT, U_OUT = 62, 62
G_FILL, U_FILL = 78, 78
G_UP, U_UP = 80, 80
G_DOWN, U_DOWN = 168, 168
G_PE = 232
G_PG, U_PG = 234, 184
G_CONV, U_CONV = 250, 200
G_FOX, U_FOX = 258, 208
G_MEM, U_MEM = 290, 240
G_CG, U_CG = 298, 248
G_PW = 302
G_OUT2, U_OUT2 = 303, 252
N_BLOCKS = 319

V = {}


def _vector_columns():
    at = 0
    for name, n in (("ln_mix_pre", KT), ("lb", HEADS), ("hgrn_norm", HEADS), ("ln_mix_post", KT), ("ln_ffn_pre", KT),
                    ("conv", 4 * 2 * FT), ("ln_ffn_post", KT), ("norm_g_2", KT), ("mem_norm_g_2", KT),
                    ("taps", GROUPS * TAPS), ("conv_b_2", GROUPS), ("conv_ln_g", GROUPS), ("conv_ln_b", GROUPS),
                    ("final_g", KT)):
        V[name] = at
        at += n
    return at


N_VEC = _vector_columns()


class Chain:

    def __init__(self, eng, sem):
        self.eng, self.sem, self.base, self.j = eng, sem, 0, 0

    def link(self, ins):
        self.j += 1
        ins.then_inc(self.sem, 1)
        self.eng.wait_ge(self.sem, self.base + self.j)

    def enter(self, i, per):
        self.start, self.per = self.base + self.j, per
        self.base, self.j = self.start + i * per, 0

    def leave(self, n):
        assert self.j == self.per, f"{self.sem}: {self.j} steps in the loop's body, {self.per} stated"
        self.base, self.j = self.start + n * self.per, 0


def build(nc, a, out):
    with ExitStack() as ctx:
        def sem(name):
            return ctx.enter_context(nc.semaphore(name))

        at = [(nc.sbuf_base + 31) // 32 * 32]

        def sb(name, shape, dt=F32):
            size = int(np.prod(shape[1:])) * mybir.dt.size(dt)
            t = nc.alloc_sbuf_tensor_at(name, shape, dt, offset=at[0])
            at[0] += (size + 31) // 32 * 32
            return t

        def over(name, region_at, offset, shape, dt=F32):
            return nc.alloc_sbuf_tensor_at(name, shape, dt, offset=region_at + offset)

        stage_at = at[0]
        stage = sb("stage", [P, NS, BW])
        wlo = over("wlo", stage_at, 0, [P, NS, BW], F32R)
        whi = sb("whi", [P, NS, BW], F32R)
        h_at = at[0]
        h = sb("h", [P, KT, T])
        vec = sb("vec", [P, N_VEC])
        ident = sb("ident", [P, P])
        ones = sb("ones", [P, P])
        bfox = sb("bfox", [FOX_ROWS, 1])
        mkv = sb("mkv", [P, HEADS, T])
        small = sb("small", [P, 2, T])
        tmp = sb("tmp", [P, 2, T])
        rstd = sb("rstd", [P, T])
        acc = sb("acc", [P, T])
        cols = sb("cols", [P, 32])
        dummy = sb("dummy", [P, 2])
        conv_at = at[0]
        lmask = sb("lmask", [P, LEVELS, 2 * P], U8)
        mult = sb("mult", [P, 3 * P], BF16)
        bias_att = sb("bias_att", [P, 3 * P], BF16)
        upb = over("upb", conv_at, 0, [P, 2, T + 2])
        cy = over("cy", conv_at, 2080, [P, 2, T])
        gl = over("gl", conv_at, 4128, [P, T])
        at[0] = conv_at + 4128 + 1024
        a_at = at[0]
        act_a = sb("act_a", [P, KT, 2 * T], F32R)
        big_at = at[0]
        big = sb("big", [P, FT, 2 * T], F32R)
        KB = 1024

        mem_raw = over("mem_raw", big_at, 0, [P, KT, T])
        squares = over("squares", big_at, 64 * KB, [P, KT, T])
        xs_mix = big[:, 0:KT, :]
        xs_mem = big[:, KT:2 * KT, :]
        lmask_in = over("lmask_in", big_at, 80 * KB, [P, LEVELS, 2 * P], BF16)
        w1 = [64 * KB]

        def work1(name, shape):
            t = over(name, big_at, w1[0], shape)
            w1[0] += int(np.prod(shape[1:])) * 4
            assert w1[0] <= 86 * KB
            return t

        w0 = [0]

        def work0(name, shape):
            t = over(name, h_at, w0[0], shape)
            w0[0] += int(np.prod(shape[1:])) * 4
            assert w0[0] <= 16 * KB
            return t

        pfx = work1("pfx", [P, T])
        sfx = work1("sfx", [P, T])
        kk = work1("kk", [P, T])
        qq = work1("qq", [P, T])
        lev_in = work1("lev_in", [P, LEVELS, T])
        sT = work1("sT", [P, 3 * P])
        iT = work1("iT", [P, T])
        vtok = work1("vtok", [P, 2, P])
        aqT = work1("aqT", [P, T])
        akT = work1("akT", [P, T])
        avT = work1("avT", [P, T])
        avtok = work1("avtok", [P, 2, P])
        hfx = work0("hfx", [P, T])
        hqx = work0("hqx", [P, T])
        hgx = work0("hgx", [P, T])
        ef = work0("ef", [P, T])
        eq = work0("eq", [P, T])
        eg = work0("eg", [P, T])
        on1 = work0("on1", [P, T])
        osq = work0("osq", [P, T])
        osb = work0("osb", [P, T])
        var = work0("var", [P, T])
        sm = work0("sm", [P, 3 * P])
        pT = work0("pT", [P, 3 * P])
        mixed = over("mixed", big_at, 64 * KB, [P, KT, T])
        sq1 = over("sq1", big_at, 80 * KB, [P, T])
        rstd_mem = over("rstd_mem", big_at, 86 * KB, [P, T])
        mem_again = over("mem_again", a_at, 0, [P, KT, T])
        y = over("y", a_at, 0, [P, KT, T])
        p_raw = over("p_raw", a_at, 20 * KB, [P, 2, T])
        sq2 = over("sq2", a_at, 22 * KB, [P, T])
        xs_p = act_a[:, 8:10, :]
        xs_h = big[:, 0:KT, :]
        pe_out = over("pe_out", big_at, 32 * KB, [P, KT, T])
        pg_x = over("pg_x", big_at, 48 * KB, [P, 2, T])
        pg_s = over("pg_s", big_at, 50 * KB, [P, 2, T])
        xs_y = big[:, 0:KT, :]
        xs_cv = big[:, 40:44, :]
        w2 = [32 * KB]

        def work2(name, shape):
            t = over(name, big_at, w2[0], shape)
            w2[0] += (int(np.prod(shape[1:])) * 4 + 31) // 32 * 32
            assert w2[0] <= 80 * KB
            return t

        upad = work2("upad", [P, GROUPS, TAPS - 1 + T])
        uc = work2("uc", [P, GROUPS, T])
        usq = work2("usq", [P, GROUPS, T])
        cx = work2("cx", [P, 2, T])
        ce = work2("ce", [P, T])
        mu = work2("mu", [P, T])
        bias_fox = work2("bias_fox", [P, 3 * P // 2])[:, :].bitcast(BF16)
        wfg = work2("wfg", [P, KT, FOX_ROWS])
        sg_c = work2("sg_c", [P, GROUPS, T])
        fqT = work2("fqT", [P, T])
        fkT = work2("fkT", [P, T])
        fvT = work2("fvT", [P, T])
        fgx = work2("fgx", [P, T])
        fge = work2("fge", [P, T])
        fvtok = work2("fvtok", [P, 2, P])
        fs = work2("fs", [P, 4 * P])
        fpT = work2("fpT", [P, 4 * P])
        fo = work2("fo", [P, T])
        zf = work2("zf", [FOX_ROWS, T])
        z1 = work2("z1", [FOX_ROWS, T])
        z2 = work2("z2", [FOX_ROWS, T])
        one8 = work2("one8", [FOX_ROWS, T])
        fox_rows = work2("fox_rows", [FOX_ROWS, 2 * HEADS + 2 + PARTS])
        cc = work2("cc", [FOX_ROWS, T])
        cpos = work2("cpos", [FOX_ROWS, T // 2])[:, :].bitcast(BF16)
        cneg = work2("cneg", [FOX_ROWS, T // 2])[:, :].bitcast(BF16)
        cpart = [work2(f"cpart{n}", [FOX_ROWS, T // 2])[:, :].bitcast(BF16) for n in range(2)]
        sq4 = work2("sq4", [P, 2, T])
        sq3 = sq4[:, 0, :]
        h4 = over("h4", a_at, 0, [P, KT, T])
        o_out = over("o_out", a_at, 16 * KB, [P, KT, T])
        assert at[0] <= nc.sbuf_top, at[0] - nc.sbuf_top

        ps = ctx.enter_context(nc.psum_tensor("ps", [P, 2, 2 * T], F32))
        ps_lev = ctx.enter_context(nc.psum_tensor("ps_lev", [P, 2, 2, T], F32))
        ps_sc = ctx.enter_context(nc.psum_tensor("ps_sc", [P, 2 * T], F32))
        ps_t = ctx.enter_context(nc.psum_tensor("ps_t", [P, 2 * T], F32))
        bank_a = ctx.enter_context(nc.psum_tensor("bank_a", [P, 2 * T], F32))
        ps_a, ps_cross = bank_a[:, 0:T], bank_a[:, T:T + P]
        ps_b = ctx.enter_context(nc.psum_tensor("ps_b", [P, 2 * T], F32))[:, 0:T]

        whole_outputs = [ps_lev[:, 0, 0, :], ps_lev[:, 1, 0, :], ps_sc[:, 0:T], ps_t[:, 0:T]]

        S = {}

        def s(name):
            if name not in S:
                S[name] = sem(name)
            return S[name]

        once = {name: (kind, n + 1) for kind, names in (
            ("summed", ("x_summed", "mixed_summed", "mem_summed", "h1_summed", "y_summed", "h3_summed", "uc_summed",
                        "usq_summed", "h4_summed")),
            ("mean_square", ("x_ms", "mixed_ms", "mem_ms", "h1_ms", "y_ms", "h3_ms", "uc_ms", "h4_ms")),
            ("normed", ("x_norm", "mixed_norm", "mem_norm", "h1_norm", "y_norm", "h3_norm", "uc_norm", "h4_norm")),
            ("squares_added", ("x_sum", "mem_sum", "h1_sum", "uc_sum", "usq_sum")),
        ) for n, name in enumerate(names)}

        def event(name):
            kind, n = once[name]
            return s(kind), n

        steps = {name: (kind, n * count) for kind, count, names in (
            ("square_added", KT, ("mixed_acc", "y_acc", "h3_acc", "h4_acc")),
            ("gain_put", KT, ("mixed_gain", "y_gain", "h4_gain")),
            ("norm_put", QUARTERS - 1, ("mixed_scaled", "y_scaled")),
            ("residual_put", QUARTERS - 1, ("h1_ready", "h2_ready")),
            ("tile_high", KT, ("xs_x_hi", "xs_mem_hi", "xs_u_hi")),
        ) for n, name in enumerate(names)}

        def step(name, n):
            kind, before = steps[name]
            return s(kind), n + before

        w_landed = [sem(f"w_landed{i}") for i in range(NS)]
        w_hi, w_lo, w_used = sem("w_hi"), sem("w_lo"), sem("w_used")
        part_made, small_ready, out_free = sem("part_made"), sem("small_ready"), sem("out_free")
        vector_step, scalar_step, pool_step = sem("vector_step"), sem("scalar_step"), sem("pool_step")

        def wait(eng, name, n):
            if not (isinstance(n, int) and n == 0):
                eng.wait_ge(s(name), n)

        def output_made(eng, g, o, last, before):
            eng.wait_ge(*((w_used, g + 1) if o == last else (part_made, before + o + 1)))

        block = ctx.enter_context(nc.Block())

        def cells_of(c):
            return slice(c * BW // QUARTERS, (c + 1) * BW // QUARTERS)

        def x_landed(c):
            if c < QUARTERS - 1:
                return [(s(f"x_in{c}"), 2 * 16)]
            return [(s(f"x_in{c}"), 16), (w_landed[0], 16)]

        def first_done(part, c):
            return s("first_" + part) if c < QUARTERS - 1 else {"hi": w_hi, "lo": w_lo}[part]

        def first_count(part, g, c):
            return first_done(part, c), g + 1 if c == QUARTERS - 1 else g * (QUARTERS - 1) + c + 1

        def odd(t, m):
            names = " ".join("acd"[n] for n in range(len(t.shape) - 1))
            return t.rearrange(f"{names} (b two m) -> {names} b two m", two=2, m=m)[(slice(None),) * len(t.shape) + (1,)]

        def quarter(c):
            return slice(c * KT // QUARTERS, (c + 1) * KT // QUARTERS)

        def column(name, i, n=1):
            return vec[:, bass.ds(V[name] + i, n)]

        @block.sync
        def _(sp):
            def load(g, source, slot):
                if not (isinstance(g, int) and g < NS):
                    sp.wait_ge(w_used, g - (NS - 1))
                width = source.shape[-1]
                sp.dma_start(stage[:, slot, 0:width], source).then_inc(w_landed[slot], 16)

            def load_run(start, count, source):
                n = count // NS
                with sp.Fori(0, n) as i:
                    for j in range(NS):
                        load(start + i * NS + j, source[i * NS + j], (start + j) % NS)
                for j in range(n * NS, count):
                    load(start + j, source[j], (start + j) % NS)

            def constant(dst, name, done="consts_in"):
                full = tuple(slice(None) for _ in dst.shape)
                sp.dma_start(dst[full], a[name]).then_inc(s(done), 16)

            sp.dma_start(vec[:, 0:KT], a["vec"][:, 0:KT]).then_inc(s("vec_in"), 16)
            for c in range(QUARTERS):
                part = cells_of(c)
                sp.dma_start(stage[:, 0, part], a["w_a"][0][:, part])\
                    .then_inc(s(f"x_in{c}") if c < QUARTERS - 1 else w_landed[0], 16)
                sp.dma_start(h[:, quarter(c), :], a["xT"][:, quarter(c), :]).then_inc(s(f"x_in{c}"), 16)
            load(1, a["w_a"][1], 1)
            load(2, a["w_a"][2], 2)
            sp.dma_start(vec[:, KT:], a["vec"][:, KT:]).then_inc(s("consts_in"), 16)
            for dst, name in ((ident, "ident"), (ones, "ones"), (mult, "mult"), (bias_att, "bias_att"),
                              (lmask_in, "lmask"), (bfox, "bfox")):
                constant(dst, name)
            load(3, a["w_a"][3], 3)
            load(4, a["w_a"][4], 0)
            load(5, a["w_a"][5], 1)
            constant(mem_raw, "memT", "mem_in")
            load(6, a["w_a"][6], 2)
            load(7, a["w_a"][7], 3)
            load_run(2 * NS, G_OUT - 2 * NS, a["w_a"][2 * NS:G_OUT])
            load_run(G_OUT, NS, a["w_a"][G_OUT:G_OUT + NS])
            sp.wait_ge(s("mix_done"), HEADS)
            for c in range(2 * QUARTERS):
                load(G_OUT + NS + c, a["w_a"][G_OUT + NS + c], (G_OUT + NS + c) % NS)
                dst, src, done = (mem_again, "memT", "mem_back") if c < QUARTERS else (h, "xT", "x_back")
                q = quarter(c % QUARTERS)
                sp.dma_start(dst[:, q, :], a[src][:, q, :]).then_inc(s(done), 16)
            load_run(G_OUT + 3 * NS, G_DOWN - G_OUT - 3 * NS, a["w_a"][G_OUT + 3 * NS:G_DOWN])
            load_run(G_DOWN, 4, a["w_down"][0:4])
            sp.wait_ge(w_used, G_DOWN)
            sp.dma_start(p_raw[:, :, :], a["pT"]).then_inc(s("p_in"), 16)
            load_run(G_DOWN + 4, G_PE - G_DOWN - 4, a["w_down"][4:])
            load_run(G_PE, G_CONV + 4 - G_PE, a["w_b"])
            sp.wait_ge(s("h3_ready"), KT)
            sp.dma_start(bias_fox, a["bias_fox"]).then_inc(s("fox_in"), 16)
            sp.dma_start(wfg[:, :, :], a["wfg"]).then_inc(s("fox_in"), 16)
            sp.dma_start(fox_rows[:, :], a["fox_rows"]).then_inc(s("fox_in"), 16)
            load_run(G_CONV + 4, N_BLOCKS - G_CONV - 4, a["w_b"][G_CONV + 4 - G_PE:])
            for c in range(QUARTERS):
                sp.wait_ge(*(s("o_ready"), c + 1) if c < QUARTERS - 1 else (s("o_last"), 1))
                sp.dma_start(out[:, quarter(c), :], o_out[:, quarter(c), :]).then_inc(s("out_done"), 16)
            sp.wait_ge(s("out_done"), QUARTERS * 16)

        @block.scalar
        def _(act):
            chain = Chain(act, scalar_step)
            link = chain.link

            def hi(start, i, per, j, cells=KT):
                slot = (start + j) % NS
                act.wait_ge(w_landed[slot], i * (16 * per // NS) + 16 * ((start + j) // NS + 1))
                act.activation(whi[:, slot, 0:cells * P], stage[:, slot, 0:cells * P], ACT.Copy).then_inc(w_hi, 1)

            def evac(u, b, ahead=0):
                act.wait_ge(w_used, u + ahead + 1)
                act.wait_ge(out_free, u + 1)
                act.activation(small[:, b, :], ps[:, b, T:2 * T], ACT.Copy).then_inc(small_ready, 1)

            def inverse_root(t, waits, done):
                act.wait_ge(*waits)
                link(act.activation(t, t, ACT.Ln))
                act.activation(t, t, ACT.Exp, scale=-0.5).then_inc(done, 1)

            def norm(t, name):
                inverse_root(t, event(name + "_ms"), event(name + "_norm")[0])

            def split_hi(dst, src, done, scale=1.0):
                act.activation(dst, src, ACT.Copy, scale=scale).then_inc(step(done, 0)[0] if done in steps else s(done), 1)

            act.wait_ge(out_free, 2)
            act.activation(dummy[:, 1:2], dummy[:, 0:1], ACT.Copy)

            def hi_quarter(g, c):
                part = cells_of(c)
                act.activation(whi[:, g, part], stage[:, g, part], ACT.Copy).then_inc(first_done("hi", c), 1)

            act.wait_ge(s("vec_in"), 16)
            for c in range(QUARTERS):
                for done, n in x_landed(c):
                    act.wait_ge(done, n)
                hi_quarter(0, c)
                for k in range(KT)[quarter(c)]:
                    split_hi(act_a[:, k, 0:T], h[:, k, :], "xs_x_hi", column("ln_mix_pre", k))
            act.wait_ge(w_landed[1], 16)
            for c in range(QUARTERS):
                hi_quarter(1, c)
            evac(0, 0)
            hi(G_MIX, 0, 8, 2)
            hi(G_MIX, 0, 8, 3)
            evac(1, 1)
            hi(G_MIX, 0, 8, 4)
            norm(rstd[:, :], "x")
            evac(2, 0)

            def mem_hi(half):
                for k in range(half * KT // 2, (half + 1) * KT // 2):
                    split_hi(xs_mem[:, k, 0:T], mem_raw[:, k, :], "xs_mem_hi", column("mem_norm_g_2", k))

            def attention_turned(n):
                wait(act, "p_turned", n + 1)
                act.activation(pT[:, :], ps_t[:, 0:3 * P], ACT.Copy).then_inc(s("pT_ready"), 1)

            def attention_out(n):
                wait(act, "att_out", n + 1)
                act.activation(xs_mix[:, bass.ds(HEADS + n, 1), 0:T], ps_b.unsqueeze(1), ACT.Copy).then_inc(s("att_hi"), 1)

            def recurrence_out(n):
                wait(act, "o_done", n + 1)
                act.activation(xs_mix[:, bass.ds(n, 1), 0:T], osb[:, :].unsqueeze(1), ACT.Copy).then_inc(s("o_hi"), 1)

            def mixers_head(i, before=None, memory=True):
                first = before is None
                start, b = (G_MIX, 0) if first else (G_MIX - 1, 1)
                u = U_MIX + i * 8 - b
                if not first:
                    evac(u, b)
                    hi(start, i, 8, 3)
                wait(act, "hf_lin", i + 1)
                act.activation(ef[:, :], hfx[:, :], ACT.Exp, scale=-1.0).then_inc(s("hf_exp"), 1)
                if not first:
                    attention_turned(before)
                    evac(u + 1, 1 - b)
                    hi(start, i, 8, 4)
                wait(act, "hq_lin", i + 1)
                act.activation(eq[:, :], hqx[:, :], ACT.Exp, scale=-1.0).then_inc(s("hq_exp"), 1)
                if first:
                    evac(u + 3, 1 - b)
                    hi(start, i, 8, 5)
                else:
                    attention_out(before)
                    evac(u + 2, b)
                    hi(start, i, 8, 5)
                    inverse_root(var[:, :], (s("var_ready"), before + 1), s("o_norm"))
                    evac(u + 3, 1 - b)
                hi(start, i, 8, 6)
                if not first:
                    recurrence_out(before)
                evac(u + 4, b)
                hi(start, i, 8, 7)
                wait(act, "i_turned", i + 1)
                act.activation(vtok[:, :, :], ps_t[:, 0:T].rearrange("p (a b) -> p a b", a=2), ACT.Copy).then_inc(s("vtok_ready"), 1)
                if first:
                    act.wait_ge(s("consts_in"), 7 * 16)
                    act.wait_ge(s("mem_in"), 16)
                    mem_hi(0)
                evac(u + 5, 1 - b)
                hi(start, i, 8, 8)
                wait(act, "lev_ready", i * 5 + 5)
                act.activation(sT[:, P:2 * P], ps_cross, ACT.Copy).then_inc(s("cross_ready"), 1)
                wait(act, "att_max", i + 1)
                act.activation(sm[:, 0:P], sm[:, 0:P], ACT.Exp, bias=cols[:, 2:3]).then_inc(s("att_exp"), 1)
                act.activation(sm[:, P:3 * P], sm[:, P:3 * P], ACT.Exp, bias=cols[:, 3:4]).then_inc(s("att_exp"), 1)
                if first:
                    mem_hi(1)
                last = not first and not memory
                evac(u + 6, b)
                if not last:
                    hi(start, i, 8, 9)
                wait(act, "av_turned", i + 1)
                act.activation(avtok[:, :, :], ps_t[:, 0:T].rearrange("p (a b) -> p a b", a=2), ACT.Copy).then_inc(s("avtok_ready"), 1)
                wait(act, "hg_lin", i + 1)
                act.activation(eg[:, :], hgx[:, :], ACT.Exp, scale=-1.0).then_inc(s("hg_exp"), 1)
                if memory:
                    evac(u + 7, 1 - b)
                    hi(start, i, 8, 10)
                wait(act, "hg_out", i + 1)
                act.activation(osq[:, :], ps_a, ACT.Square).then_inc(s("osq_ready"), 1)
                if last:
                    hi(start, i, 8, 9)

            mixers_head(0, memory=False)
            with act.Fori(0, HEADS - 2) as n:
                chain.enter(n, 1)
                mixers_head(n + 1, n)
                chain.leave(HEADS - 2)
            mixers_head(HEADS - 1, HEADS - 2, memory=False)
            attention_turned(HEADS - 1)
            inverse_root(var[:, :], (s("var_ready"), HEADS), s("o_norm"))
            attention_out(HEADS - 1)
            recurrence_out(HEADS - 1)

            for j in range(4):
                evac(U_OUT + j, j % 2)
                hi(G_OUT, 0, 0, j + 3)
            with act.Fori(0, 3) as i:
                for j in range(4):
                    evac(U_OUT + 4 + 4 * i + j, j % 2)
                    hi(G_OUT + 4, i, 4, j + 3)
            norm(rstd[:, :], "mixed")
            evac(U_FILL, U_FILL % 2)
            hi(G_FILL, 0, 0, 3)
            def split_h1(c):
                act.wait_ge(*step("h1_ready", c) if c else (s("h1_first"), 1))
                for k in range(KT)[quarter(c)]:
                    split_hi(act_a[:, k, 0:T], h[:, k, :], "xs_u_hi", column("ln_ffn_pre", k))

            def square_h1(c):
                act.activation(mixed[:, quarter(c), :], h[:, quarter(c), :], ACT.Square).then_inc(s("h1_sq"), 1)

            split_h1(0)
            split_h1(1)
            evac(U_FILL + 1, 1)
            split_h1(2)
            square_h1(0)
            square_h1(1)
            split_h1(3)
            hi(G_FILL, 0, 0, 4)
            square_h1(2)
            square_h1(3)

            def first_tap(block, b):
                w = [vec[:, bass.ds(V["conv"] + 4 * block + c, 1)] for c in (2, 3)]
                act.wait_ge(s("up_ready"), block + 1)
                act.activation(cy[:, b, :], upb[:, b, 2:T + 2], ACT.Identity, scale=w[0], bias=w[1])\
                   .then_inc(s("tap_made"), 1)

            def split_gated(pair):
                act.wait_ge(s("gv_done"), pair + 1)
                act.activation(big[:, bass.ds(pair, 1), 0:T], cy[:, 1:2, :], ACT.Copy).then_inc(s("xs_g_hi"), 1)

            def mlp_pairs(i, first=False, last=False):
                for q in range(2):
                    u = U_UP + 4 * i + 2 * q
                    pair = 2 * i + q
                    if not (first and q):
                        evac(u, 0)
                    hi(G_UP, i, 4, 2 * q + 3, DOWN_CELLS if last and q else KT)
                    if first and not q:
                        evac(u + 1, 1)
                        norm(rstd[:, :], "h1")
                        first_tap(2 * pair, 0)
                        evac(u + 2, 0)
                        hi(G_UP, i, 4, 4)
                    else:
                        split_gated(pair - 1)
                        first_tap(2 * pair, 0)
                        evac(u + 1, 1)
                        hi(G_UP, i, 4, 2 * q + 4, DOWN_CELLS if last else KT)
                    first_tap(2 * pair + 1, 1)
                    act.wait_ge(s("gate_conv"), pair + 1)
                    act.activation(gl[:, :], cy[:, 0, :], ACT.Gelu_apprx_tanh).then_inc(s("gelu_done"), 1)

            norm(rstd_mem[:, :], "mem")
            mlp_pairs(0, first=True)
            with act.Fori(0, FT // 2 - 2) as n:
                mlp_pairs(n + 1)
            mlp_pairs(FT // 2 - 1, last=True)
            split_gated(FT - 1)

            def down_pair(i, last=False):
                for j in range(8):
                    if j % 4 == 3:
                        act.wait_ge(w_used, G_DOWN + 8 * i + j + 1)
                        act.wait_ge(out_free, U_DOWN + 2 * i + j // 4 + 1)
                        act.activation(small[:, j // 4, :], ps[:, j // 4, T:2 * T], ACT.Copy).then_inc(small_ready, 1)
                    if last and j == 7:
                        act.activation(dummy[:, 1:2], ones[:, 0:1], ACT.Ln)
                    hi(G_DOWN, i, 8, j + 3, KT if last and j + 3 >= 8 else DOWN_CELLS)

            with act.Fori(0, KT // 2 - 1) as i:
                down_pair(i)
            act.wait_ge(s("p_in"), 16)
            for k in range(2):
                split_hi(xs_p[:, k, 0:T], p_raw[:, k, :], "xs_p_hi")
            down_pair(KT // 2 - 1, last=True)

            def keep(outputs):
                for o in outputs:
                    output_made(act, G_PE + o // 8, o % 8, 7, o // 8 * 7)
                    act.activation(pe_out[:, o, :], whole_outputs[o % 4], ACT.Copy).then_inc(s("pe_kept"), 1)

            def split_h2(c):
                act.wait_ge(*step("h2_ready", c) if c else (s("h2_first"), 1))
                act.activation(xs_h[:, quarter(c), 0:T], h[:, quarter(c), :], ACT.Copy).then_inc(s("xs_h_hi"), 1)

            keep(range(3))
            norm(rstd[:, :], "y")
            keep(range(3, 7))
            hi(G_PE, 0, 0, 3)
            keep(range(7, 11))
            split_h2(0)
            keep(range(11, 13))
            split_h2(1)
            keep(range(13, 16))
            split_h2(2)
            split_h2(3)
            hi(G_PE, 0, 0, 4)

            act.activation(dummy[:, 0:1], rstd[:, 0:1], ACT.Sigmoid)
            def split_h3(k):
                act.wait_ge(s("h3_ready"), k + 1)
                act.activation(act_a[:, bass.ds(k, 1), 0:T], h[:, bass.ds(k, 1), :], ACT.Copy,
                               scale=column("norm_g_2", k)).then_inc(s("xs_n_hi"), 1)

            def gate_blocks(i, first=False):
                for j in range(4):
                    k = 4 * i + j
                    evac(U_PG + k, j % 2, G_PG - U_PG)
                    hi(G_PG, i, 4, j + 3)
                    act.wait_ge(out_free, U_PG + k + 3)
                    act.activation(pg_s[:, j % 2, :], pg_x[:, j % 2, :], ACT.Sigmoid).then_inc(s("pg_sig"), 1)
                    if j or not first:
                        split_h3(k - 1)

            gate_blocks(0, first=True)
            with act.Fori(0, 3) as n:
                gate_blocks(n + 1)
            split_h3(KT - 1)

            act.activation(dummy[:, 1:2], ones[:, 0:1], ACT.Ln)
            for n in range(GROUPS):
                u = U_CONV + 2 * n
                evac(u, 0, G_PG - U_PG)
                hi(G_CONV, 0, 0, 2 * n + 3)
                evac(u + 1, 1, G_PG - U_PG)
                if n == 0:
                    norm(rstd[:, :], "h3")
                else:
                    hi(G_CONV, 0, 0, 2 * n + 4)
                act.wait_ge(s("cv_lin"), n + 1)
                act.activation(ce[:, :], cx[:, 1, :], ACT.Sigmoid).then_inc(s("cv_sig"), 1)
                if n == 0:
                    hi(G_CONV, 0, 0, 4)
            act.wait_ge(s("z_abs"), 1)
            act.activation(z1[:, :], z1[:, :], ACT.Exp, scale=-1.0).then_inc(s("z_exp"), 1)
            act.wait_ge(s("z_exp"), 1)
            act.activation(z1[:, :], z1[:, :], ACT.Ln, bias=1.0).then_inc(s("z_ln"), 1)

            def fox_turned(n):
                wait(act, "fp_turned", n + 1)
                act.activation(fpT[:, 0:3 * P], ps_t[:, 0:3 * P], ACT.Copy).then_inc(s("fpT_ready"), 1)

            def fox_out(n):
                wait(act, "fo_done", n + 1)
                act.activation(xs_y[:, bass.ds(GROUPS + n, 1), 0:T], fo[:, :].unsqueeze(1), ACT.Copy).then_inc(s("fo_hi"), 1)

            def fox_head(i, before=None):
                u = U_FOX + 4 * i
                evac(u, 0, G_PG - U_PG)
                hi(G_FOX, i, 4, 3)
                if before is not None:
                    fox_turned(before)
                evac(u + 1, 1, G_PG - U_PG)
                hi(G_FOX, i, 4, 4)
                evac(u + 2, 0, G_PG - U_PG)
                hi(G_FOX, i, 4, 5)
                if before is not None:
                    fox_out(before)
                wait(act, "fox_max", i + 1)
                act.activation(fs[:, 0:P], fs[:, 0:P], ACT.Exp, bias=cols[:, 10:11], accum_out=cols[:, 12:13]).then_inc(s("fox_exp"), 1)
                act.activation(fs[:, P:3 * P], fs[:, P:3 * P], ACT.Exp, bias=cols[:, 11:12], accum_out=cols[:, 13:14]).then_inc(s("fox_exp"), 1)
                evac(u + 3, 1, G_PG - U_PG)
                hi(G_FOX, i, 4, 6)
                wait(act, "fg_lin", i + 1)
                act.activation(fge[:, :], fgx[:, :], ACT.Exp, scale=-1.0).then_inc(s("fg_exp"), 1)
                wait(act, "fv_turned", i + 1)
                act.activation(fvtok[:, :, :], ps_b.rearrange("p (a b) -> p a b", a=2), ACT.Copy).then_inc(s("fvtok_ready"), 1)

            fox_head(0)
            with act.Fori(0, HEADS - 1) as n:
                fox_head(n + 1, n)

            def memory_turned(n):
                act.wait_ge(s("mp_turned"), n + 1)
                act.activation(fpT[:, :], ps_t[:, :], ACT.Copy).then_inc(s("mpT_ready"), 1)

            def memory_out(n):
                act.wait_ge(s("mo_done"), n + 1)
                act.activation(xs_y[:, GROUPS + HEADS + n, 0:T], fo[:, :], ACT.Copy).then_inc(s("mo_hi"), 1)

            for n in range(MEM_HEADS):
                u = U_MEM + 2 * n
                evac(u, 0, G_PG - U_PG)
                hi(G_MEM, 0, 0, 2 * n + 3)
                memory_turned(n - 1) if n else fox_turned(HEADS - 1)
                if n == 2:
                    norm(mu[:, :], "uc")
                evac(u + 1, 1, G_PG - U_PG)
                hi(G_MEM, 0, 0, 2 * n + 4)
                memory_out(n - 1) if n else fox_out(HEADS - 1)
                act.wait_ge(s("mem_max"), n + 1)
                for t in range(2):
                    act.activation(fs[:, t * T:t * T + T], ps_sc[:, t * T:t * T + T], ACT.Exp, bias=cols[:, 20 + t:21 + t],
                                   accum_out=cols[:, 22 + t:23 + t]).then_inc(s("mem_exp"), 1)
                act.wait_ge(s("mg_lin"), n + 1)
                act.activation(fge[:, :], fgx[:, :], ACT.Exp, scale=-1.0).then_inc(s("mg_exp"), 1)
                act.wait_ge(s("mv_turned"), n + 1)
                act.activation(fvtok[:, :, :], ps_b.rearrange("p (a b) -> p a b", a=2), ACT.Copy).then_inc(s("mvtok_ready"), 1)

            act.wait_ge(s("cl_ready"), GROUPS)
            act.activation(usq[:, :, :], uc[:, :, :], ACT.Sigmoid).then_inc(s("cl_sig"), 1)
            for k in range(GROUPS):
                evac(U_CG + k, k % 2, G_CG - U_CG)
                hi(G_CG, 0, 0, k + 3)
                if k == 0:
                    memory_turned(MEM_HEADS - 1)
                    act.wait_ge(s("cs_ready"), 1)
                    act.activation(xs_cv[:, :, 0:T], uc[:, :, :], ACT.Copy).then_inc(s("xs_cv_hi"), 1)
                if k == 1:
                    memory_out(MEM_HEADS - 1)
                act.wait_ge(s("cg_lin"), k + 1)
                act.activation(usq[:, k, :], sg_c[:, k, :], ACT.Sigmoid).then_inc(s("cg_sig"), 1)
            for k in range(GROUPS):
                act.wait_ge(s("yc_ready"), k + 1)
                split_hi(xs_y[:, k, 0:T], usq[:, k, :], "xs_yc_hi")
            hi(G_PW, 0, 0, 3)

            with act.Fori(0, 3) as i:
                for j in range(4):
                    evac(U_OUT2 + 4 * i + j, j % 2, G_OUT2 - U_OUT2)
                    hi(G_OUT2, i, 4, j + 3)
            for j in range(4):
                evac(U_OUT2 + 12 + j, j % 2, G_OUT2 - U_OUT2)
                if j < 1:
                    hi(G_OUT2, 0, 0, 12 + j + 3)
            act.wait_ge(s("h4_ready"), KT)
            act.activation(sq4[:, 1, :], h4[:, KT - 1, :], ACT.Square).then_inc(s("h4_last_sq"), 1)
            norm(rstd[:, :], "h4")

        @block.vector
        def _(dve):
            chain = Chain(dve, vector_step)
            link = chain.link

            def lo(start, i, per, j, cells=KT):
                dve.wait_ge(w_hi, i * per + (start + j + 1))
                slot = (start + j) % NS
                part = slice(0, cells * P)
                dve.tensor_tensor(wlo[:, slot, part], stage[:, slot, part], whi[:, slot, part].bitcast(F32),
                                  ALU.subtract).then_inc(w_lo, 1)

            def add(u, b, dst=None):
                dve.wait_ge(small_ready, u + 1)
                dve.tensor_tensor(tmp[:, b, :] if dst is None else dst, ps[:, b, 0:T], small[:, b, :],
                                  ALU.add).then_inc(out_free, 1)

            def scaled(u, b, dst, done, by=None, factor=None):
                dve.wait_ge(out_free, u + 3)
                by = rstd[:, :] if by is None else by
                if factor is None:
                    dve.tensor_tensor(dst, tmp[:, b, :], by, ALU.mult).then_inc(s(done), 1)
                else:
                    dve.scalar_tensor_tensor(out=dst, in0=tmp[:, b, :], scalar=factor, in1=by,
                                             op0=ALU.mult, op1=ALU.mult).then_inc(s(done), 1)

            def logistic(e, exp_done, n):
                dve.wait_ge(s(exp_done), n)
                link(dve.tensor_scalar(e, e, LARGE, 1.0, ALU.min, ALU.add))
                link(dve.reciprocal(e, e))

            def mean_square(src, n, done):
                dve.tensor_scalar(n, src, 1.0 / D, EPS, ALU.mult, ALU.add).then_inc(event(done)[0], 1)

            dve.memset(dummy[:, :], 0.0).then_inc(out_free, 2)
            def lo_quarter(g, c):
                part = cells_of(c)
                dve.wait_ge(*first_count("hi", g, c))
                dve.tensor_tensor(wlo[:, g, part], stage[:, g, part], whi[:, g, part].bitcast(F32),
                                  ALU.subtract).then_inc(first_done("lo", c), 1)

            dve.wait_ge(s("vec_in"), 16)
            for c in range(QUARTERS):
                lo_quarter(0, c)
                for k in range(KT)[quarter(c)]:
                    dve.wait_ge(*step("xs_x_hi", k + 1))
                    dve.scalar_tensor_tensor(out=act_a[:, k, T:2 * T], in0=h[:, k, :], scalar=column("ln_mix_pre", k),
                                             in1=act_a[:, k, 0:T].bitcast(F32), op0=ALU.mult, op1=ALU.subtract)\
                       .then_inc(s("xs_x"), 1)
            for c in range(QUARTERS):
                lo_quarter(1, c)
            lo(G_MIX, 0, 8, 2)
            add(0, 0)
            dve.wait_ge(s("consts_in"), 7 * 16)
            lb, omlb, ex = cols[:, 16:24], cols[:, 24:32], cols[:, 8:16]
            link(dve.tensor_tensor(ex, column("lb", 0, HEADS), column("lb", 0, HEADS), ALU.subtract))
            link(dve.tensor_scalar(ex, ex, 1.0, None, ALU.add))
            link(dve.tensor_tensor(lb, ex, ex, ALU.subtract))
            link(dve.tensor_scalar(omlb, lb, -1.0, 1.0, ALU.mult, ALU.add))
            link(dve.tensor_copy(lmask[:, :, :], lmask_in[:, :, :]))
            lo(G_MIX, 0, 8, 3)
            dve.wait_ge(*event("x_summed"))
            mean_square(ps_a, rstd[:, :], "x_ms")
            add(1, 1)
            lo(G_MIX, 0, 8, 4)
            link(dve.memset(sT[:, :], 0.0))
            dve.wait_ge(*event("x_norm"))

            def mem_lo(half):
                for k in range(half * KT // 2, (half + 1) * KT // 2):
                    dve.wait_ge(*step("xs_mem_hi", k + 1))
                    dve.scalar_tensor_tensor(out=xs_mem[:, k, T:2 * T], in0=mem_raw[:, k, :],
                                             scalar=column("mem_norm_g_2", k), in1=xs_mem[:, k, 0:T].bitcast(F32),
                                             op0=ALU.mult, op1=ALU.subtract).then_inc(s("xs_mem"), 1)

            def recurrence_gated(n):
                wait(dve, "osq_ready", n + 1)
                link(dve.scalar_tensor_tensor(out=on1[:, :], in0=ps_a, scalar=column("hgrn_norm", n), in1=eg[:, :],
                                              op0=ALU.mult, op1=ALU.mult))
                wait(dve, "o_summed", n + 1)
                dve.tensor_scalar(var[:, :], ps_lev[:, 1, 0, :], 1.0 / P, EPS, ALU.mult, ALU.add).then_inc(s("var_ready"), 1)

            def attention_split(n):
                wait(dve, "att_hi", n + 1)
                dve.tensor_tensor(xs_mix[:, bass.ds(HEADS + n, 1), T:2 * T], ps_b.unsqueeze(1),
                                  xs_mix[:, bass.ds(HEADS + n, 1), 0:T].bitcast(F32), ALU.subtract).then_inc(s("att_split"), 1)

            def recurrence_normed(n):
                wait(dve, "o_norm", n + 1)
                dve.tensor_tensor(osb[:, :], on1[:, :], var[:, :], ALU.mult).then_inc(s("o_done"), 1)

            def recurrence_split(n):
                wait(dve, "o_hi", n + 1)
                dve.tensor_tensor(xs_mix[:, bass.ds(n, 1), T:2 * T], osb[:, :].unsqueeze(1),
                                  xs_mix[:, bass.ds(n, 1), 0:T].bitcast(F32), ALU.subtract).then_inc(s("mix_done"), 1)

            diag = sT[:, :].rearrange("p (c t) -> p c t", c=3)[:, 0:3:2, :]

            def place_levels(i, levels):
                for n in levels:
                    if n % 2 == 0:
                        wait(dve, "lev_ready", i * 5 + n // 2 + 1)
                    wait(dve, "lev_used", i * LEVELS + n)
                    dve.memset(dummy[:, 0:1], 0.0)
                    mask, made = lmask[:, n, :].rearrange("p (c t) -> p c t", c=2), ps_lev[:, n // 2 % 2, n % 2, :]
                    if n == 0:
                        dst, made = diag, made.rearrange("p (c t) -> p c t", c=2)
                    else:
                        m = 2 ** (n - 1)
                        dst, mask = odd(diag, m), odd(mask, m)
                        made = made[:, 0:P].rearrange("p (c b m) -> p c b m", c=2, m=m)
                    dve.copy_predicated(dst, mask, made).then_inc(s("lev_used"), 1)

            def mixers_head(i, before=None, memory=True):
                first = before is None
                start, b = (G_MIX, 0) if first else (G_MIX - 1, 1)
                u = U_MIX + i * 8 - b
                if first:
                    scaled(u, 0, hfx[:, :], "hf_lin")
                    dve.wait_ge(s("hf_lin"), 1)
                    add(u + 2, 0)
                    scaled(u + 1, 1, hqx[:, :], "hq_lin")
                else:
                    add(u, b)
                    scaled(u, b, hfx[:, :], "hf_lin")
                    lo(start, i, 8, 3)
                    recurrence_gated(before)
                logistic(ef[:, :], "hf_exp", i + 1)
                wait(dve, "lev_in_ready", i * LEVELS)
                wait(dve, "lev_ready", i * 5)
                link(dve.tensor_scalar(pfx[:, :], ef[:, :], cols[:, bass.ds(24 + i, 1)], cols[:, bass.ds(16 + i, 1)],
                                       ALU.mult, ALU.add))
                dve.tensor_scalar(kk[:, :], pfx[:, :], -1.0, 1.0, ALU.mult, ALU.add).then_inc(s("fk_ready"), 1)
                if not first:
                    add(u + 1, 1 - b)
                    scaled(u + 1, 1 - b, hqx[:, :], "hq_lin")
                    lo(start, i, 8, 4)
                if first:
                    dve.wait_ge(s("hq_lin"), 1)
                    add(u + 3, 1)
                logistic(eq[:, :], "hq_exp", i + 1)
                dve.tensor_tensor(qq[:, :], hqx[:, :], eq[:, :], ALU.mult).then_inc(s("q_ready"), 1)
                if not first:
                    attention_split(before)
                    add(u + 2, b)
                lo(start, i, 8, 5)
                scaled(u + 2, b, iT[:, :], "i_ready")
                if not first:
                    add(u + 3, 1 - b)
                lo(start, i, 8, 6)
                scaled(u + 3, 1 - b, aqT[:, :], "aq_ready", factor=SCALE)
                if not first:
                    recurrence_normed(before)
                if first:
                    dve.wait_ge(s("i_ready"), 1)
                add(u + 4, b)
                lo(start, i, 8, 7)
                scaled(u + 4, b, akT[:, :], "ak_ready")
                if not first:
                    recurrence_split(before)
                place_levels(i, range(4))
                if first:
                    mem_lo(0)
                add(u + 5, 1 - b)
                lo(start, i, 8, 8)
                scaled(u + 5, 1 - b, avT[:, :], "av_ready")
                wait(dve, "sc_ready", i + 1)
                wait(dve, "p_turned", i)
                link(dve.tensor_tensor(sm[:, :], ps_sc[:, 0:3 * P], bias_att[:, :], ALU.add))
                link(dve.tensor_reduce(cols[:, 0:1], sm[:, 0:P], AX_X, ALU.max))
                link(dve.tensor_reduce(cols[:, 1:2], sm[:, P:3 * P], AX_X, ALU.max))
                dve.tensor_scalar(cols[:, 2:4], cols[:, 0:2], -1.0, None, ALU.mult).then_inc(s("att_max"), 1)
                place_levels(i, range(4, LEVELS))
                if first:
                    mem_lo(1)
                add(u + 6, b)
                if memory:
                    lo(start, i, 8, 9)
                scaled(u + 6, b, hgx[:, :], "hg_lin")
                wait(dve, "att_exp", 2 * i + 2)
                link(dve.tensor_tensor(sm[:, :], sm[:, :], mult[:, :], ALU.mult))
                link(dve.tensor_reduce(cols[:, 4:5], sm[:, 0:P], AX_X, ALU.add))
                link(dve.tensor_reduce(cols[:, 5:6], sm[:, P:3 * P], AX_X, ALU.add))
                link(dve.reciprocal(cols[:, 6:8], cols[:, 4:6]))
                dve.tensor_scalar(sm[:, 0:P], sm[:, 0:P], cols[:, 6:7], None, ALU.mult).then_inc(s("p_ready"), 1)
                dve.tensor_scalar(sm[:, P:3 * P], sm[:, P:3 * P], cols[:, 7:8], None, ALU.mult).then_inc(s("p_ready"), 1)
                if first:
                    lo(start, i, 8, 9)
                if memory:
                    add(u + 7, 1 - b, dst=mkv[:, bass.ds(i, 1), :].squeeze(1))
                    lo(start, i, 8, 10)
                logistic(eg[:, :], "hg_exp", i + 1)
                link(dve.tensor_tensor(eg[:, :], eg[:, :], hgx[:, :], ALU.mult))

            mixers_head(0, memory=False)
            with dve.Fori(0, HEADS - 2) as n:
                chain.enter(n, 16)
                mixers_head(n + 1, n)
                chain.leave(HEADS - 2)
            mixers_head(HEADS - 1, HEADS - 2, memory=False)
            recurrence_gated(HEADS - 1)
            lo(G_MIX - 1, HEADS - 1, 8, 9)
            attention_split(HEADS - 1)
            recurrence_normed(HEADS - 1)
            recurrence_split(HEADS - 1)

            for j in range(4):
                add(U_OUT + j, j % 2, dst=mixed[:, j, :])
                lo(G_OUT, 0, 0, j + 3)
            with dve.Fori(0, 3) as i:
                for j in range(4):
                    add(U_OUT + 4 + 4 * i + j, j % 2, dst=mixed[:, bass.ds(4 + 4 * i + j, 1), :].squeeze(1))
                    lo(G_OUT + 4, i, 4, j + 3)
            dve.wait_ge(*event("mixed_summed"))
            mean_square(ps_a, rstd[:, :], "mixed_ms")
            dve.wait_ge(*step("mixed_gain", KT))
            dve.wait_ge(*event("mixed_norm"))
            by_norm = rstd[:, :].unsqueeze(1).to_broadcast([P, KT // QUARTERS, T])

            def normed(t, c, name):
                dve.tensor_tensor(t[:, quarter(c), :], t[:, quarter(c), :], by_norm, ALU.mult).then_inc(step(name, 0)[0], 1)

            def add_first(t, scaled, done):
                dve.wait_ge(*step(scaled, 1))
                dve.tensor_tensor(h[:, quarter(0), :], h[:, quarter(0), :], t[:, quarter(0), :], ALU.add).then_inc(s(done), 1)

            def split_h1(c):
                for k in range(KT)[quarter(c)]:
                    dve.wait_ge(*step("xs_u_hi", k + 1))
                    dve.scalar_tensor_tensor(out=act_a[:, k, T:2 * T], in0=h[:, k, :], scalar=column("ln_ffn_pre", k),
                                             in1=act_a[:, k, 0:T].bitcast(F32), op0=ALU.mult, op1=ALU.subtract)\
                       .then_inc(s("xs_u"), 1)

            add(U_FILL, 0, dst=mkv[:, 0, :])
            normed(mixed, 0, "mixed_scaled")
            dve.wait_ge(s("x_back"), QUARTERS * 16)
            add_first(mixed, "mixed_scaled", "h1_first")
            normed(mixed, 1, "mixed_scaled")
            normed(mixed, 2, "mixed_scaled")
            split_h1(0)
            split_h1(1)
            split_h1(2)
            lo(G_FILL, 0, 0, 3)
            split_h1(3)
            add(U_FILL + 1, 1, dst=mkv[:, HEADS - 1, :])
            lo(G_FILL, 0, 0, 4)
            dve.wait_ge(*event("mem_summed"))
            mean_square(ps_sc[:, 0:T], rstd_mem[:, :], "mem_ms")
            link(dve.memset(upb[:, :, 0:2], 0.0))

            def conv(block, b, done):
                w = [vec[:, bass.ds(V["conv"] + 4 * block + c, 1)] for c in range(2)]
                dve.wait_ge(s("tap_made"), block + 1)
                link(dve.scalar_tensor_tensor(out=cy[:, b, :], in0=upb[:, b, 1:T + 1], scalar=w[1], in1=cy[:, b, :],
                                              op0=ALU.mult, op1=ALU.add))
                dve.scalar_tensor_tensor(out=cy[:, b, :], in0=upb[:, b, 0:T], scalar=w[0], in1=cy[:, b, :],
                                         op0=ALU.mult, op1=ALU.add).then_inc(s(done), 1)

            def gate(pair):
                conv(2 * pair + 1, 1, "val_conv")
                dve.wait_ge(s("gelu_done"), pair + 1)
                dve.wait_ge(s("val_conv"), pair + 1)
                dve.tensor_tensor(cy[:, 1, :], cy[:, 1, :], gl[:, :], ALU.mult).then_inc(s("gv_done"), 1)

            def split_gated(pair):
                dve.wait_ge(s("xs_g_hi"), pair + 1)
                dve.tensor_tensor(big[:, bass.ds(pair, 1), T:2 * T], cy[:, 1:2, :],
                                  big[:, bass.ds(pair, 1), 0:T].bitcast(F32), ALU.subtract).then_inc(s("xs_g"), 1)

            def mlp_pairs(i, first=False, last=False):
                for q in range(2):
                    u = U_UP + 4 * i + 2 * q
                    pair = 2 * i + q
                    if not (first and q):
                        add(u, 0)
                    if first and not q:
                        lo(G_UP, i, 4, 3)
                        add(u + 1, 1)
                        dve.wait_ge(*event("h1_summed"))
                        mean_square(ps_b, rstd[:, :], "h1_ms")
                        conv(2 * pair, 0, "gate_conv")
                        add(u + 2, 0)
                        lo(G_UP, i, 4, 4)
                    else:
                        gate(pair - 1)
                        lo(G_UP, i, 4, 2 * q + 3, DOWN_CELLS if last and q else KT)
                        split_gated(pair - 1)
                        add(u + 1, 1)
                        conv(2 * pair, 0, "gate_conv")
                        lo(G_UP, i, 4, 2 * q + 4, DOWN_CELLS if last else KT)

            mlp_pairs(0, first=True)
            with dve.Fori(0, FT // 2 - 2) as n:
                chain.enter(n, 4)
                mlp_pairs(n + 1)
                chain.leave(FT // 2 - 2)
            mlp_pairs(FT // 2 - 1, last=True)
            gate(FT - 1)
            split_gated(FT - 1)

            def down_pair(i, last=False):
                for j in range(8):
                    if j % 4 == 3:
                        add(U_DOWN + 2 * i + j // 4, j // 4, dst=y[:, bass.ds(2 * i + j // 4, 1), :].squeeze(1))
                    if not (last and j >= 6):
                        lo(G_DOWN, i, 8, j + 3, KT if last and j + 3 >= 8 else DOWN_CELLS)

            with dve.Fori(0, KT // 2 - 1) as i:
                down_pair(i)
            for k in range(2):
                dve.wait_ge(s("xs_p_hi"), k + 1)
                dve.tensor_tensor(xs_p[:, k, T:2 * T], p_raw[:, k, :], xs_p[:, k, 0:T].bitcast(F32),
                                  ALU.subtract).then_inc(s("xs_p"), 1)
            down_pair(KT // 2 - 1, last=True)
            def split_h2(c):
                dve.wait_ge(s("xs_h_hi"), c + 1)
                dve.tensor_tensor(xs_h[:, quarter(c), T:2 * T], h[:, quarter(c), :],
                                  xs_h[:, quarter(c), 0:T].bitcast(F32), ALU.subtract).then_inc(s("xs_h"), 1)

            lo(G_PE, 0, 0, 1)
            dve.wait_ge(*event("y_summed"))
            mean_square(ps_a, rstd[:, :], "y_ms")
            lo(G_PE, 0, 0, 2)
            dve.wait_ge(*step("y_gain", KT))
            dve.wait_ge(*event("y_norm"))
            normed(y, 0, "y_scaled")
            normed(y, 1, "y_scaled")
            add_first(y, "y_scaled", "h2_first")
            normed(y, 2, "y_scaled")
            split_h2(0)
            lo(G_PE, 0, 0, 3)
            split_h2(1)
            split_h2(2)
            split_h2(3)
            lo(G_PE, 0, 0, 4)
            dve.wait_ge(s("pe_kept"), KT)

            def gated(k, b):
                dve.wait_ge(s("pg_sig"), k + 1)
                link(dve.tensor_tensor(pg_s[:, b:b + 1, :], pg_s[:, b:b + 1, :], pe_out[:, bass.ds(k, 1), :], ALU.mult))
                dve.tensor_tensor(h[:, bass.ds(k, 1), :], h[:, bass.ds(k, 1), :], pg_s[:, b:b + 1, :], ALU.add)\
                   .then_inc(s("h3_ready"), 1)

            def split_h3(k):
                dve.wait_ge(s("xs_n_hi"), k + 1)
                dve.scalar_tensor_tensor(out=act_a[:, bass.ds(k, 1), T:2 * T], in0=h[:, bass.ds(k, 1), :],
                                         scalar=column("norm_g_2", k), in1=act_a[:, bass.ds(k, 1), 0:T].bitcast(F32),
                                         op0=ALU.mult, op1=ALU.subtract).then_inc(s("xs_n"), 1)

            def gate_blocks(i, first=False):
                for j in range(4):
                    k = 4 * i + j
                    add(U_PG + k, j % 2, dst=pg_x[:, j % 2, :])
                    if j or not first:
                        gated(k - 1, (j - 1) % 2)
                    lo(G_PG, i, 4, j + 3)
                    if j or not first:
                        split_h3(k - 1)

            gate_blocks(0, first=True)
            with dve.Fori(0, 3) as n:
                chain.enter(n, 4)
                gate_blocks(n + 1)
                chain.leave(3)
            gated(KT - 1, 1)
            split_h3(KT - 1)
            link(dve.memset(upad[:, :, :], 0.0))
            link(dve.memset(one8[:, :], 1.0))
            for n in range(GROUPS):
                u = U_CONV + 2 * n
                add(u, 0)
                if n == 0:
                    dve.wait_ge(*event("h3_summed"))
                    mean_square(ps_b, rstd[:, :], "h3_ms")
                    lo(G_CONV, 0, 0, 3)
                    add(u + 1, 1)
                    dve.wait_ge(s("fox_in"), 3 * 16)
                    dve.tensor_tensor(wfg[:, :, :], wfg[:, :, :],
                                      column("norm_g_2", 0, KT).unsqueeze(2).to_broadcast([P, KT, FOX_ROWS]), ALU.mult).then_inc(s("wfg_ready"), 1)
                    dve.wait_ge(*event("h3_norm"))
                    scaled(u, 0, cx[:, 0, :], "ca_lin")
                    scaled(u + 1, 1, cx[:, 1, :], "cv_lin")
                    lo(G_CONV, 0, 0, 4)
                else:
                    lo(G_CONV, 0, 0, 2 * n + 3)
                    scaled(u, 0, cx[:, 0, :], "ca_lin")
                    add(u + 1, 1)
                    lo(G_CONV, 0, 0, 2 * n + 4)
                    scaled(u + 1, 1, cx[:, 1, :], "cv_lin")
                dve.wait_ge(s("cv_sig"), n + 1)
                dve.wait_ge(s("ca_lin"), n + 1)
                dve.tensor_tensor(upad[:, n, TAPS - 1:], cx[:, 0, :], ce[:, :], ALU.mult).then_inc(s("u_ready"), 1)

            dve.wait_ge(s("fl_ready"), 1)
            link(dve.tensor_tensor(zf[:, :], ps_t[0:FOX_ROWS, 0:T], rstd[0:FOX_ROWS, :], ALU.mult))
            link(dve.tensor_scalar(zf[:, :], zf[:, :], bfox[:, 0:1], None, ALU.add))
            link(dve.tensor_scalar(z1[:, :], zf[:, :], -1.0, None, ALU.mult))
            dve.tensor_tensor(z1[:, :], zf[:, :], z1[:, :], ALU.max).then_inc(s("z_abs"), 1)
            link(dve.tensor_scalar(zf[:, :], zf[:, :], 0.0, None, ALU.min))
            dve.wait_ge(s("z_ln"), 1)
            link(dve.tensor_tensor(z2[:, :], zf[:, :], z1[:, :], ALU.subtract))
            link(dve.tensor_tensor_scan(cc[:, :], one8[:, :], z2[:, :], 0.0, ALU.mult, ALU.add))
            for n, (whole_c, left) in enumerate(((cc, z1), (z1, z2))):
                link(dve.tensor_copy(cpart[n], whole_c[:, :]))
                link(dve.tensor_tensor(left[:, :], whole_c[:, :], cpart[n], ALU.subtract))
            keeps = [fox_rows[:, 2 * HEADS + 2 + n:2 * HEADS + 3 + n] for n in range(PARTS)]
            link(dve.tensor_scalar(cc[:, :], z2[:, :], keeps[2], None, ALU.mult))
            for n in range(2):
                link(dve.scalar_tensor_tensor(out=cc[:, :], in0=cpart[n], scalar=keeps[n], in1=cc[:, :],
                                              op0=ALU.mult, op1=ALU.add))

            def fox_gated(n):
                wait(dve, "fo_ready", n + 1)
                dve.tensor_tensor(fo[:, :], ps_a, fge[:, :], ALU.mult).then_inc(s("fo_done"), 1)

            def fox_split(n):
                wait(dve, "fo_hi", n + 1)
                dve.tensor_tensor(xs_y[:, bass.ds(GROUPS + n, 1), T:2 * T], fo[:, :].unsqueeze(1),
                                  xs_y[:, bass.ds(GROUPS + n, 1), 0:T].bitcast(F32), ALU.subtract).then_inc(s("fo_split"), 1)

            def fox_head(i, before=None):
                u = U_FOX + 4 * i
                add(u, 0)
                lo(G_FOX, i, 4, 3)
                wait(dve, "fsc_ready", i)
                scaled(u, 0, fqT[:, :], "fq_ready", factor=SCALE)
                for n, t in enumerate((cpos, cneg)):
                    dve.tensor_scalar(t, cc[:, :], fox_rows[:, bass.ds(i + n * HEADS, 1)],
                                      fox_rows[:, 2 * HEADS + n:2 * HEADS + n + 1], ALU.mult, ALU.add).then_inc(s("c_ready"), 1)
                add(u + 1, 1)
                lo(G_FOX, i, 4, 4)
                scaled(u + 1, 1, fkT[:, :], "fk2_ready")
                add(u + 2, 0)
                lo(G_FOX, i, 4, 5)
                scaled(u + 2, 0, fvT[:, :], "fv_ready")
                if before is not None:
                    fox_gated(before)
                wait(dve, "fsc_ready", i + 1)
                wait(dve, "fp_turned", i)
                link(dve.tensor_tensor(fs[:, 0:3 * P], ps_sc[:, 0:3 * P], bias_fox, ALU.add))
                link(dve.tensor_reduce(cols[:, 8:9], fs[:, 0:P], AX_X, ALU.max))
                link(dve.tensor_reduce(cols[:, 9:10], fs[:, P:3 * P], AX_X, ALU.max))
                dve.tensor_scalar(cols[:, 10:12], cols[:, 8:10], -1.0, None, ALU.mult).then_inc(s("fox_max"), 1)
                if before is not None:
                    fox_split(before)
                add(u + 3, 1)
                wait(dve, "fox_exp", 2 * i + 2)
                link(dve.reciprocal(cols[:, 14:16], cols[:, 12:14]))
                dve.tensor_scalar(fs[:, 0:P], fs[:, 0:P], cols[:, 14:15], None, ALU.mult).then_inc(s("fp_ready"), 1)
                dve.tensor_scalar(fs[:, P:3 * P], fs[:, P:3 * P], cols[:, 15:16], None, ALU.mult).then_inc(s("fp_ready"), 1)
                lo(G_FOX, i, 4, 6)
                scaled(u + 3, 1, fgx[:, :], "fg_lin")
                logistic(fge[:, :], "fg_exp", i + 1)
                link(dve.tensor_tensor(fge[:, :], fge[:, :], fgx[:, :], ALU.mult))

            fox_head(0)
            with dve.Fori(0, HEADS - 1) as n:
                chain.enter(n, 7)
                fox_head(n + 1, n)
                chain.leave(HEADS - 1)

            uc_mean = ps_lev[:, 0, 0, :]
            uc_square = ps_lev[:, 1, 0, :]
            by_mean = mu[:, :].unsqueeze(1).to_broadcast([P, GROUPS, T])

            def memory_gated(n):
                dve.wait_ge(s("mo_ready"), n + 1)
                dve.tensor_tensor(fo[:, :], ps_a, fge[:, :], ALU.mult).then_inc(s("mo_done"), 1)

            def memory_split(n):
                dve.wait_ge(s("mo_hi"), n + 1)
                dve.tensor_tensor(xs_y[:, GROUPS + HEADS + n, T:2 * T], fo[:, :],
                                  xs_y[:, GROUPS + HEADS + n, 0:T].bitcast(F32), ALU.subtract).then_inc(s("mo_split"), 1)

            for n in range(MEM_HEADS):
                u = U_MEM + 2 * n
                if n == 2:
                    dve.wait_ge(*event("usq_summed"))
                    dve.tensor_scalar(mu[:, :], uc_square, 1.0 / (GROUPS * P), EPS, ALU.mult, ALU.add).then_inc(event("uc_ms")[0], 1)
                add(u, 0)
                scaled(u, 0, fqT[:, :], "mq_ready", factor=SCALE)
                lo(G_MEM, 0, 0, 2 * n + 3)
                if n == 3:
                    dve.wait_ge(*event("uc_norm"))
                    link(dve.tensor_tensor(uc[:, :, :], uc[:, :, :], by_mean, ALU.mult))
                    for k in range(GROUPS):
                        dve.tensor_scalar(uc[:, k, :], uc[:, k, :], column("conv_ln_g", k), column("conv_ln_b", k),
                                          ALU.mult, ALU.add).then_inc(s("cl_ready"), 1)
                add(u + 1, 1)
                memory_gated(n - 1) if n else fox_gated(HEADS - 1)
                dve.wait_ge(s("msc_ready"), n + 1)
                link(dve.tensor_reduce(cols[:, 18:20], ps_sc[:, :].rearrange("p (c t) -> p c t", c=2), AX_X, ALU.max))
                dve.tensor_scalar(cols[:, 20:22], cols[:, 18:20], -1.0, None, ALU.mult).then_inc(s("mem_max"), 1)
                scaled(u + 1, 1, fgx[:, :], "mg_lin")
                lo(G_MEM, 0, 0, 2 * n + 4)
                memory_split(n - 1) if n else fox_split(HEADS - 1)
                dve.wait_ge(s("mem_exp"), 2 * n + 2)
                link(dve.reciprocal(cols[:, 24:26], cols[:, 22:24]))
                for t in range(2):
                    dve.tensor_scalar(fs[:, t * T:t * T + T], fs[:, t * T:t * T + T], cols[:, 24 + t:25 + t], None,
                                      ALU.mult).then_inc(s("mp_ready"), 1)
                logistic(fge[:, :], "mg_exp", n + 1)
                link(dve.tensor_tensor(fge[:, :], fge[:, :], fgx[:, :], ALU.mult))
                if n == 0:
                    dve.wait_ge(*event("uc_summed"))
                    link(dve.tensor_scalar(mu[:, :], uc_mean, 1.0 / (GROUPS * P), None, ALU.mult))
                    link(dve.tensor_tensor(uc[:, :, :], uc[:, :, :], by_mean, ALU.subtract))
                    dve.tensor_tensor(usq[:, :, :], uc[:, :, :], uc[:, :, :], ALU.mult).then_inc(s("usq_ready"), 1)
            dve.wait_ge(s("cl_sig"), 1)
            dve.tensor_tensor(uc[:, :, :], uc[:, :, :], usq[:, :, :], ALU.mult).then_inc(s("cs_ready"), 1)

            for k in range(GROUPS):
                add(U_CG + k, k % 2)
                scaled(U_CG + k, k % 2, sg_c[:, k, :], "cg_lin")
                lo(G_CG, 0, 0, k + 3)
                if k == 1:
                    memory_gated(MEM_HEADS - 1)
                    dve.wait_ge(s("xs_cv_hi"), 1)
                    dve.tensor_tensor(xs_cv[:, :, T:2 * T], uc[:, :, :], xs_cv[:, :, 0:T].bitcast(F32),
                                      ALU.subtract).then_inc(s("xs_cv"), 1)
                if k == 1:
                    memory_split(MEM_HEADS - 1)
                dve.wait_ge(s("cg_sig"), k + 1)
                link(dve.tensor_tensor(sg_c[:, k, :], sg_c[:, k, :], usq[:, k, :], ALU.mult))
            for k in range(GROUPS + 1):
                if k < GROUPS:
                    output_made(dve, G_PW, k, GROUPS - 1, 14)
                    dve.tensor_tensor(usq[:, k, :], whole_outputs[k], sg_c[:, k, :], ALU.mult).then_inc(s("yc_ready"), 1)
                if k:
                    dve.wait_ge(s("xs_yc_hi"), k)
                    dve.tensor_tensor(xs_y[:, k - 1, T:2 * T], usq[:, k - 1, :], xs_y[:, k - 1, 0:T].bitcast(F32),
                                      ALU.subtract).then_inc(s("xs_yc"), 1)
            lo(G_PW, 0, 0, 3)

            def out2(i, j, ahead):
                u = U_OUT2 + 4 * i + j
                add(u, j % 2)
                if ahead:
                    lo(G_OUT2, i, 4, j + 3)
                dve.wait_ge(out_free, u + 3)
                k = 4 * i + j
                dve.tensor_tensor(h4[:, bass.ds(k, 1), :], tmp[:, j % 2:j % 2 + 1, :], h[:, bass.ds(k, 1), :],
                                  ALU.add).then_inc(s("h4_ready"), 1)

            with dve.Fori(0, 3) as i:
                for j in range(4):
                    out2(i, j, True)
            for j in range(4):
                out2(3, j, j < 1)
            dve.wait_ge(*event("h4_summed"))
            mean_square(ps_a, rstd[:, :], "h4_ms")
            dve.wait_ge(*event("h4_norm"))
            dve.wait_ge(*step("h4_gain", KT - 1))
            for c in range(QUARTERS - 1):
                dve.tensor_tensor(o_out[:, quarter(c), :], h4[:, quarter(c), :], by_norm, ALU.mult).then_inc(s("o_ready"), 1)

        @block.gpsimd
        def _(pool):
            chain = Chain(pool, pool_step)
            link = chain.link

            def halve(t, n, dst, done):
                while n > 2:
                    n //= 2
                    link(pool.tensor_tensor(t[:, 0:n, :], t[:, 0:n, :], t[:, n:2 * n, :], ALU.add))
                pool.tensor_tensor(dst, t[:, 0, :], t[:, 1, :], ALU.add).then_inc(event(done)[0], 1)

            for c in range(QUARTERS):
                for done, n in x_landed(c):
                    pool.wait_ge(done, n)
                link(pool.tensor_tensor(squares[:, quarter(c), :], h[:, quarter(c), :], h[:, quarter(c), :], ALU.mult))
            halve(squares, KT, acc[:, :], "x_sum")

            def decays(i):
                wait(pool, "fk_ready", i + 1)
                wait(pool, "q_ready", i + 1)
                wait(pool, "lev_ready", i * 5)
                for L in range(LEVELS):
                    m = 2 ** L

                    def halves(t):
                        v = t.rearrange("p (b two m) -> p b two m", two=2, m=m)
                        return v[:, :, 0, :], v[:, :, 1, :]

                    shape = [P, T // (2 * m), m]
                    (x0, x1), (p0, p1), (s0, s1) = halves(lev_in[:, L, :]), halves(pfx[:, :]), halves(sfx[:, :])
                    (k0, _), (_, q1) = halves(kk[:, :]), halves(qq[:, :])
                    link(pool.tensor_tensor(x1, q1, p1, ALU.mult))
                    if L == 0:
                        both = ones[:, :].unsqueeze(1).to_broadcast([P, 2, P])
                        link(pool.tensor_tensor(sfx[:, :].rearrange("p (a b) -> p a b", a=2), both, both, ALU.mult))
                    pool.tensor_tensor(x0, k0, s0, ALU.mult).then_inc(s("lev_in_ready"), 1)
                    if L < LEVELS - 1:
                        pool.wait_ge(s("lev_in_ready"), i * LEVELS + L + 1)
                        link(pool.tensor_tensor(s0, s0, p1[:, :, m - 1:m].to_broadcast(shape), ALU.mult))
                        link(pool.tensor_tensor(p1, p1, p0[:, :, m - 1:m].to_broadcast(shape), ALU.mult))

            decays(0)
            with pool.Fori(0, HEADS - 1) as n:
                chain.enter(n, 23)
                decays(n + 1)
                chain.leave(HEADS - 1)

            def squares_and_gain(count, tile, sq, ready, done, gain):
                link(pool.memset(acc[:, :], 0.0))
                total = acc[:, :].unsqueeze(1)
                with pool.Fori(0, count) as i:
                    chain.enter(i, 1)
                    ready(i)
                    link(pool.tensor_tensor(sq, tile(i), tile(i), ALU.mult))
                    pool.tensor_tensor(total, total, sq, ALU.add).then_inc(step(done + "_acc", 0)[0], 1)
                    if gain is not None:
                        g = column(gain, i).unsqueeze(2).to_broadcast([P, 1, T])
                        pool.tensor_tensor(tile(i), tile(i), g, ALU.mult).then_inc(step(done + "_gain", 0)[0], 1)
                    pool.wait_ge(*step(done + "_acc", i + 1))
                    chain.leave(count)

            pool.wait_ge(s("mem_back"), QUARTERS * 16)
            link(pool.tensor_tensor(mem_again[:, :, :], mem_again[:, :, :], mem_again[:, :, :], ALU.mult))
            halve(mem_again, KT, rstd_mem[:, :], "mem_sum")
            squares_and_gain(KT, lambda i: mixed[:, bass.ds(i, 1), :], sq1[:, :].unsqueeze(1),
                             lambda i: pool.wait_ge(out_free, U_OUT + i + 3), "mixed", "ln_mix_post")
            def residual(t, name):
                by_norm = rstd[:, :].unsqueeze(1).to_broadcast([P, KT // QUARTERS, T])
                last = quarter(QUARTERS - 1)
                pool.wait_ge(*step(name + "_gain", KT))
                link(pool.tensor_tensor(t[:, last, :], t[:, last, :], by_norm, ALU.mult))
                for c in range(1, QUARTERS):
                    if c < QUARTERS - 1:
                        pool.wait_ge(*step(name + "_scaled", c + 1))
                    pool.tensor_tensor(h[:, quarter(c), :], h[:, quarter(c), :], t[:, quarter(c), :], ALU.add)\
                        .then_inc(step({"mixed": "h1", "y": "h2"}[name] + "_ready", 0)[0], 1)

            pool.wait_ge(*event("mixed_norm"))
            pool.wait_ge(s("x_back"), QUARTERS * 16)
            residual(mixed, "mixed")
            for c in range(1, QUARTERS):
                pool.wait_ge(s("h1_sq"), c + 1)
                link(pool.tensor_tensor(mixed[:, quarter(0), :], mixed[:, quarter(0), :], mixed[:, quarter(c), :], ALU.add))
            halve(mixed, KT // QUARTERS, acc[:, :], "h1_sum")
            pool.wait_ge(*event("h1_norm"))
            def token_norm(i):
                for q in range(4):
                    n = 4 * i + q
                    pool.wait_ge(out_free, U_UP + n + 3)
                    wait(pool, "gate_conv" if q % 2 == 0 else "val_conv", 2 * i + q // 2)
                    pool.tensor_tensor(upb[:, q % 2, 2:T + 2], tmp[:, q % 2, :], rstd[:, :], ALU.mult).then_inc(s("up_ready"), 1)

            token_norm(0)
            pool.wait_ge(*event("mem_norm"))
            pool.tensor_tensor(mkv[:, :, :], mkv[:, :, :], rstd_mem[:, :].unsqueeze(1).to_broadcast([P, HEADS, T]),
                               ALU.mult).then_inc(s("mkv_ready"), 1)
            with pool.Fori(0, FT // 2 - 1) as n:
                token_norm(n + 1)
            squares_and_gain(KT, lambda i: y[:, bass.ds(i, 1), :], sq2[:, :].unsqueeze(1),
                             lambda i: pool.wait_ge(out_free, U_DOWN + i + 3), "y", "ln_ffn_post")
            pool.wait_ge(*event("y_norm"))
            residual(y, "y")
            squares_and_gain(KT, lambda i: h[:, bass.ds(i, 1), :], sq3.unsqueeze(1),
                             lambda i: pool.wait_ge(s("h3_ready"), i + 1), "h3", None)

            pool.wait_ge(s("u_ready"), GROUPS)
            taps = vec[:, V["taps"]:V["taps"] + GROUPS * TAPS].rearrange("p (k t) -> p k t", k=GROUPS)
            every = [P, GROUPS, T]

            def tap_product(dst, tap):
                return pool.tensor_tensor(dst, upad[:, :, bass.ds(tap, T)],
                                          taps[:, :, bass.ds(tap, 1)].to_broadcast(every), ALU.mult)

            tap_product(uc[:, :, :], 0).then_inc(s("tap_done"), 1)
            pool.wait_ge(s("tap_done"), 1)
            pool.tensor_tensor(uc[:, :, :], uc[:, :, :], column("conv_b_2", 0, GROUPS).unsqueeze(2).to_broadcast(every),
                               ALU.add).then_inc(s("tap_done"), 1)
            with pool.Fori(0, (TAPS - 1) // 2) as i:
                chain.enter(i, 2)
                for j, made in enumerate((usq, sg_c)):
                    pool.wait_ge(s("tap_done"), 2 * i + j + 1)
                    link(tap_product(made[:, :, :], 2 * i + j + 1))
                    pool.wait_ge(s("tap_done"), 2 * i + j + 2)
                    pool.tensor_tensor(uc[:, :, :], uc[:, :, :], made[:, :, :], ALU.add).then_inc(s("tap_done"), 1)
                chain.leave((TAPS - 1) // 2)
            pool.wait_ge(s("tap_done"), TAPS + 1)
            link(pool.tensor_tensor(sg_c[:, 0:2, :], uc[:, 0:2, :], uc[:, 2:4, :], ALU.add))
            pool.tensor_tensor(sg_c[:, 2, :], sg_c[:, 0, :], sg_c[:, 1, :], ALU.add).then_inc(event("uc_sum")[0], 1)
            pool.wait_ge(s("usq_ready"), 1)
            link(pool.tensor_tensor(usq[:, 0:2, :], usq[:, 0:2, :], usq[:, 2:4, :], ALU.add))
            pool.tensor_tensor(usq[:, 0, :], usq[:, 0, :], usq[:, 1, :], ALU.add).then_inc(event("usq_sum")[0], 1)
            pool.wait_ge(*event("h3_ms"))
            squares_and_gain(KT - 1, lambda i: h4[:, bass.ds(i, 1), :], sq4[:, 0:1, :],
                             lambda i: pool.wait_ge(s("h4_ready"), i + 1), "h4", "final_g")
            pool.wait_ge(s("h4_last_sq"), 1)
            link(pool.tensor_tensor(h4[:, KT - 1, :], h4[:, KT - 1, :],
                                    column("final_g", KT - 1).to_broadcast([P, T]), ALU.mult))
            pool.wait_ge(*step("h4_gain", KT - 1))
            pool.wait_ge(*event("h4_norm"))
            by_norm = rstd[:, :].unsqueeze(1).to_broadcast([P, KT // QUARTERS, T])
            last = quarter(QUARTERS - 1)
            pool.tensor_tensor(o_out[:, last, :], h4[:, last, :], by_norm, ALU.mult).then_inc(s("o_last"), 1)

        @block.tensor
        def _(pe):
            def product(slot, c, act, bank, start, stop):
                pe.matmul(ps[:, bank, :], whi[:, slot, c * P:(c + 1) * P], act, start=start, stop=False)
                return pe.matmul(ps[:, bank, T:2 * T], wlo[:, slot, c * P:(c + 1) * P], act[:, 0:T],
                                 start=False, stop=stop)

            def cells(slot, bank, xs, order, opens=True, closes=True, ready=None):
                for n, c in enumerate(order):
                    if ready is not None:
                        ready(c)
                    ins = product(slot, c, xs[:, c, :], bank, opens and n == 0, closes and n == len(order) - 1)
                return ins

            def await_block(start, i, per, j, u):
                pe.wait_ge(w_lo, i * per + (start + j + 1))
                pe.wait_ge(out_free, u + 1)

            def whole(start, i, per, j, u, bank, xs, order=tuple(range(KT)), ready=None):
                await_block(start, i, per, j, u)
                cells((start + j) % NS, bank, xs, order, ready=ready).then_inc(w_used, 1)

            def column_sums(dst, srcs, waits, done):
                for n, src in enumerate(srcs):
                    pe.wait_ge(*waits(n))
                    ins = pe.matmul(dst, ones[:, :], src, start=n == 0, stop=n == len(srcs) - 1)
                ins.then_inc(event(done)[0], 1)

            def turn(dst, src, done, inc=1):
                ins = pe.transpose(dst, src, ident[:, :])
                if inc:
                    ins.then_inc(s(done), 1)

            def masked_scores(q, k, terms):
                for t, (c0, c1) in enumerate(((0, P), (P, 3 * P))):
                    rows, n = slice(t * P, t * P + P), c1 - c0
                    for m, (l, r) in enumerate(terms(rows, n)):
                        pe.matmul(ps_sc[:, c0:c1], l, r, start=m == 0, stop=False)
                    ins = pe.matmul(ps_sc[:, c0:c1], q[:, rows], k[:, 0:n], start=not terms(rows, n), stop=True)
                return ins

            def weighted(dst, v, pt):
                pe.matmul(dst, v[:, 0, :], pt[:, 0:T], start=True, stop=False)
                return pe.matmul(dst[:, P:T], v[:, 1, :], pt[:, T:3 * P], start=False, stop=True)

            def recurrence_summed(n):
                wait(pe, "osq_ready", n + 1)
                wait(pe, "lev_used", (n + 1) * LEVELS)
                pe.matmul(ps_lev[:, 1, 0, :], ones[:, :], osq[:, :], start=True, stop=True).then_inc(s("o_summed"), 1)

            def attention_turned(n):
                wait(pe, "p_ready", 2 * n + 2)
                wait(pe, "avtok_ready", n + 1)
                for c in range(3):
                    turn(ps_t[:, c * P:(c + 1) * P], sm[:, c * P:(c + 1) * P], "p_turned", c == 2)

            def attention_out(n):
                wait(pe, "pT_ready", n + 1)
                weighted(ps_b, avtok, pT).then_inc(s("att_out"), 1)

            def levels(i, which):
                for n in which:
                    if 4 <= n < LEVELS and n % 2 == 0:
                        wait(pe, "lev_used", i * LEVELS + n - 2)
                    if n:
                        wait(pe, "lev_in_ready", i * LEVELS + n)
                    keys, queries = (kk, qq) if n == 0 else (lev_in[:, n - 1, :],) * 2
                    if n < LEVELS:
                        width = P if n == 0 else P // 2
                        for c in range(2):
                            tile = slice(c * P, c * P + P)
                            ins = pe.matmul(ps_lev[:, n // 2 % 2, n % 2, c * width:(c + 1) * width], keys[:, tile],
                                            queries[:, tile] if n == 0 else odd(queries[:, tile], 2 ** (n - 1)),
                                            start=True, stop=True)
                    else:
                        ins = pe.matmul(ps_cross, keys[:, 0:P], queries[:, P:T], start=True, stop=True)
                    if n % 2 or n == LEVELS:
                        ins.then_inc(s("lev_ready"), 1)

            def mixers_head(i, before=None, memory=True):
                first = before is None
                start, b = (G_MIX, 0) if first else (G_MIX - 1, 1)
                u = U_MIX + i * 8 - b

                def first_whole(g, u, b):
                    def ready(c):
                        if g == 0:
                            pe.wait_ge(s("xs_x"), c + 1)
                        if c % (KT // QUARTERS) == 0:
                            pe.wait_ge(*first_count("lo", g, c * QUARTERS // KT))

                    pe.wait_ge(out_free, u + 1)
                    cells(g, b, act_a, range(KT), ready=ready).then_inc(w_used, 1)

                first_whole(0, u, b) if first else whole(start, i, 8, 0, u, b, act_a)
                if not first:
                    recurrence_summed(before)
                    attention_turned(before)
                first_whole(1, u + 1, 1 - b) if first else whole(start, i, 8, 1, u + 1, 1 - b, act_a)
                if not first:
                    attention_out(before)
                    whole(start, i, 8, 2, u + 2, b, act_a)
                else:
                    await_block(start, i, 8, 2, u + 2)
                    cells(2, b, act_a, range(KT // 2), closes=False)
                    pe.wait_ge(s("consts_in"), 7 * 16)
                    column_sums(ps_a, [acc[:, :]], lambda n: event("x_sum"), "x_summed")
                    cells(2, b, act_a, range(KT // 2, KT), opens=False).then_inc(w_used, 1)
                whole(start, i, 8, 3, u + 3, 1 - b, act_a)
                whole(start, i, 8, 4, u + 4, b, act_a)
                if first:
                    whole(start, i, 8, 5, u + 5, 1 - b, act_a)
                wait(pe, "i_ready", i + 1)
                turn(ps_t[:, 0:P], iT[:, 0:P], None, 0)
                turn(ps_t[:, P:T], iT[:, P:T], "i_turned")
                wait(pe, "fk_ready", i + 1)
                wait(pe, "q_ready", i + 1)
                wait(pe, "var_ready", i)
                levels(i, range(4))
                if not first:
                    whole(start, i, 8, 5, u + 5, 1 - b, act_a)
                wait(pe, "aq_ready", i + 1)
                wait(pe, "ak_ready", i + 1)
                wait(pe, "att_max", i)
                masked_scores(aqT, akT, lambda rows, n: ()).then_inc(s("sc_ready"), 1)
                if not first:
                    levels(i, range(4, LEVELS + 1))
                if first:
                    await_block(start, i, 8, 6, u + 6)
                    cells((start + 6) % NS, b, act_a, range(3 * KT // 4), closes=False)
                    levels(i, range(4, LEVELS + 1))
                    cells((start + 6) % NS, b, act_a, range(3 * KT // 4, KT), opens=False).then_inc(w_used, 1)
                else:
                    whole(start, i, 8, 6, u + 6, b, act_a)
                wait(pe, "av_ready", i + 1)
                wait(pe, "vtok_ready", i + 1)
                turn(ps_t[:, 0:P], avT[:, 0:P], None, 0)
                turn(ps_t[:, P:T], avT[:, P:T], "av_turned")
                if memory:
                    pe.wait_ge(s("xs_mem"), KT)
                    whole(start, i, 8, 7, u + 7, 1 - b, xs_mem)
                wait(pe, "lev_used", (i + 1) * LEVELS)
                wait(pe, "cross_ready", i + 1)
                weighted(ps_a, vtok, sT).then_inc(s("hg_out"), 1)

            mixers_head(0, memory=False)
            with pe.Fori(0, HEADS - 2) as n:
                mixers_head(n + 1, n)
            mixers_head(HEADS - 1, HEADS - 2, memory=False)

            late = (HEADS - 1, 2 * HEADS - 1)
            early = [c for c in range(KT) if c not in late]
            half = len(early) // 2
            pe.wait_ge(s("mix_done"), HEADS - 1)
            await_block(G_OUT, 0, 0, 0, U_OUT)
            cells(G_OUT % NS, 0, xs_mix, early, closes=False)
            recurrence_summed(HEADS - 1)
            attention_turned(HEADS - 1)
            await_block(G_OUT, 0, 0, 1, U_OUT + 1)
            cells((G_OUT + 1) % NS, 1, xs_mix, early[:half], closes=False)
            attention_out(HEADS - 1)
            cells((G_OUT + 1) % NS, 1, xs_mix, early[half:], opens=False, closes=False)
            pe.wait_ge(s("att_split"), HEADS)
            pe.wait_ge(s("mix_done"), HEADS)
            for j in range(2):
                cells((G_OUT + j) % NS, j, xs_mix, late, opens=False).then_inc(w_used, 1)
            for j in range(2, 4):
                whole(G_OUT, 0, 0, j, U_OUT + j, j % 2, xs_mix)
            with pe.Fori(0, 3) as i:
                for j in range(4):
                    whole(G_OUT + 4, i, 4, j, U_OUT + 4 + 4 * i + j, j % 2, xs_mix)
            await_block(G_FILL, 0, 0, 0, U_FILL)
            cells(G_FILL % NS, 0, xs_mem, range(KT // 2), closes=False)
            column_sums(ps_a, [acc[:, :]], lambda n: step("mixed_acc", KT), "mixed_summed")
            cells(G_FILL % NS, 0, xs_mem, range(KT // 2, KT), opens=False).then_inc(w_used, 1)
            column_sums(ps_sc[:, 0:T], [rstd_mem[:, :]], lambda n: event("mem_sum"), "mem_summed")
            whole(G_FILL, 0, 0, 1, U_FILL + 1, 1, xs_mem)

            for j in range(2):
                whole(G_UP, 0, 0, j, U_UP + j, j % 2, act_a, ready=None if j else lambda c: pe.wait_ge(s("xs_u"), c + 1))
            await_block(G_UP, 0, 0, 2, U_UP + 2)
            cells((G_UP + 2) % NS, 0, act_a, range(KT // 2), closes=False)
            column_sums(ps_b, [acc[:, :]], lambda n: event("h1_sum"), "h1_summed")
            cells((G_UP + 2) % NS, 0, act_a, range(KT // 2, KT), opens=False).then_inc(w_used, 1)
            whole(G_UP, 0, 0, 3, U_UP + 3, 1, act_a)
            with pe.Fori(0, FT // 2 - 1) as i:
                for j in range(4):
                    whole(G_UP + 4, i, 4, j, U_UP + 4 + 4 * i + j, j % 2, act_a)
            with pe.Fori(0, KT // 2) as i:
                for j in range(8):
                    part, bank = j % 4, j // 4
                    pe.wait_ge(w_lo, G_DOWN + 8 * i + j + 1)
                    if part == 0:
                        pe.wait_ge(out_free, U_DOWN + 2 * i + bank + 1)
                    if j < 4:
                        pe.wait_ge(s("xs_g"), DOWN_CELLS * (part + 1))
                    for c in range(DOWN_CELLS):
                        k = DOWN_CELLS * part + c
                        ins = product((G_DOWN + j) % NS, c, big[:, k, :], bank, k == 0, k == FT - 1)
                    ins.then_inc(w_used, 1)

            def parts(g, outs, last, per, xs, kept=None):
                pe.wait_ge(w_lo, g + 1)
                for o in outs:
                    if kept is not None and kept + o >= len(whole_outputs):
                        pe.wait_ge(s("pe_kept"), kept + o - len(whole_outputs) + 1)
                    place = whole_outputs[o % len(whole_outputs)]
                    for c in range(per):
                        cell = slice((o * per + c) * P, (o * per + c + 1) * P)
                        x_hi, x_lo = xs[:, c, 0:T], xs[:, c, T:2 * T]
                        pe.matmul(place, whi[:, g % NS, cell], x_hi, start=c == 0, stop=False)
                        pe.matmul(place, whi[:, g % NS, cell], x_lo, start=False, stop=False)
                        ins = pe.matmul(place, wlo[:, g % NS, cell], x_hi, start=False, stop=c == per - 1)
                    ins.then_inc(w_used if o == last else part_made, 1)

            pe.wait_ge(s("xs_p"), 2)
            parts(G_PE, range(4), 7, 2, xs_p, 0)
            column_sums(ps_a, [acc[:, :]], lambda n: step("y_acc", KT), "y_summed")
            parts(G_PE, range(4, 8), 7, 2, xs_p, 0)
            parts(G_PE + 1, range(8), 7, 2, xs_p, 8)
            for j in range(4):
                whole(G_PG, 0, 0, j, U_PG + j, j % 2, xs_h,
                      ready=None if j else lambda c: pe.wait_ge(s("xs_h"), c * QUARTERS // KT + 1))
            with pe.Fori(0, 3) as i:
                for j in range(4):
                    whole(G_PG + 4, i, 4, j, U_PG + 4 + 4 * i + j, j % 2, xs_h)

            late = KT - 2
            for j in range(2):
                await_block(G_CONV, 0, 0, j, U_CONV + j)
                cells((G_CONV + j) % NS, j, act_a, range(late), closes=False,
                      ready=None if j else lambda c: pe.wait_ge(s("xs_n"), c + 1))
            for j in range(2):
                cells((G_CONV + j) % NS, j, act_a, range(late, KT), opens=False,
                      ready=None if j else lambda c: pe.wait_ge(s("xs_n"), c + 1)).then_inc(w_used, 1)
            column_sums(ps_b, [acc[:, :]], lambda n: step("h3_acc", KT), "h3_summed")
            for j in range(2, 2 * GROUPS):
                whole(G_CONV, 0, 0, j, U_CONV + j, j % 2, act_a)
            pe.wait_ge(s("wfg_ready"), 1)
            for k in range(KT):
                ins = pe.matmul(ps_t[0:FOX_ROWS, 0:T], wfg[:, k, :], h[:, k, :], start=k == 0, stop=k == KT - 1)
            ins.then_inc(s("fl_ready"), 1)

            def fox_turned(n):
                wait(pe, "fp_ready", 2 * n + 2)
                for c in range(3):
                    turn(ps_t[:, c * P:(c + 1) * P], fs[:, c * P:(c + 1) * P], "fp_turned", c == 2)

            def fox_out(n):
                wait(pe, "fvtok_ready", n + 1)
                wait(pe, "fpT_ready", n + 1)
                weighted(ps_a, fvtok, fpT).then_inc(s("fo_ready"), 1)

            def fox_head(i, before=None):
                u = U_FOX + 4 * i
                whole(G_FOX, i, 4, 0, u, 0, act_a)
                if before is not None:
                    fox_turned(before)
                whole(G_FOX, i, 4, 1, u + 1, 1, act_a)
                if before is not None:
                    fox_out(before)
                whole(G_FOX, i, 4, 2, u + 2, 0, act_a)
                wait(pe, "c_ready", 2 * i + 2)
                wait(pe, "fq_ready", i + 1)
                wait(pe, "fk2_ready", i + 1)
                wait(pe, "fox_max", i)
                masked_scores(fqT, fkT, lambda rows, n: ((cpos[:, rows], cneg[:, 0:n]),))\
                    .then_inc(s("fsc_ready"), 1)
                whole(G_FOX, i, 4, 3, u + 3, 1, act_a)
                wait(pe, "fv_ready", i + 1)
                turn(ps_b[:, 0:P], fvT[:, 0:P], None, 0)
                turn(ps_b[:, P:T], fvT[:, P:T], "fv_turned")

            fox_head(0)
            with pe.Fori(0, HEADS - 1) as n:
                fox_head(n + 1, n)

            def memory_turned(n):
                pe.wait_ge(s("mp_ready"), 2 * n + 2)
                for t in range(2):
                    for m in range(2):
                        turn(ps_t[:, m * T + t * P:m * T + t * P + P], fs[:, t * T + m * P:t * T + m * P + P],
                             "mp_turned", t and m)

            def memory_out(n):
                pe.wait_ge(s("mvtok_ready"), n + 1)
                pe.wait_ge(s("mpT_ready"), n + 1)
                wait(pe, "mo_done", n)
                pe.matmul(ps_a, fvtok[:, 0, :], fpT[:, 0:T], start=True, stop=False)
                pe.matmul(ps_a, fvtok[:, 1, :], fpT[:, T:2 * T], start=False, stop=True).then_inc(s("mo_ready"), 1)

            column_sums(ps_lev[:, 0, 0, :], [sg_c[:, 2, :]], lambda n: event("uc_sum"), "uc_summed")
            pe.wait_ge(s("mkv_ready"), 1)
            for n in range(MEM_HEADS):
                u = U_MEM + 2 * n
                whole(G_MEM, 0, 0, 2 * n, u, 0, act_a)
                memory_turned(n - 1) if n else fox_turned(HEADS - 1)
                whole(G_MEM, 0, 0, 2 * n + 1, u + 1, 1, act_a)
                memory_out(n - 1) if n else fox_out(HEADS - 1)
                pe.wait_ge(s("mq_ready"), n + 1)
                for t in range(2):
                    ins = pe.matmul(ps_sc[:, t * T:t * T + T], fqT[:, t * P:t * P + P], mkv[:, n, :], start=True, stop=True)
                ins.then_inc(s("msc_ready"), 1)
                turn(ps_b[:, 0:P], mkv[:, MEM_HEADS + n, 0:P], None, 0)
                turn(ps_b[:, P:T], mkv[:, MEM_HEADS + n, P:T], "mv_turned")
                if n == 1:
                    column_sums(ps_lev[:, 1, 0, :], [usq[:, 0, :]], lambda n: event("usq_sum"), "usq_summed")
            for k in range(GROUPS):
                whole(G_CG, 0, 0, k, U_CG + k, k % 2, act_a)
                if k == 0:
                    memory_turned(MEM_HEADS - 1)
                if k == 1:
                    memory_out(MEM_HEADS - 1)
            pe.wait_ge(s("xs_cv"), 1)
            parts(G_PW, range(GROUPS), GROUPS - 1, GROUPS, xs_cv)

            pe.wait_ge(s("fo_split"), HEADS)
            pe.wait_ge(s("mo_split"), MEM_HEADS)
            order = tuple(range(GROUPS, KT)) + tuple(range(GROUPS))
            with pe.Fori(0, 4) as i:
                for j in range(4):
                    whole(G_OUT2, i, 4, j, U_OUT2 + 4 * i + j, j % 2, xs_y, order,
                          ready=None if j else lambda c: c == 0 and pe.wait_ge(s("xs_yc"), GROUPS))
            column_sums(ps_a, [acc[:, :], sq4[:, 1, :]],
                        lambda n: (s("h4_last_sq"), 1) if n else step("h4_acc", KT - 1), "h4_summed")


def kernel(**inputs):
    import concourse.bacc as bacc
    from concourse.bass_utils import run_bass_kernel_spmd

    f32, b16 = np.float32, mybir.dt.np(BF16)
    get = {n: np.asarray(x) for n, x in inputs.items()}

    def features(x):
        return np.ascontiguousarray(x.T.reshape(-1, P, x.shape[0]).transpose(1, 0, 2))

    def vector(x):
        return x.reshape(-1, P).T

    def blocks(w):
        k, n = w.shape
        return w.reshape(k // P, P, n // P, P).transpose(2, 1, 0, 3).reshape(n // P, P, k)

    w_in, w_in2 = get["w_in"][0], get["w_in_2"][0]
    hq, hf, hi, hg, aq, ak, av = (blocks(w) for w in np.split(w_in, 7, axis=1))
    mkv = blocks(get["w_mem_kv_2"][0])
    mix = np.stack([hf, hq, hi, aq, ak, av, hg, mkv], axis=1).reshape(8 * HEADS, P, BW)
    mix = np.delete(mix, [7, 8 * HEADS - 1], axis=0)
    up = blocks(get["w_up"][0])
    up = np.stack([up[:FT], up[FT:]], axis=1).reshape(2 * FT, P, BW)
    w_a = np.concatenate([mix, blocks(get["w_out"][0]), mkv[[0, HEADS - 1]], up])
    w_down = get["w_down"][0].reshape(4, DOWN_CELLS, P, KT, P).transpose(3, 0, 2, 1, 4).reshape(4 * KT, P, DOWN_CELLS * P)
    w_pe = blocks(get["w_pe"][0]).reshape(2, 8, P, 2, P).transpose(0, 2, 1, 3, 4).reshape(2, P, BW)
    c = GROUPS * P
    fw = HEADS * P
    at = np.cumsum([0, c, c, c, fw, fw, fw, HEADS, fw, c, c])
    cv_a, cv_b, cv_g, fq, fk, fv, fl, fg, mq, mg = (w_in2[:, a:b] for a, b in zip(at[:-1], at[1:]))
    conv = np.stack([blocks(cv_a), blocks(cv_b)], axis=1).reshape(2 * GROUPS, P, BW)
    fox = np.stack([blocks(fq), blocks(fk), blocks(fv), blocks(fg)], axis=1).reshape(4 * HEADS, P, BW)
    mem = np.stack([blocks(mq), blocks(mg)], axis=1).reshape(2 * MEM_HEADS, P, BW)
    pw = blocks(get["w_conv_pw_2"][0]).transpose(1, 0, 2).reshape(1, P, BW)
    w_b = np.concatenate([w_pe, blocks(get["w_pg"][0]), conv, fox, mem, blocks(cv_g), pw, blocks(get["w_out_2"][0])])
    wfg = np.ascontiguousarray(np.tile(fl.reshape(KT, P, HEADS).transpose(1, 0, 2), 2 * PARTS))
    bfox = np.tile(get["b_f_2"].reshape(HEADS), 2 * PARTS).reshape(FOX_ROWS, 1)
    fox_rows = np.zeros((2, PARTS, HEADS, 2 * HEADS + 2 + PARTS), f32)
    fox_rows[0, :, :, :HEADS], fox_rows[1, :, :, 2 * HEADS] = np.eye(HEADS), 1
    fox_rows[1, :, :, HEADS:2 * HEADS], fox_rows[0, :, :, 2 * HEADS + 1] = -np.eye(HEADS), 1
    for part in range(PARTS):
        fox_rows[:, part, :, 2 * HEADS + 2 + part] = 1
    fox_rows = fox_rows.reshape(FOX_ROWS, -1)

    cw = np.stack([vector(x) for x in (*get["conv_w"][0], get["conv_b"][0])], axis=2)
    cw = np.stack([cw[:, :FT], cw[:, FT:]], axis=2).reshape(P, 8 * FT)
    taps = np.stack([vector(x) for x in get["conv_w_2"][0]], axis=2).reshape(P, GROUPS * TAPS)
    vec = np.concatenate([
        vector(get["ln_mix_pre"]), vector(get["lb_logits"]), vector(get["hgrn_norm"]), vector(get["ln_mix_post"]),
        vector(get["ln_ffn_pre"]), cw, vector(get["ln_ffn_post"]), vector(get["norm_g_2"]), vector(get["mem_norm_g_2"]),
        taps, vector(get["conv_b_2"]), vector(get["conv_ln_g_2"]), vector(get["conv_ln_b_2"]), vector(get["final_g_2"])],
        axis=1)

    t, k = np.arange(T)[:, None], np.arange(T)[None, :]

    def tiles(m):
        return np.ascontiguousarray(np.concatenate([m[:P, :P], m[P:, :]], axis=1))

    dist = t - k
    count = sum(((dist >= 0) & (dist <= w) & (dist % d == 0)).astype(f32) for w, d in ((128, 1), (512, 4), (2048, 16)))
    one = np.arange(P)
    lmask = [one[:, None] == one[None, :]]
    for level in range(LEVELS - 1):
        b = one // 2 ** level
        lmask.append((b[:, None] % 2 == 0) & (b[None, :] == b[:, None] + 1))
    lmask = np.stack([np.concatenate([m, m], axis=1) for m in lmask], axis=1).astype(b16)

    arrays = {
        "xT": features(get["x"][0]), "memT": features(get["mem_2"][0]), "pT": features(get["p"][0, 0]),
        "w_a": w_a, "w_down": w_down, "w_b": w_b, "wfg": wfg, "bfox": bfox, "fox_rows": fox_rows, "vec": vec,
        "ident": np.eye(P, dtype=f32), "ones": np.ones((P, P), f32), "mult": tiles(count).astype(b16),
        "bias_att": tiles(np.where(count > 0, 0.0, MASKED)).astype(b16),
        "bias_fox": tiles(np.where(dist >= 0, 0.0, MASKED)).astype(b16), "lmask": lmask,
    }
    nc = bacc.Bacc("TRN2", target_bir_lowering=False, num_devices=1, dynamic_dma_scratch_size=1024)
    drams, sent = {}, {}
    for name, x in arrays.items():
        sent[f"in_{name}"] = np.ascontiguousarray(x)
        drams[name] = nc.dram_tensor(f"in_{name}", x.shape, mybir.dt.from_np(x.dtype), kind="ExternalInput").ap()
    out = nc.dram_tensor("out", (P, KT, T), F32, kind="ExternalOutput").ap()
    build(nc, drams, out)
    r = run_bass_kernel_spmd(nc, [sent], core_ids=[0])
    got = r.results[0]["out"]
    return np.ascontiguousarray(got.transpose(1, 0, 2).reshape(D, T).T).reshape(1, T, D)
```
